# Optimizing a Trainium2 kernel written in Bass

```python
import jax
import jax.numpy as jnp
from jax import lax
import numpy as np

D_MODEL = 1024
BATCH = 1
SEQ = 512
DEPTH = 1

HEAD_DIM = 64
LRU_WIDTH = D_MODEL // 2
LRU_BLOCKS = 8
LRU_BLOCK_DIM = LRU_WIDTH // LRU_BLOCKS
CONV_WIDTH = 4
LRU_C = 8.0
NSA_HEADS = D_MODEL // 128
NSA_KV_HEADS = 2
NSA_GROUP = NSA_HEADS // NSA_KV_HEADS
NSA_WIDTH = NSA_HEADS * HEAD_DIM
NSA_KV_WIDTH = NSA_KV_HEADS * HEAD_DIM
CMP_LEN = 32
CMP_STRIDE = 16
SLC_LEN = 64
N_SELECT = 16
WINDOW = 512
SLC_Q_CHUNK = 32
FOX_HEADS = D_MODEL // 128
FOX_WIDTH = FOX_HEADS * HEAD_DIM
Q_BLOCK = 128
D_MIX = LRU_WIDTH + NSA_WIDTH + FOX_WIDTH
IN_SPLITS = (LRU_WIDTH, LRU_WIDTH,
             NSA_WIDTH, NSA_KV_WIDTH, NSA_KV_WIDTH, NSA_KV_WIDTH, NSA_KV_WIDTH, NSA_KV_WIDTH, NSA_KV_WIDTH,
             3 * NSA_HEADS, NSA_WIDTH,
             FOX_WIDTH, FOX_WIDTH, FOX_WIDTH, FOX_HEADS, FOX_WIDTH)
D_IN = sum(IN_SPLITS)
IN_OFFSETS = tuple(int(o) for o in np.cumsum(IN_SPLITS)[:-1])
NORM_EPS = 1e-6
NEG_INF = -1e30
FORCE_SCORE = 1e9
ATTN_SCALE = HEAD_DIM ** -0.5

kernel_name = 'hybrid_rglru_nsa_fox_block'

def rmsnorm(x, g):
    x32 = x.astype(jnp.float32)
    y = x32 * lax.rsqrt(jnp.mean(x32 * x32, axis=-1, keepdims=True) + NORM_EPS)
    return (y * g.astype(jnp.float32)).astype(x.dtype)

def split_heads(t, n_heads):
    return t.reshape(t.shape[0], t.shape[1], n_heads, HEAD_DIM)

def safe_softmax(s, mask):
    s = jnp.where(mask, s.astype(jnp.float32), NEG_INF)
    m = jnp.max(s, axis=-1, keepdims=True)
    e = jnp.where(mask, jnp.exp(s - m), 0.0)
    return e / jnp.maximum(jnp.sum(e, axis=-1, keepdims=True), 1e-30)

def linear_combine(c1, c2):
    a1, b1 = c1
    a2, b2 = c2
    return a1 * a2, a2 * b1 + b2

def rglru_group(u, z, conv_w, conv_b, wa, ba, wx, bx, lam):
    bsz, seq, width = u.shape
    u_pad = jnp.pad(u, ((0, 0), (CONV_WIDTH - 1, 0), (0, 0)))
    xc = conv_b + sum(u_pad[:, k:k + seq] * conv_w[k] for k in range(CONV_WIDTH))
    xh = xc.reshape(bsz, seq, LRU_BLOCKS, LRU_BLOCK_DIM)
    r = jax.nn.sigmoid(jnp.einsum('bshi,hij->bshj', xh, wa).reshape(bsz, seq, width) + ba)
    i = jax.nn.sigmoid(jnp.einsum('bshi,hij->bshj', xh, wx).reshape(bsz, seq, width) + bx)
    log_a = -LRU_C * r.astype(jnp.float32) * jax.nn.softplus(-lam.astype(jnp.float32))
    a = jnp.exp(log_a)
    b = jnp.sqrt(-jnp.expm1(2.0 * log_a)) * (i * xc).astype(jnp.float32)
    _, h = lax.associative_scan(linear_combine, (a, b), axis=1)
    return h.astype(u.dtype) * jax.nn.silu(z)

def nsa_compressed(q, kc, vc, pe_k, pe_v, wck, wcv, k_g):
    bsz, seq = kc.shape[0], kc.shape[1]
    n_cmp = (seq - CMP_LEN) // CMP_STRIDE + 1
    n_slc = seq // SLC_LEN
    starts = jnp.arange(n_cmp) * CMP_STRIDE
    tok = starts[:, None] + jnp.arange(CMP_LEN)[None, :]
    k_cmp = jnp.einsum('bnlgd,lde->bnge', kc[:, tok] + pe_k[:, None, :], wck)
    v_cmp = jnp.einsum('bnlgd,lde->bnge', vc[:, tok] + pe_v[:, None, :], wcv)
    k_cmp = rmsnorm(k_cmp, k_g)
    qg = q.reshape(bsz, seq, NSA_KV_HEADS, NSA_GROUP, HEAD_DIM)
    s = jnp.einsum('bsgrd,bngd->bgrsn', qg, k_cmp) * ATTN_SCALE
    t = jnp.arange(seq)
    mask = (starts + CMP_LEN - 1)[None, :] <= t[:, None]
    p = safe_softmax(s, mask)
    o = jnp.einsum('bgrsn,bngd->bsgrd', p, v_cmp).reshape(bsz, seq, NSA_HEADS, HEAD_DIM)
    slc_starts = jnp.arange(n_slc) * SLC_LEN
    overlap = ((starts[:, None] <= slc_starts[None, :] + SLC_LEN - 1)
               & (starts[:, None] + CMP_LEN - 1 >= slc_starts[None, :])).astype(jnp.float32)
    importance = jnp.einsum('bgrsn,nj->bgsj', p, overlap)
    return o.astype(q.dtype), importance

def nsa_selected(q, ks, vs, importance):
    bsz, seq = ks.shape[0], ks.shape[1]
    n_slc = seq // SLC_LEN
    k_sel = min(N_SELECT, n_slc)
    t = jnp.arange(seq)
    blk_t = t // SLC_LEN
    j = jnp.arange(n_slc)
    valid = j[None, :] <= blk_t[:, None]
    forced = (j[None, :] == 0) | (j[None, :] == blk_t[:, None]) | (j[None, :] == blk_t[:, None] - 1)
    score = jnp.where(valid, jnp.where(forced, FORCE_SCORE, importance), NEG_INF)
    vals, idx = lax.top_k(score, k_sel)
    sel_ok = vals > 0.5 * NEG_INF
    ks_blk = ks.reshape(bsz, n_slc, SLC_LEN, NSA_KV_HEADS, HEAD_DIM).transpose(0, 3, 1, 2, 4)
    vs_blk = vs.reshape(bsz, n_slc, SLC_LEN, NSA_KV_HEADS, HEAD_DIM).transpose(0, 3, 1, 2, 4)
    n_chunk = seq // SLC_Q_CHUNK
    q_c = q.reshape(bsz, n_chunk, SLC_Q_CHUNK, NSA_KV_HEADS, NSA_GROUP, HEAD_DIM).transpose(1, 0, 2, 3, 4, 5)
    idx_c = idx.reshape(bsz, NSA_KV_HEADS, n_chunk, SLC_Q_CHUNK, k_sel).transpose(2, 0, 1, 3, 4)
    ok_c = sel_ok.reshape(bsz, NSA_KV_HEADS, n_chunk, SLC_Q_CHUNK, k_sel).transpose(2, 0, 1, 3, 4)
    t_c = t.reshape(n_chunk, SLC_Q_CHUNK)
    bi = jnp.arange(bsz)[:, None, None, None]
    gi = jnp.arange(NSA_KV_HEADS)[None, :, None, None]

    def chunk(args):
        qb, ib, okb, tb = args
        kk = ks_blk[bi, gi, ib]
        vv = vs_blk[bi, gi, ib]
        s = jnp.einsum('bcgrd,bgcknd->bgrckn', qb, kk) * ATTN_SCALE
        pos = ib[..., None] * SLC_LEN + jnp.arange(SLC_LEN)
        mask = okb[..., None] & (pos <= tb[None, None, :, None, None])
        s = s.reshape(bsz, NSA_KV_HEADS, NSA_GROUP, SLC_Q_CHUNK, k_sel * SLC_LEN)
        mask = mask.reshape(bsz, NSA_KV_HEADS, 1, SLC_Q_CHUNK, k_sel * SLC_LEN)
        p = safe_softmax(s, mask)
        vv = vv.reshape(bsz, NSA_KV_HEADS, SLC_Q_CHUNK, k_sel * SLC_LEN, HEAD_DIM)
        return jnp.einsum('bgrcm,bgcmd->bcgrd', p, vv).astype(q.dtype)

    o = lax.map(chunk, (q_c, idx_c, ok_c, t_c))
    return o.transpose(1, 0, 2, 3, 4, 5).reshape(bsz, seq, NSA_HEADS, HEAD_DIM)

def nsa_window(q, kw, vw):
    bsz, seq = kw.shape[0], kw.shape[1]
    n_blk = seq // Q_BLOCK
    span = Q_BLOCK + WINDOW
    k_pad = jnp.pad(kw, ((0, 0), (WINDOW, 0), (0, 0), (0, 0)))
    v_pad = jnp.pad(vw, ((0, 0), (WINDOW, 0), (0, 0), (0, 0)))
    q_b = q.reshape(bsz, n_blk, Q_BLOCK, NSA_KV_HEADS, NSA_GROUP, HEAD_DIM).transpose(1, 0, 2, 3, 4, 5)

    def blk(args):
        b_idx, qb = args
        start = b_idx * Q_BLOCK
        kb = lax.dynamic_slice_in_dim(k_pad, start, span, axis=1)
        vb = lax.dynamic_slice_in_dim(v_pad, start, span, axis=1)
        t = start + jnp.arange(Q_BLOCK)
        s_pos = start - WINDOW + jnp.arange(span)
        diff = t[:, None] - s_pos[None, :]
        mask = (s_pos[None, :] >= 0) & (diff >= 0) & (diff < WINDOW)
        s = jnp.einsum('bqgrd,bkgd->bgrqk', qb, kb) * ATTN_SCALE
        p = safe_softmax(s, mask)
        return jnp.einsum('bgrqk,bkgd->bqgrd', p, vb).astype(q.dtype)

    o = lax.map(blk, (jnp.arange(n_blk), q_b))
    return o.transpose(1, 0, 2, 3, 4, 5).reshape(bsz, seq, NSA_HEADS, HEAD_DIM)

def nsa_group(q, kc, vc, ks, vs, kw, vw, gate_logits, z, q_g, k_g, pe_k, pe_v, wck, wcv, gate_b):
    bsz, seq = q.shape[0], q.shape[1]
    q = rmsnorm(split_heads(q, NSA_HEADS), q_g)
    kc, vc, ks, vs, kw, vw = (split_heads(t, NSA_KV_HEADS) for t in (kc, vc, ks, vs, kw, vw))
    o_cmp, importance = nsa_compressed(q, kc, vc, pe_k, pe_v, wck, wcv, k_g[0])
    o_slc = nsa_selected(q, rmsnorm(ks, k_g[1]), vs, importance)
    o_win = nsa_window(q, rmsnorm(kw, k_g[2]), vw)
    g = jax.nn.sigmoid(gate_logits + gate_b).reshape(bsz, seq, NSA_HEADS, 3)
    o = g[..., 0:1] * o_cmp + g[..., 1:2] * o_slc + g[..., 2:3] * o_win
    return o.reshape(bsz, seq, NSA_WIDTH).astype(z.dtype) * jax.nn.silu(z)

def fox_group(q, k, v, f_logits, z, q_g, k_g, f_b):
    bsz, seq = q.shape[0], q.shape[1]
    q = rmsnorm(split_heads(q, FOX_HEADS), q_g)
    k = rmsnorm(split_heads(k, FOX_HEADS), k_g)
    v = split_heads(v, FOX_HEADS)
    log_f = jax.nn.log_sigmoid(f_logits.astype(jnp.float32) + f_b.astype(jnp.float32))
    c = jnp.cumsum(log_f, axis=1).transpose(0, 2, 1)
    n_blk = seq // Q_BLOCK
    q_b = q.reshape(bsz, n_blk, Q_BLOCK, FOX_HEADS, HEAD_DIM).transpose(1, 0, 2, 3, 4)
    c_b = c.reshape(bsz, FOX_HEADS, n_blk, Q_BLOCK).transpose(2, 0, 1, 3)
    s_pos = jnp.arange(seq)

    def blk(args):
        b_idx, qb, cb = args
        t = b_idx * Q_BLOCK + jnp.arange(Q_BLOCK)
        s = (jnp.einsum('bqhd,bshd->bhqs', qb, k).astype(jnp.float32) * ATTN_SCALE
             + cb[..., None] - c[:, :, None, :])
        mask = s_pos[None, :] <= t[:, None]
        p = safe_softmax(s, mask)
        return jnp.einsum('bhqs,bshd->bqhd', p, v).astype(q.dtype)

    o = lax.map(blk, (jnp.arange(n_blk), q_b, c_b))
    o = o.transpose(1, 0, 2, 3, 4).reshape(bsz, seq, FOX_WIDTH)
    return o.astype(z.dtype) * jax.nn.silu(z)

def hybrid_layer(x, norm_g, w_in, w_out, conv_w, conv_b, lru_wa, lru_ba, lru_wx, lru_bx, lru_lambda,
                 nsa_q_g, nsa_k_g, cmp_pe_k, cmp_pe_v, cmp_wk, cmp_wv, nsa_gate_b,
                 fox_q_g, fox_k_g, fox_f_b):
    h = rmsnorm(x, norm_g)
    proj = jnp.einsum('bsd,de->bse', h, w_in)
    (lru_u, lru_z, nsa_q, nsa_kc, nsa_vc, nsa_ks, nsa_vs, nsa_kw, nsa_vw, nsa_gl, nsa_z,
     fox_q, fox_k, fox_v, fox_fl, fox_z) = jnp.split(proj, IN_OFFSETS, axis=-1)
    y_lru = rglru_group(lru_u, lru_z, conv_w, conv_b, lru_wa, lru_ba, lru_wx, lru_bx, lru_lambda)
    y_nsa = nsa_group(nsa_q, nsa_kc, nsa_vc, nsa_ks, nsa_vs, nsa_kw, nsa_vw, nsa_gl, nsa_z,
                      nsa_q_g, nsa_k_g, cmp_pe_k, cmp_pe_v, cmp_wk, cmp_wv, nsa_gate_b)
    y_fox = fox_group(fox_q, fox_k, fox_v, fox_fl, fox_z, fox_q_g, fox_k_g, fox_f_b)
    y = jnp.concatenate([y_lru, y_nsa, y_fox], axis=-1)
    return x + jnp.einsum('bse,ed->bsd', y, w_out)

def setup_inputs(seed: int = 0) -> dict:
    key = jax.random.key(seed)
    ks = jax.random.split(key, 22)
    f32 = jnp.float32

    def nrm(k, shape, scale):
        return jax.random.normal(k, shape, f32) * scale

    L = DEPTH
    a0 = jax.random.uniform(ks[10], (L, LRU_WIDTH), f32, 0.9, 0.999)
    return {
        'x': nrm(ks[0], (BATCH, SEQ, D_MODEL), 1.0),
        'norm_g': 1.0 + nrm(ks[1], (L, D_MODEL), 0.1),
        'w_in': nrm(ks[2], (L, D_MODEL, D_IN), D_MODEL ** -0.5),
        'w_out': nrm(ks[3], (L, D_MIX, D_MODEL), D_MIX ** -0.5),
        'conv_w': nrm(ks[4], (L, CONV_WIDTH, LRU_WIDTH), CONV_WIDTH ** -0.5),
        'conv_b': nrm(ks[5], (L, LRU_WIDTH), 0.02),
        'lru_wa': nrm(ks[6], (L, LRU_BLOCKS, LRU_BLOCK_DIM, LRU_BLOCK_DIM), LRU_BLOCK_DIM ** -0.5),
        'lru_ba': nrm(ks[7], (L, LRU_WIDTH), 0.1),
        'lru_wx': nrm(ks[8], (L, LRU_BLOCKS, LRU_BLOCK_DIM, LRU_BLOCK_DIM), LRU_BLOCK_DIM ** -0.5),
        'lru_bx': nrm(ks[9], (L, LRU_WIDTH), 0.1),
        'lru_lambda': jnp.log(a0) - jnp.log1p(-a0),
        'nsa_q_g': 1.0 + nrm(ks[11], (L, HEAD_DIM), 0.1),
        'nsa_k_g': 1.0 + nrm(ks[12], (L, 3, HEAD_DIM), 0.1),
        'cmp_pe_k': nrm(ks[13], (L, CMP_LEN, HEAD_DIM), 0.1),
        'cmp_pe_v': nrm(ks[14], (L, CMP_LEN, HEAD_DIM), 0.1),
        'cmp_wk': nrm(ks[15], (L, CMP_LEN, HEAD_DIM, HEAD_DIM), (CMP_LEN * HEAD_DIM) ** -0.5),
        'cmp_wv': nrm(ks[16], (L, CMP_LEN, HEAD_DIM, HEAD_DIM), (CMP_LEN * HEAD_DIM) ** -0.5),
        'nsa_gate_b': nrm(ks[17], (L, 3 * NSA_HEADS), 0.1),
        'fox_q_g': 1.0 + nrm(ks[18], (L, HEAD_DIM), 0.1),
        'fox_k_g': 1.0 + nrm(ks[19], (L, HEAD_DIM), 0.1),
        'fox_f_b': 2.0 + nrm(ks[20], (L, FOX_HEADS), 0.5),
    }

def reference(x, norm_g, w_in, w_out, conv_w, conv_b, lru_wa, lru_ba, lru_wx, lru_bx, lru_lambda,
              nsa_q_g, nsa_k_g, cmp_pe_k, cmp_pe_v, cmp_wk, cmp_wv, nsa_gate_b,
              fox_q_g, fox_k_g, fox_f_b):
    for l in range(DEPTH):
        x = hybrid_layer(x, norm_g[l], w_in[l], w_out[l], conv_w[l], conv_b[l], lru_wa[l], lru_ba[l],
                         lru_wx[l], lru_bx[l], lru_lambda[l], nsa_q_g[l], nsa_k_g[l], cmp_pe_k[l],
                         cmp_pe_v[l], cmp_wk[l], cmp_wv[l], nsa_gate_b[l], fox_q_g[l], fox_k_g[l],
                         fox_f_b[l])
    return x


_drawn_inputs = setup_inputs


def setup_inputs(seed=0):
    import zlib

    import numpy as np

    out = dict(_drawn_inputs(seed))
    spreads = {}
    factors = {'conv_b': 3.551,
     'lru_ba': 8.0,
     'lru_bx': 8.0,
     'nsa_q_g': 8.0,
     'nsa_k_g': 8.0,
     'cmp_pe_k': 8.0,
     'cmp_pe_v': 3.499,
     'nsa_gate_b': 8.0,
     'fox_q_g': 5.491,
     'fox_k_g': 5.369}
    for name, (base, spread) in spreads.items():
        noise = np.random.default_rng([zlib.crc32(name.encode()), seed]).standard_normal(out[name].shape)
        drawn = base * np.exp(spread * noise) if base else spread * noise
        out[name] = jnp.asarray(drawn.astype(out[name].dtype))
    for name, factor in factors.items():
        out[name] = (out[name] * factor).astype(out[name].dtype)
    return out
```

```python
from contextlib import ExitStack

import numpy as np

import concourse.bass as bass
from concourse import mybir

F32 = mybir.dt.float32
F32R = mybir.dt.float32r
BF16 = mybir.dt.bfloat16
ACT = mybir.ActivationFunctionType
ALU = mybir.AluOpType
AX = mybir.AxisListType

P = 128
SEQ, D = 512, 1024
HD = 64
KT = D // P
NT = SEQ // P
LRU_T = 512 // P
HEADS = 8
KVH = 2
GROUP = HEADS // KVH
CMP_LEN, CMP_STRIDE = 32, 16
N_CMP = (SEQ - CMP_LEN) // CMP_STRIDE + 1
CMP_PAD = 32
CONV = 4
D_MIX = 1536
ET = D_MIX // P
EPS = 1e-6
NEG = -1e30

CHUNKS = ([("u", j) for j in range(4)] + [("zl", j) for j in range(4)] + [("fg", 0), ("kc", 0), ("vc", 0)]
          + [("ks", 0), ("kw", 0)] + [("nq", j) for j in range(4)] + [("vn", 0), ("vn", 1)]
          + [("fq", j) for j in range(4)] + [("fk", 0)] + [("vf", j) for j in range(4)]
          + [("fk", j) for j in range(1, 4)] + [("zn", j) for j in range(4)] + [("zf", j) for j in range(4)])
N_IN = len(CHUNKS)
N_STREAM = N_IN + ET
AT = {x: c for c, x in enumerate(CHUNKS)}
NORMED = [c for c, (kind, _) in enumerate(CHUNKS) if kind in ("ks", "kw", "nq", "fq", "fk")]
TOKEN_MAJOR = ("vn", "vf")
NSA_END = AT["vn", 1] + 1
FOX_END = AT["fk", 3] + 1
RAW, HL = 2, 4
AHEAD = 3

COLS = {"u": 0, "zl": 512, "nq": 1024, "kc": 1536, "vc": 1664, "ks": 1792, "vs": 1920, "kw": 2048, "vw": 2176,
        "gl": 2304, "zn": 2328, "fq": 2840, "fk": 3352, "vf": 3864, "fl": 4376, "zf": 4384}

CH = {}
_at = 0
for _n, _w in (("norm_g", KT), ("conv_w", CONV * LRU_T), ("conv_b", LRU_T), ("ba", LRU_T), ("bx", LRU_T),
               ("lam", LRU_T), ("nq_g", 1), ("kcmp_g", 1), ("ks_g", 1), ("kw_g", 1), ("fq_g", 1), ("fk_g", 1),
               ("fg_b", 1), ("pe_k", CMP_LEN // 2), ("pe_v", CMP_LEN // 2)):
    CH[_n] = _at
    _at += _w
CH_W = _at

IDENT, BLOCK, ONES, CAUSAL, CMPMASK, CONST_W = 0, P, 2 * P, 3 * P, 4 * P, 4 * P + NT * CMP_PAD

GAIN = {"ks": "ks_g", "kw": "kw_g", "nq": "nq_g", "fq": "fq_g", "fk": "fk_g"}


def program(nc, xT, x_tok, w_in, w_out, chan, const, lru_w, cmp_w, out):
    ctx = ExitStack()
    with ctx:
        def sem(name):
            return ctx.enter_context(nc.semaphore(name))

        def sb(name, shape, dt=F32, where=ctx):
            return where.enter_context(nc.sbuf_tensor(name, shape, dt))

        raw = sb("raw", [P, RAW, D])
        wh = sb("wh", [P, HL, D], F32R)
        wl = sb("wl", [P, HL, D], F32R)
        cst = sb("cst", [P, CONST_W])
        chn = sb("chn", [P, CH_W])
        ident, block_mean, ones = (cst[:, o:o + P] for o in (IDENT, BLOCK, ONES))
        ident_b = sb("ident_b", [P, P], BF16)
        mask_b = sb("mask_b", [P, P], BF16)
        head_sel = sb("head_sel", [96, HEADS, P], BF16)
        c_parts = sb("c_parts", [96, SEQ], BF16)
        rstd_bc = sb("rstd_bc", [P, SEQ])
        rstd_col = sb("rstd_col", [P, NT])
        y_lru = sb("y_lru", [P, LRU_T, SEQ])
        gates = sb("gates", [P, NT, 3 * HEADS])
        qr = sb("qr", [P, 2, SEQ])
        sq = sb("sq", [P, SEQ])
        std = sb("std", [P, SEQ])
        c_work = sb("c_work", [96, SEQ])
        c_mid = sb("c_mid", [HEADS, SEQ], BF16)
        head_out = sb("head_out", [P, NT * HD])
        h_stage = sb("h_stage", [P, SEQ], F32R)
        l_stage = sb("l_stage", [P, SEQ], F32R)
        eps1 = sb("eps1", [P, 1])
        eps64 = sb("eps64", [P, 1])
        one1 = sb("one1", [P, 1])
        csp = sb("csp", [P, 2, LRU_T])
        negmax = sb("negmax", [P, 4])
        rsum = sb("rsum", [P, 3, NT])
        rcp = sb("rcp", [P, 2, NT])
        k_cmp = sb("k_cmp", [HD, KVH, CMP_PAD])
        k_cmp_sq = sb("k_cmp_sq", [HD, KVH, CMP_PAD])
        k_cmp_h = sb("k_cmp_h", [P, KVH, CMP_PAD], F32R)
        k_cmp_l = sb("k_cmp_l", [P, KVH, CMP_PAD], F32R)
        v_cmp = sb("v_cmp", [HD, KVH, CMP_PAD])
        v_blocks = sb("v_blocks", [P, KVH, GROUP * HD])
        cmp_stat = sb("cmp_stat", [P, 3, HEADS])

        with ExitStack() as v:
            xh = sb("xh", [P, KT, SEQ], F32R, v)
            xl = sb("xl", [P, KT, SEQ], F32R, v)
            with ExitStack() as m:
                q_nsa = sb("q_nsa", [P, HEADS, SEQ], F32R, m)
                kh_nsa = sb("kh_nsa", [P, 2 * KVH, SEQ], F32R, m)
                kl_nsa = sb("kl_nsa", [P, 2 * KVH, SEQ], F32R, m)
                cmp_w_sb = sb("cmp_w_sb", [P, 2, CMP_LEN // 2, HD], F32, m)
                kv_cm = sb("kv_cm", [P, 2, SEQ], F32, m)
                kv_pair = sb("kv_pair", [P, KVH, SEQ], F32, m)
                kv_pe = sb("kv_pe", [P, 2, KVH, SEQ // 16, 8], F32, m)
                with ExitStack() as w:
                    x_raw = sb("x_raw", [P, KT, SEQ], F32, w)
                with ExitStack() as w:
                    u_pad = sb("u_pad", [P, LRU_T, SEQ + CONV - 1], F32, w)
                    xc = sb("xc", [P, LRU_T, SEQ], F32, w)
                    tau = sb("tau", [P, LRU_T, SEQ], F32, w)
                    ig = sb("ig", [P, LRU_T, SEQ], F32, w)
                    lru_w_sb = sb("lru_w_sb", [P, 2, LRU_T, P], F32, w)
                with ExitStack() as w:
                    v_nsa = sb("v_nsa", [P, NT, 2 * KVH * HD], F32, w)
                    v_fox = sb("v_fox", [P, NT, HEADS * HD], F32, w)
                    o_nsa = sb("o_nsa", [P, NT, HEADS * HD], F32, w)
                    o_fox = sb("o_fox", [P, NT, HEADS * HD], F32, w)
                    probs = sb("probs", [P, 3, SEQ], F32, w)
                    pT = sb("pT", [P, 3, SEQ], F32, w)
            with ExitStack() as m:
                q_fox = sb("q_fox", [P, HEADS, SEQ], F32R, m)
                kh_fox = sb("kh_fox", [P, HEADS, SEQ], F32R, m)
                kl_fox = sb("kl_fox", [P, HEADS, SEQ], F32R, m)
            with ExitStack() as m:
                yh = sb("yh", [P, ET, SEQ], F32R, m)
                yl = sb("yl", [P, ET, SEQ], F32R, m)
        with ExitStack() as v:
            x_res = sb("x_res", [P, NT, D], F32, v)
            y_out = sb("y_out", [P, NT, D], F32, v)

        bank = [ctx.enter_context(nc.psum_tensor(f"bank{i}", [P, SEQ], F32)) for i in range(8)]
        PROJ = (bank[0], bank[1])
        AUX_A, AUX_B, MEAN = bank[2], bank[3], bank[4]
        SCORE = (bank[4], bank[5], bank[6])
        PT = (bank[7], bank[1])
        OUT = (bank[2], bank[3])

        x_loaded = [sem(f"x_loaded{k}") for k in range(KT)]
        const_loaded, chan_loaded = sem("const_loaded"), sem("chan_loaded")
        lru_w_loaded, cmp_w_loaded = sem("lru_w_loaded"), sem("cmp_w_loaded")
        raw_loaded = [sem(f"raw_loaded{i}") for i in range(RAW)]
        wh_ready, wl_ready, w_used = sem("wh_ready"), sem("wl_ready"), sem("w_used")
        xh_ready, xl_ready, x_sq = sem("xh_ready"), sem("xl_ready"), sem("x_sq")
        x_sq_used = sem("x_sq_used")
        mean_ready, std_ready = sem("mean_ready"), sem("std_ready")
        rstd_ready, rstd_T, rcol_ready = sem("rstd_ready"), sem("rstd_T"), sem("rcol_ready")
        small_consts = sem("small_consts")
        proj_done, proj_read = sem("proj_done"), sem("proj_read")
        conv_first, conv_done = sem("conv_first"), sem("conv_done")
        lru_gates, lru_sig, lru_tau = sem("lru_gates"), sem("lru_sig"), sem("lru_tau")
        lam_act, csp_ready = sem("lam_act"), sem("csp_ready")
        zl_sig, zl_done, sel_ready = sem("zl_sig"), sem("zl_done"), sem("sel_ready")
        lru_sqrt = sem("lru_sqrt")
        fg_act, gates_T, gates_ready, c_ready = sem("fg_act"), sem("gates_T"), sem("gates_ready"), sem("c_ready")
        kv_shifted = [sem("kv_shifted_k"), sem("kv_shifted_v")]
        kv_pe_ready, cmp_prod = sem("kv_pe_ready"), sem("cmp_prod")
        cmp_evac, cmp_sq, cmp_mean, cmp_std = sem("cmp_evac"), sem("cmp_sq"), sem("cmp_mean"), sem("cmp_std")
        k_cmp_n, k_cmp_hr, k_cmp_ready = sem("k_cmp_n"), sem("k_cmp_hr"), sem("k_cmp_ready")
        v_cmp_T, v_cmp_ready = sem("v_cmp_T"), sem("v_cmp_ready")
        sq_ready, norm_mean, norm_std = sem("sq_ready"), sem("norm_mean"), sem("norm_std")
        normed, h_ready, l_ready, stacked = sem("normed"), sem("h_ready"), sem("l_ready"), sem("stacked")
        cmp_s, cmp_shift, cmp_exp, cmp_p = sem("cmp_s"), sem("cmp_shift"), sem("cmp_exp"), sem("cmp_p")
        cmp_pT, cmp_pT_sb, cmp_o, cmp_o_read = sem("cmp_pT"), sem("cmp_pT_sb"), sem("cmp_o"), sem("cmp_o_read")
        s_ready, max_ready, p_ready = sem("s_ready"), sem("max_ready"), sem("p_ready")
        pT_ready, pT_dve, pT_act = sem("pT_ready"), sem("pT_dve"), sem("pT_act")
        av_done, head_done = sem("av_done"), sem("head_done")
        oT_ready, z_ready, z_sig, y_ready = sem("oT_ready"), sem("z_ready"), sem("z_sig"), sem("y_ready")
        yh_ready, yl_ready = sem("yh_ready"), sem("yl_ready")
        out_sum, out_ready, res_loaded, stored = sem("out_sum"), sem("out_ready"), sem("res_loaded"), sem("stored")

        def chain(eng, name):
            s, n = sem(name), [0]

            def link(ins):
                n[0] += 1
                ins.then_inc(s, 1)
                eng().wait_ge(s, n[0])
            return link

        def proj_units(c):
            return sum(1 if k not in TOKEN_MAJOR else NT if j % 2 == 0 else 0 for k, j in CHUNKS[:c])

        def nth_normed(c):
            return NORMED.index(c)

        def stack_copies(c):
            return sum(4 if CHUNKS[x][0] in ("nq", "fq") else 8 for x in NORMED[:c])

        heads = [("nsa", h, b) for h in range(HEADS) for b in (1, 2)] + [("fox", h, 0) for h in range(HEADS)]
        NSA_UNITS, UNITS = 2 * HEADS * NT, len(heads) * NT

        def scores_of(u):
            group, h, b = heads[u // NT]
            if group == "nsa":
                k = 2 * (b - 1) + h // GROUP
                return q_nsa[:, h, :], kh_nsa[:, k, :], kl_nsa[:, k, :]
            return q_fox[:, h, :], kh_fox[:, h, :], kl_fox[:, h, :]

        def values_of(u):
            group, h, b = heads[u // NT]
            if group == "nsa":
                k = 2 * (b - 1) + h // GROUP
                return v_nsa[:, :, k * HD:(k + 1) * HD]
            return v_fox[:, :, h * HD:(h + 1) * HD]

        def wait_pT(eng, u):
            if u % NT == NT - 1:
                eng.wait_ge(pT_act, u // NT + 1)
            else:
                eng.wait_ge(pT_dve, 3 * (u // NT) + u % NT + 1)

        def steps(first, last):
            return [(s, (lambda u: u if first <= u < last else None)) for s in range(first, last + 5)]

        block = ctx.enter_context(nc.Block())

        @block.sync
        def _(sp):
            def load_w(c):
                if c >= N_STREAM:
                    return
                if c >= RAW:
                    sp.wait_ge(wl_ready, c - RAW + 1)
                src = w_in[c] if c < N_IN else w_out[c - N_IN]
                sp.dma_start(raw[:, c % RAW, :], src).then_inc(raw_loaded[c % RAW], 16)

            def stack(c):
                kind, j = CHUNKS[c]
                n = nth_normed(c)
                sp.wait_ge(h_ready, n + 1)
                sp.wait_ge(l_ready, n + 1)
                if kind == "fq" and j == 0:
                    sp.wait_ge(s_ready, NSA_UNITS)
                for s in range(2):
                    half = slice(s * HD, (s + 1) * HD)
                    if kind in ("nq", "fq"):
                        dst = (q_nsa if kind == "nq" else q_fox)[:, 2 * j + s, :]
                        copies = [(dst[0:HD], h_stage), (dst[HD:P], l_stage)]
                    else:
                        if kind == "fk":
                            dh, dl = kh_fox[:, 2 * j + s, :], kl_fox[:, 2 * j + s, :]
                        else:
                            k = s + (KVH if kind == "kw" else 0)
                            dh, dl = kh_nsa[:, k, :], kl_nsa[:, k, :]
                        copies = [(dh[0:HD], h_stage), (dh[HD:P], h_stage), (dl[0:HD], l_stage), (dl[HD:P], l_stage)]
                    for dst, src in copies:
                        sp.dma_start(dst.bitcast(F32), src[half, :].bitcast(F32)).then_inc(stacked, 16)

            def pair_up(i):
                sp.wait_ge(proj_read, proj_units(AT["kc" if i == 0 else "vc", 0]) + 1)
                if i == 1:
                    sp.wait_ge(kv_pe_ready, 1)
                for g in range(KVH):
                    half = slice(g * HD, (g + 1) * HD)
                    sp.dma_start(kv_pair[0:HD, g, :], kv_cm[half, i, :]).then_inc(kv_shifted[i], 16)
                    sp.dma_start(kv_pair[HD:P, g, 0:SEQ - 1], kv_cm[half, i, 1:SEQ]).then_inc(kv_shifted[i], 16)

            sp.dma_start(chn[:, :], chan).then_inc(chan_loaded, 16)
            for k in range(KT):
                sp.dma_start(x_raw[:, k, :], xT[:, k, :]).then_inc(x_loaded[k], 16)
                if k == 1:
                    sp.dma_start(cst[:, :], const).then_inc(const_loaded, 16)
            load_w(0)
            load_w(1)
            sp.dma_start(cmp_w_sb[:, :, :, :], cmp_w).then_inc(cmp_w_loaded, 16)
            sp.wait_ge(xl_ready, KT)
            sp.wait_ge(x_sq, KT)
            sp.dma_start(lru_w_sb[:, :, :, :], lru_w).then_inc(lru_w_loaded, 16)
            for c in range(2, N_STREAM + 6):
                load_w(c)
                k = c - 5
                if 0 <= k < N_IN:
                    if CHUNKS[k][0] in ("kc", "vc"):
                        pair_up(0 if CHUNKS[k][0] == "kc" else 1)
                    elif k in NORMED:
                        stack(k)
                if c == N_IN + 4:
                    sp.wait_ge(w_used, N_IN)
                    sp.dma_start(x_res[:, :, :], x_tok).then_inc(res_loaded, 16)
            for t in range(NT):
                sp.wait_ge(out_ready, 2 * (t + 1))
                sp.dma_start(out[t * P:(t + 1) * P, :], y_out[:, t, :]).then_inc(stored, 16)
            sp.wait_ge(stored, 16 * NT)

        @block.gpsimd
        def _(pool):
            nc.gpsimd.memset(eps1[:, :], EPS)
            nc.gpsimd.memset(eps64[:, :], 64 * EPS)
            nc.gpsimd.memset(one1[:, :], 1.0)
            nc.gpsimd.memset(c_parts[:, :], 0.0)
            nc.gpsimd.memset(k_cmp[:, :, :], 0.0)
            nc.gpsimd.memset(v_cmp[:, :, :], 0.0)
            nc.gpsimd.memset(v_blocks[:, :, :], 0.0).then_inc(small_consts, 1)
            for c in range(N_STREAM):
                pool.wait_ge(wh_ready, c + 1)
                nc.gpsimd.tensor_tensor(wl[:, c % HL, :], raw[:, c % RAW, :], wh[:, c % HL, :].bitcast(F32),
                                        ALU.subtract).then_inc(wl_ready, 1)

        @block.scalar
        def _(act):
            link = chain(lambda: act, "act_chain")

            def split(c):
                if c >= N_STREAM:
                    return
                act.wait_ge(raw_loaded[c % RAW], 16 * (c // RAW + 1))
                if c >= HL:
                    act.wait_ge(w_used, c - HL + 1)
                act.activation(wh[:, c % HL, :], raw[:, c % RAW, :], ACT.Copy).then_inc(wh_ready, 1)

            def ch(name, j=0):
                return chn[:, CH[name] + j:CH[name] + j + 1]

            def before(c):
                kind, j = CHUNKS[c]
                if kind == "u":
                    act.wait_ge(proj_read, proj_units(c) + 1)
                    act.activation(xc[:, j, :], u_pad[:, j, 0:SEQ], ACT.Identity, bias=ch("conv_b", j),
                                   scale=ch("conv_w", j)).then_inc(conv_first, 1)
                if kind == "zl":
                    act.wait_ge(proj_read, proj_units(c) + 1)
                    act.activation(sq[:, :], y_lru[:, j, :], ACT.Sigmoid).then_inc(zl_sig, 1)
                if c in NORMED:
                    act.wait_ge(proj_read, proj_units(c) + 1)
                    n = nth_normed(c)
                    if n >= 1:
                        act.wait_ge(norm_mean, n)
                    act.activation(sq[:, :], qr[:, n % 2, :], ACT.Square).then_inc(sq_ready, 1)

            def after(c):
                kind, j = CHUNKS[c]
                if kind == "u":
                    if j == 0:
                        act.wait_ge(csp_ready, 1)
                    act.wait_ge(lru_gates, j + 1)
                    act.activation(tau[:, j, :], AUX_A[:, :], ACT.Sigmoid, bias=ch("ba", j)).then_inc(lru_sig, 1)
                    act.activation(ig[:, j, :], AUX_B[:, :], ACT.Sigmoid, bias=ch("bx", j)).then_inc(lru_sig, 1)
                    act.wait_ge(lru_sig, 2 * j + 2)
                    act.activation(tau[:, j, :], tau[:, j, :], ACT.Tanh,
                                   scale=csp[:, 0, j:j + 1]).then_inc(lru_tau, 1)
                if kind == "fg":
                    act.wait_ge(proj_read, proj_units(c) + 1)
                    b = ch("fg_b")
                    act.activation(std[0:64, :], qr[0:64, 0, :], ACT.Sigmoid, bias=b[0:64]).then_inc(fg_act, 1)
                    link(act.activation(sq[0:HEADS, :], qr[0:HEADS, 0, :], ACT.Abs, bias=b[0:HEADS]))
                    link(act.activation(sq[0:HEADS, :], sq[0:HEADS, :], ACT.Exp, scale=-1.0))
                    act.activation(sq[0:HEADS, :], sq[0:HEADS, :], ACT.Ln, bias=one1[0:HEADS, :]).then_inc(fg_act, 1)
                if c in NORMED:
                    n = nth_normed(c)
                    act.wait_ge(norm_mean, n + 1)
                    eighth = kind in ("nq", "fq")
                    act.activation(std[:, :], MEAN[:, :], ACT.Sqrt, bias=(eps64 if eighth else eps1)[:, :],
                                   scale=64.0 if eighth else 1.0).then_inc(norm_std, 1)
                    act.wait_ge(normed, n + 1)
                    if n >= 1:
                        act.wait_ge(stacked, 16 * stack_copies(n))
                    act.activation(h_stage[:, :], qr[:, n % 2, :], ACT.Copy).then_inc(h_ready, 1)

            def unit_exp(u):
                v, t = divmod(u, NT)
                act.wait_ge(max_ready, u + 1)
                if u >= 3:
                    act.wait_ge(pT_ready, u - 2)
                if v >= 3:
                    act.wait_ge(head_done, v - 2)
                n = (t + 1) * P
                act.activation(probs[:, u % 3, 0:n], SCORE[u % 3][:, 0:n], ACT.Exp, bias=negmax[:, u % 4:u % 4 + 1],
                               accum_out=rsum[:, v % 3, t:t + 1]).then_inc(p_ready, 1)

            def attention(first, last):
                for s, inside in steps(first, last):
                    if inside(s) is not None:
                        unit_exp(s)
                    u = inside(s - 2)
                    if u is not None and u % NT == NT - 1:
                        act.wait_ge(pT_ready, u + 1)
                        if u >= 3:
                            act.wait_ge(av_done, u - 2)
                        act.activation(pT[:, u % 3, :], PT[u % 2][:, :], ACT.Copy).then_inc(pT_act, 1)

            act.wait_ge(chan_loaded, 16)
            act.wait_ge(small_consts, 1)
            lam = chn[:, CH["lam"]:CH["lam"] + LRU_T]
            link(act.activation(csp[:, 1, :], lam, ACT.Abs))
            link(act.activation(csp[:, 1, :], csp[:, 1, :], ACT.Exp, scale=-1.0))
            act.activation(csp[:, 1, :], csp[:, 1, :], ACT.Ln, bias=one1[:, :]).then_inc(lam_act, 1)
            for k in range(KT):
                act.wait_ge(x_loaded[k], 16)
                act.activation(xh[:, k, :], x_raw[:, k, :], ACT.Copy, scale=ch("norm_g", k)).then_inc(xh_ready, 1)
            for c in range(AHEAD):
                split(c)
            act.wait_ge(mean_ready, 1)
            act.activation(rstd_bc[:, :], MEAN[:, :], ACT.Sqrt, bias=eps1[:, :], scale=1.0 / D).then_inc(std_ready, 1)
            for c in range(NSA_END):
                split(c + AHEAD)
                before(c)
                if c >= 1:
                    after(c - 1)
                if c == AT["fg", 0] + 1:
                    act.wait_ge(lru_tau, LRU_T)
                    for j in range(LRU_T):
                        act.wait_ge(conv_done, LRU_T)
                        act.wait_ge(lru_gates, LRU_T)
                        act.activation(u_pad[:, j, 0:SEQ], tau[:, j, :], ACT.Sqrt, scale=4.0).then_inc(lru_sqrt, 1)
                if c == AT["nq", 1]:
                    act.wait_ge(cmp_evac, 1)
                    act.activation(k_cmp_sq[:, :, :], k_cmp[:, :, :], ACT.Square).then_inc(cmp_sq, 1)
                if c == AT["nq", 3]:
                    act.wait_ge(cmp_mean, 1)
                    act.activation(k_cmp_sq[:, :, :], AUX_A[0:HD, 0:KVH * CMP_PAD].rearrange(
                        "p (g n) -> p g n", g=KVH), ACT.Sqrt, bias=eps1[0:HD, :]).then_inc(cmp_std, 1)
                if c == AT["vn", 0]:
                    act.wait_ge(k_cmp_n, 1)
                    for half in (slice(0, HD), slice(HD, P)):
                        act.activation(k_cmp_h[half, :, :], k_cmp[:, :, :], ACT.Copy).then_inc(k_cmp_hr, 1)
            for t in range(NT):
                act.wait_ge(cmp_shift, t + 1)
                act.activation(probs[:, t % 2, 0:HEADS * CMP_PAD], probs[:, t % 2, 0:HEADS * CMP_PAD],
                               ACT.Exp).then_inc(cmp_exp, 1)
            attention(0, NSA_UNITS)
            for c in range(NSA_END, FOX_END):
                split(c + AHEAD)
                before(c)
                after(c - 1)
            after(FOX_END - 1)
            attention(NSA_UNITS, UNITS)
            act.wait_ge(s_ready, UNITS)
            for e in range(LRU_T):
                act.activation(yh[:, e, :], y_lru[:, e, :], ACT.Copy).then_inc(yh_ready, 1)
            for c in range(FOX_END, N_IN):
                split(c + AHEAD)
                i = c - FOX_END
                act.wait_ge(z_ready, i + 1)
                act.activation(sq[:, :], qr[:, i % 2, :], ACT.Sigmoid).then_inc(z_sig, 1)
                act.wait_ge(y_ready, i + 1)
                act.activation(yh[:, LRU_T + i, :], qr[:, i % 2, :], ACT.Copy).then_inc(yh_ready, 1)
            for e in range(ET):
                split(N_IN + e + AHEAD)

        @block.vector
        def _(dve):
            link = chain(lambda: dve, "dve_chain")

            def ch(name, j=0):
                return chn[:, CH[name] + j:CH[name] + j + 1]

            def evac(c):
                kind, j = CHUNKS[c]
                if kind in TOKEN_MAJOR:
                    if j % 2:
                        return
                    for t in range(NT):
                        unit = proj_units(c) + t
                        dve.wait_ge(proj_done, unit + 1)
                        if kind == "vn":
                            dst = v_nsa[:, t, :]
                        else:
                            dst = v_fox[:, t, j * P:(j + 2) * P]
                        dve.tensor_scalar(dst, PROJ[unit % 2][:, 0:2 * P], rstd_col[:, t:t + 1], None,
                                          ALU.mult).then_inc(proj_read, 1)
                    return
                unit = proj_units(c)
                dve.wait_ge(proj_done, unit + 1)
                rows = 64 if kind == "fg" else P
                if kind == "u":
                    dst = u_pad[:, j, CONV - 1:]
                elif kind == "zl":
                    dst = y_lru[:, j, :]
                elif kind in ("kc", "vc"):
                    dst = kv_cm[:, 0 if kind == "kc" else 1, :]
                elif kind == "fg":
                    dst = qr[0:64, 0, :]
                elif kind in ("zn", "zf"):
                    dst = qr[:, (c - FOX_END) % 2, :]
                    if c - FOX_END >= 2:
                        dve.wait_ge(yl_ready, LRU_T + c - FOX_END - 1)
                else:
                    n = nth_normed(c)
                    dst = qr[:, n % 2, :]
                    if n >= 2:
                        dve.wait_ge(l_ready, n - 1)
                dve.tensor_tensor(dst, PROJ[unit % 2][0:rows, :], rstd_bc[0:rows, :], ALU.mult).then_inc(proj_read, 1)

            def before(c):
                evac(c)
                kind, j = CHUNKS[c]
                if kind == "u":
                    for k in range(1, CONV):
                        if k == 1:
                            dve.wait_ge(conv_first, j + 1)
                        ins = dve.scalar_tensor_tensor(xc[:, j, :], u_pad[:, j, k:k + SEQ],
                                                       ch("conv_w", k * LRU_T + j), xc[:, j, :], ALU.mult, ALU.add)
                        if k < CONV - 1:
                            link(ins)
                        else:
                            ins.then_inc(conv_done, 1)
                if kind == "zl":
                    dve.wait_ge(zl_sig, j + 1)
                    dve.tensor_tensor(y_lru[:, j, :], y_lru[:, j, :], sq[:, :], ALU.mult).then_inc(zl_done, 1)

            def after(c):
                kind, j = CHUNKS[c]
                if c in NORMED:
                    n = nth_normed(c)
                    dve.wait_ge(norm_std, n + 1)
                    link(dve.reciprocal(std[:, :], std[:, :]))
                    dve.scalar_tensor_tensor(qr[:, n % 2, :], qr[:, n % 2, :], ch(GAIN[kind]), std[:, :], ALU.mult,
                                             ALU.mult).then_inc(normed, 1)
                    dve.wait_ge(h_ready, n + 1)
                    dve.tensor_tensor(l_stage[:, :], qr[:, n % 2, :], h_stage[:, :].bitcast(F32),
                                      ALU.subtract).then_inc(l_ready, 1)
                if kind == "fg":
                    forget_gates()

            def forget_gates():
                f = qr[0:HEADS, 0, :]
                a, b = qr[0:HEADS, 1, :], c_work[0:HEADS, :]
                dve.wait_ge(fg_act, 2)
                link(dve.tensor_scalar(f, f, ch("fg_b")[0:HEADS], 0.0, ALU.add, ALU.min))
                link(dve.tensor_tensor(f, f, sq[0:HEADS, :], ALU.subtract))
                link(dve.memset(a, 1.0))
                link(dve.tensor_tensor_scan(b, a, f, 0.0, ALU.mult, ALU.subtract))
                dve.wait_ge(small_consts, 1)
                link(dve.tensor_copy(c_parts[0:HEADS, :], b))
                link(dve.tensor_tensor(b, b, c_parts[0:HEADS, :], ALU.subtract))
                link(dve.tensor_copy(c_mid[0:HEADS, :], b))
                link(dve.tensor_tensor(b, b, c_mid[0:HEADS, :], ALU.subtract))
                dve.tensor_copy(c_parts[32:32 + HEADS, :], c_mid[0:HEADS, :])
                dve.tensor_copy(c_parts[64:64 + HEADS, :], b).then_inc(c_ready, 1)

            def branch_gates():
                dve.wait_ge(gates_T, 1)
                dve.tensor_copy(gates[:, :, :], AUX_A[:, 0:NT * 64].rearrange("p (t c) -> p t c", t=NT)
                                [:, :, 32:32 + 3 * HEADS]).then_inc(gates_ready, 1)

            def lru_tail(j):
                t, r, g = tau[:, j, :], u_pad[:, j, 0:SEQ], ig[:, j, :]
                dve.wait_ge(lru_sqrt, j + 1)
                link(dve.tensor_tensor(g, g, xc[:, j, :], ALU.mult))
                link(dve.tensor_tensor(g, g, r, ALU.mult))
                link(dve.tensor_scalar(r, t, 1.0, None, ALU.add))
                link(dve.tensor_scalar(t, t, -1.0, 1.0, ALU.mult, ALU.add))
                link(dve.reciprocal(r, r))
                link(dve.tensor_tensor(t, t, r, ALU.mult))
                link(dve.tensor_tensor(g, g, r, ALU.mult))
                link(dve.tensor_tensor_scan(r, t, g, 0.0, ALU.mult, ALU.add))
                link(dve.tensor_tensor(y_lru[:, j, :], y_lru[:, j, :], r, ALU.mult))

            def pair_pe(i):
                dve.wait_ge(kv_shifted[i], 64)
                if i == 1:
                    dve.wait_ge(cmp_prod, 1)
                pairs = kv_pair[:, :, :].rearrange("p g (n j two) -> p g n j two", j=8, two=2)
                for part in range(2):
                    o = CH["pe_k" if i == 0 else "pe_v"] + 8 * part
                    for g in range(KVH):
                        pe_row = chn[:, o:o + 8].unsqueeze(1).broadcast_to([P, SEQ // 16, 8])
                        ins = dve.tensor_tensor(kv_pe[:, part, g, :, :], pairs[:, g, :, :, 0], pe_row, ALU.add)
                ins.then_inc(kv_pe_ready, 1)

            def cmp_out(i):
                dve.wait_ge(cmp_prod, i + 1)
                dve.wait_ge(small_consts, 1)
                src = (AUX_A if i == 0 else AUX_B)[0:HD, 0:KVH * CMP_PAD].rearrange("p (g n) -> p g n", g=KVH)
                dve.tensor_copy((k_cmp if i == 0 else v_cmp)[:, :, 0:N_CMP], src[:, :, 0:N_CMP]).then_inc(cmp_evac, 1)

            def cmp_norm():
                dve.wait_ge(cmp_std, 1)
                link(dve.reciprocal(k_cmp_sq[:, :, :], k_cmp_sq[:, :, :]))
                flat = [x[:, :, :].rearrange("p g n -> p (g n)") for x in (k_cmp, k_cmp_sq)]
                dve.scalar_tensor_tensor(flat[0], flat[0], ch("kcmp_g")[0:HD], flat[1], ALU.mult,
                                         ALU.mult).then_inc(k_cmp_n, 1)
                dve.wait_ge(k_cmp_hr, 2)
                for half in (slice(0, HD), slice(HD, P)):
                    dve.tensor_tensor(k_cmp_l[half, :, :], k_cmp[:, :, :], k_cmp_h[0:HD, :, :].bitcast(F32),
                                      ALU.subtract).then_inc(k_cmp_ready, 1)

            def cmp_values():
                dve.wait_ge(v_cmp_T, 1)
                for g in range(KVH):
                    for r in range(GROUP):
                        dve.tensor_copy(v_blocks[32 * r:32 * r + 32, g, r * HD:(r + 1) * HD],
                                        AUX_B[0:CMP_PAD, g * HD:(g + 1) * HD]).then_inc(v_cmp_ready, 1)

            def cmp_attention():
                for t in range(NT):
                    s3 = SCORE[t % 2][:, 0:HEADS * CMP_PAD].rearrange("p (h n) -> p h n", h=HEADS)
                    p3 = probs[:, t % 2, 0:HEADS * CMP_PAD].rearrange("p (h n) -> p h n", h=HEADS)
                    mask = cst[:, CMPMASK + t * CMP_PAD:CMPMASK + (t + 1) * CMP_PAD]
                    mx, sm, rc = (cmp_stat[:, i, :] for i in range(3))
                    dve.wait_ge(cmp_s, t + 1)
                    if t >= 2:
                        dve.wait_ge(cmp_pT, t - 1)
                    link(dve.tensor_tensor(p3, s3, mask.unsqueeze(1).broadcast_to([P, HEADS, CMP_PAD]), ALU.add))
                    link(dve.tensor_reduce(mx, p3, AX.X, ALU.max))
                    link(dve.tensor_scalar(mx, mx, NEG / 10, None, ALU.max))
                    dve.tensor_tensor(p3, p3, mx.unsqueeze(2).broadcast_to([P, HEADS, CMP_PAD]),
                                      ALU.subtract).then_inc(cmp_shift, 1)
                    dve.wait_ge(cmp_exp, t + 1)
                    link(dve.tensor_reduce(sm, p3, AX.X, ALU.add))
                    link(dve.tensor_scalar(sm, sm, 1e-30, None, ALU.max))
                    link(dve.reciprocal(rc, sm))
                    link(dve.tensor_tensor(rc, rc, gates[:, t, 0:3 * HEADS:3], ALU.mult))
                    dve.tensor_tensor(p3, p3, rc.unsqueeze(2).broadcast_to([P, HEADS, CMP_PAD]),
                                      ALU.mult).then_inc(cmp_p, 1)
                    dve.wait_ge(cmp_pT, t + 1)
                    if t >= 1:
                        dve.wait_ge(cmp_o, t)
                    dve.tensor_copy(pT[:, 0, 0:2 * P], PT[0][:, 0:2 * P]).then_inc(cmp_pT_sb, 1)
                    dve.wait_ge(cmp_o, t + 1)
                    dve.tensor_copy(o_nsa[:, t, :], OUT[t % 2][:, :]).then_inc(cmp_o_read, 1)

            def finish_head(v):
                group, h, b = heads[v]
                dve.wait_ge(av_done, NT * (v + 1))
                link(dve.reciprocal(rcp[:, 0, :], rsum[:, v % 3, :]))
                o = OUT[v % 2][:, 0:NT * HD].rearrange("p (t d) -> p t d", t=NT)
                if group == "nsa":
                    link(dve.tensor_tensor(rcp[:, 0, :], rcp[:, 0, :], gates[:, :, 3 * h + b], ALU.mult))
                    scaled = head_out[:, :].rearrange("p (t d) -> p t d", t=NT)
                    link(dve.tensor_tensor(scaled, o, rcp[:, 0, :].unsqueeze(2).broadcast_to([P, NT, HD]), ALU.mult))
                    acc = o_nsa[:, :, h * HD:(h + 1) * HD]
                    dve.tensor_tensor(acc, acc, scaled, ALU.add).then_inc(head_done, 1)
                else:
                    dve.tensor_tensor(o_fox[:, :, h * HD:(h + 1) * HD], o,
                                      rcp[:, 0, :].unsqueeze(2).broadcast_to([P, NT, HD]),
                                      ALU.mult).then_inc(head_done, 1)

            def attention(first, last):
                for s, inside in steps(first, last):
                    if inside(s) is not None:
                        n = (s % NT + 1) * P
                        dve.wait_ge(s_ready, s + 1)
                        dve.tensor_reduce(negmax[:, s % 4:s % 4 + 1], SCORE[s % 3][:, 0:n], AX.X, ALU.max,
                                          negate=True).then_inc(max_ready, 1)
                    u = inside(s - 2)
                    if u is not None and u % NT < NT - 1:
                        n = (u % NT + 1) * P
                        dve.wait_ge(pT_ready, u + 1)
                        if u >= 3:
                            dve.wait_ge(av_done, u - 2)
                        dve.tensor_copy(pT[:, u % 3, 0:n], PT[u % 2][:, 0:n]).then_inc(pT_dve, 1)
                    u = inside(s - 4)
                    if u is not None and u % NT == NT - 1:
                        finish_head(u // NT)

            dve.wait_ge(chan_loaded, 16)
            for k in range(KT):
                dve.wait_ge(x_loaded[k], 16)
                if k >= 2:
                    dve.wait_ge(x_sq_used, k - 1)
                dve.tensor_tensor(qr[:, k % 2, :], x_raw[:, k, :], x_raw[:, k, :], ALU.mult).then_inc(x_sq, 1)
                dve.wait_ge(xh_ready, k + 1)
                dve.scalar_tensor_tensor(xl[:, k, :], x_raw[:, k, :], ch("norm_g", k), xh[:, k, :].bitcast(F32),
                                         ALU.mult, ALU.subtract).then_inc(xl_ready, 1)
            dve.wait_ge(const_loaded, 16)
            dve.tensor_copy(ident_b[:, :], ident)
            dve.tensor_copy(mask_b[:, :], cst[:, CAUSAL:CAUSAL + P])
            sel = c_work[0:96, 0:HEADS]
            link(dve.tensor_tensor(sel, cst[0:96, IDENT:IDENT + HEADS], cst[0:96, IDENT + 32:IDENT + 32 + HEADS],
                                   ALU.add))
            link(dve.tensor_tensor(sel, sel, cst[0:96, IDENT + 64:IDENT + 64 + HEADS], ALU.add))
            dve.tensor_copy(head_sel[:, :, :], sel.unsqueeze(2).broadcast_to([96, HEADS, P])).then_inc(sel_ready, 1)
            dve.wait_ge(lam_act, 1)
            lam = chn[:, CH["lam"]:CH["lam"] + LRU_T]
            link(dve.tensor_scalar(csp[:, 0, :], lam, -1.0, 0.0, ALU.mult, ALU.max))
            link(dve.tensor_tensor(csp[:, 0, :], csp[:, 0, :], csp[:, 1, :], ALU.add))
            dve.tensor_scalar(csp[:, 0, :], csp[:, 0, :], 4.0, None, ALU.mult).then_inc(csp_ready, 1)
            dve.wait_ge(x_sq_used, KT)
            dve.memset(u_pad[:, :, 0:CONV - 1], 0.0)
            dve.wait_ge(std_ready, 1)
            dve.reciprocal(rstd_bc[:, :], rstd_bc[:, :]).then_inc(rstd_ready, 1)
            dve.wait_ge(rstd_ready, 1)
            for c in range(NSA_END):
                before(c)
                if c >= 1:
                    after(c - 1)
                if c == AT["zl", 1]:
                    dve.wait_ge(rstd_T, 1)
                    dve.tensor_copy(rstd_col[:, :], AUX_B[:, :].rearrange("p (t c) -> p t c", t=NT)[:, :, 0])\
                       .then_inc(rcol_ready, 1)
                if c == AT["kc", 0]:
                    branch_gates()
                if AT["kc", 0] <= c < AT["kc", 0] + LRU_T:
                    lru_tail(c - AT["kc", 0])
                if c == AT["kw", 0]:
                    pair_pe(0)
                if c == AT["nq", 0]:
                    cmp_out(0)
                    pair_pe(1)
                if c == AT["nq", 1]:
                    cmp_out(1)
                if c == AT["nq", 3]:
                    cmp_values()
                if c == AT["vn", 0]:
                    cmp_norm()
            cmp_attention()
            attention(0, NSA_UNITS)
            for c in range(NSA_END, FOX_END):
                before(c)
                after(c - 1)
            after(FOX_END - 1)
            attention(NSA_UNITS, UNITS)
            dve.wait_ge(s_ready, UNITS)
            for e in range(LRU_T):
                dve.wait_ge(yh_ready, e + 1)
                dve.tensor_tensor(yl[:, e, :], y_lru[:, e, :], yh[:, e, :].bitcast(F32),
                                  ALU.subtract).then_inc(yl_ready, 1)
            for c in range(FOX_END, N_IN):
                i = c - FOX_END
                evac(c)
                dve.wait_ge(proj_read, proj_units(c) + 1)
                z = qr[:, i % 2, :]
                dve.nop().then_inc(z_ready, 1)
                dve.wait_ge(oT_ready, i + 1)
                dve.wait_ge(z_sig, i + 1)
                link(dve.tensor_tensor(z, z, sq[:, :], ALU.mult))
                dve.tensor_tensor(z, z, OUT[i % 2][:, :], ALU.mult).then_inc(y_ready, 1)
                dve.wait_ge(yh_ready, LRU_T + i + 1)
                dve.tensor_tensor(yl[:, LRU_T + i, :], z, yh[:, LRU_T + i, :].bitcast(F32),
                                  ALU.subtract).then_inc(yl_ready, 1)
            dve.wait_ge(res_loaded, 16)
            for t in range(NT):
                for half in range(2):
                    dve.wait_ge(out_sum, 2 * t + half + 1)
                    cols = slice(half * 512, (half + 1) * 512)
                    dve.tensor_tensor(y_out[:, t, cols], bank[2 * t + half][:, :], x_res[:, t, cols],
                                      ALU.add).then_inc(out_ready, 1)

        @block.tensor
        def _(pe):
            def project(c):
                kind, j = CHUNKS[c]
                slot = c % HL
                if kind in TOKEN_MAJOR:
                    if j % 2:
                        return
                    pe.wait_ge(wl_ready, c + 2)
                    hi = wh[:, slot:slot + 2, :].rearrange("p s (k c) -> p k s c", k=KT)
                    lo = wl[:, slot:slot + 2, :].rearrange("p s (k c) -> p k s c", k=KT)
                    for t in range(NT):
                        unit = proj_units(c) + t
                        if unit >= 2:
                            pe.wait_ge(proj_read, unit - 1)
                        dst = PROJ[unit % 2][:, 0:2 * P].rearrange("p (s c) -> p s c", s=2)
                        toks = slice(t * P, (t + 1) * P)
                        for k in range(KT):
                            pe.matmul(dst, xh[:, k, toks], hi[:, k], start=(k == 0), stop=False)
                            pe.matmul(dst, xh[:, k, toks], lo[:, k], start=False, stop=False)
                            mm = pe.matmul(dst, xl[:, k, toks], hi[:, k], start=False, stop=(k == KT - 1))
                        if t < NT - 1:
                            mm.then_inc(proj_done, 1)
                    mm.then_inc(proj_done, 1)
                    pe.wait_ge(proj_done, proj_units(c) + NT)
                    pe.nop().then_inc(w_used, 2)
                    return
                unit = proj_units(c)
                if unit >= 2:
                    pe.wait_ge(proj_read, unit - 1)
                pe.wait_ge(wl_ready, c + 1)
                m = 64 if kind == "fg" else P
                dst = PROJ[unit % 2][0:m, :]
                for k in range(KT):
                    if c == 0:
                        pe.wait_ge(xl_ready, k + 1)
                    hi, lo = wh[:, slot, k * P:k * P + m], wl[:, slot, k * P:k * P + m]
                    pe.matmul(dst, hi, xh[:, k, :], start=(k == 0), stop=False)
                    pe.matmul(dst, hi, xl[:, k, :], start=False, stop=False)
                    mm = pe.matmul(dst, lo, xh[:, k, :], start=False, stop=(k == KT - 1))
                mm.then_inc(proj_done, 1)
                pe.wait_ge(proj_done, unit + 1)
                pe.nop().then_inc(w_used, 1)

            def head_mean(c):
                n = nth_normed(c)
                pe.wait_ge(sq_ready, n + 1)
                if n >= 1:
                    pe.wait_ge(norm_std, n)
                pe.matmul(MEAN[:, :], block_mean, sq[:, :], start=True, stop=True).then_inc(norm_mean, 1)

            def gates_of(j):
                pe.wait_ge(conv_done, j + 1)
                if j >= 1:
                    pe.wait_ge(lru_sig, 2 * j)
                if j == 0:
                    pe.wait_ge(lru_w_loaded, 16)
                pe.matmul(AUX_A[:, :], lru_w_sb[:, 0, j, :], xc[:, j, :], start=True, stop=True)
                pe.matmul(AUX_B[:, :], lru_w_sb[:, 1, j, :], xc[:, j, :], start=True, stop=True)\
                    .then_inc(lru_gates, 1)

            def compress(i):
                pe.wait_ge(kv_pe_ready, i + 1)
                pe.wait_ge(cmp_w_loaded, 16)
                dst = (AUX_A if i == 0 else AUX_B)[0:HD, 0:KVH * CMP_PAD].rearrange("p (g n) -> p g n", g=KVH)
                for j in range(CMP_LEN // 2):
                    part = j // 8
                    mm = pe.matmul(dst[:, :, 0:N_CMP], cmp_w_sb[:, i, j, :],
                                   kv_pe[:, part, :, part:part + N_CMP, j % 8],
                                   start=(j == 0), stop=(j == CMP_LEN // 2 - 1))
                mm.then_inc(cmp_prod, 1)

            def cmp_attention():
                pe.wait_ge(k_cmp_ready, 2)
                pe.wait_ge(v_cmp_ready, KVH * GROUP)
                pe.wait_ge(stacked, 16 * stack_copies(6))
                pe.wait_ge(proj_read, proj_units(NSA_END))
                pe.wait_ge(norm_std, 6)

                def scores(t):
                    if t >= 2:
                        pe.wait_ge(cmp_shift, t - 1)
                    for h in range(HEADS):
                        dst = SCORE[t % 2][:, h * CMP_PAD:(h + 1) * CMP_PAD]
                        q = q_nsa[:, h, t * P:(t + 1) * P]
                        pe.matmul(dst, q, k_cmp_h[:, h // GROUP, :], start=True, stop=False)
                        mm = pe.matmul(dst, q, k_cmp_l[:, h // GROUP, :], start=False, stop=True)
                    mm.then_inc(cmp_s, 1)

                scores(0)
                for t in range(NT):
                    if t + 1 < NT:
                        scores(t + 1)
                    pe.wait_ge(cmp_p, t + 1)
                    if t >= 1:
                        pe.wait_ge(cmp_pT_sb, t)
                    for g in range(KVH):
                        mm = pe.transpose(PT[0][:, g * P:(g + 1) * P], probs[:, t % 2, g * P:(g + 1) * P], ident)
                    mm.then_inc(cmp_pT, 1)
                    pe.wait_ge(cmp_pT_sb, t + 1)
                    if t >= 2:
                        pe.wait_ge(cmp_o_read, t - 1)
                    for g in range(KVH):
                        mm = pe.matmul(OUT[t % 2][:, g * GROUP * HD:(g + 1) * GROUP * HD], pT[:, 0, g * P:(g + 1) * P],
                                       v_blocks[:, g, :], start=True, stop=True)
                    mm.then_inc(cmp_o, 1)
                pe.wait_ge(cmp_o_read, NT)

            def unit_scores(u):
                v, t = divmod(u, NT)
                n = (t + 1) * P
                q, kh, kl = scores_of(u)
                if u >= 3:
                    pe.wait_ge(p_ready, u - 2)
                dst, q = SCORE[u % 3], q[:, t * P:(t + 1) * P]
                pe.matmul(dst[:, 0:n], q, kh[:, 0:n], start=True, stop=False)
                pe.matmul(dst[:, t * P:n], ident_b[:, :], mask_b[:, :], start=False, stop=False)
                if heads[v][0] == "fox":
                    pe.matmul(dst[:, 0:n], head_sel[:, heads[v][1], :], c_parts[:, 0:n], start=False, stop=False)
                pe.matmul(dst[:, 0:n], q, kl[:, 0:n], start=False, stop=True).then_inc(s_ready, 1)

            def unit_transpose(u):
                pe.wait_ge(p_ready, u + 1)
                if u >= 2:
                    wait_pT(pe, u - 2)
                for j in range(u % NT + 1):
                    cols = slice(j * P, (j + 1) * P)
                    mm = pe.transpose(PT[u % 2][:, cols], probs[:, u % 3, cols], ident)
                mm.then_inc(pT_ready, 1)

            def unit_values(u):
                v, t = divmod(u, NT)
                wait_pT(pe, u)
                if v >= 2 and t == 0:
                    pe.wait_ge(head_done, v - 1)
                val = values_of(u)
                for j in range(t + 1):
                    mm = pe.matmul(OUT[v % 2][:, t * HD:(t + 1) * HD], pT[:, u % 3, j * P:(j + 1) * P], val[:, j, :],
                                   start=(j == 0), stop=(j == t))
                mm.then_inc(av_done, 1)

            def attention(first, last):
                for s, inside in steps(first, last):
                    if inside(s) is not None:
                        unit_scores(s)
                    if inside(s - 2) is not None:
                        unit_transpose(s - 2)
                    if inside(s - 3) is not None:
                        unit_values(s - 3)

            pe.wait_ge(const_loaded, 16)
            for k in range(KT):
                pe.wait_ge(x_sq, k + 1)
                mm = pe.matmul(MEAN[:, :], ones, qr[:, k % 2, :], start=(k == 0), stop=(k == KT - 1))
                if k < KT - 1:
                    mm.then_inc(x_sq_used, 1)
            mm.then_inc(x_sq_used, 1)
            pe.wait_ge(x_sq_used, KT)
            pe.nop().then_inc(mean_ready, 1)
            for c in range(NSA_END):
                project(c)
                if c >= 1 and CHUNKS[c - 1][0] == "u":
                    gates_of(CHUNKS[c - 1][1])
                if c >= 1 and c - 1 in NORMED:
                    head_mean(c - 1)
                if c == AT["zl", 1]:
                    pe.wait_ge(rstd_ready, 1)
                    pe.wait_ge(lru_sig, 2 * LRU_T)
                    for t in range(NT):
                        mm = pe.transpose(AUX_B[:, t * P:(t + 1) * P], rstd_bc[:, t * P:(t + 1) * P], ident)
                    mm.then_inc(rstd_T, 1)
                if c == AT["kc", 0]:
                    pe.wait_ge(fg_act, 1)
                    for t in range(NT):
                        mm = pe.transpose(AUX_A[:, t * 64:(t + 1) * 64], std[0:64, t * P:(t + 1) * P], ident[0:64, 0:64])
                    mm.then_inc(gates_T, 1)
                if c == AT["nq", 0]:
                    pe.wait_ge(gates_ready, 1)
                    compress(0)
                if c == AT["nq", 1]:
                    pe.wait_ge(rcol_ready, 1)
                    compress(1)
                if c == AT["nq", 2]:
                    pe.wait_ge(cmp_sq, 1)
                    pe.matmul(AUX_A[0:HD, 0:KVH * CMP_PAD], block_mean[0:HD, 0:HD],
                              k_cmp_sq[:, :, :].rearrange("p g n -> p (g n)"), start=True, stop=True)\
                        .then_inc(cmp_mean, 1)
                    pe.wait_ge(cmp_evac, 2)
                    for g in range(KVH):
                        mm = pe.transpose(AUX_B[0:CMP_PAD, g * HD:(g + 1) * HD], v_cmp[:, g, :], ident[0:HD, 0:HD])
                    mm.then_inc(v_cmp_T, 1)
            cmp_attention()
            attention(0, NSA_UNITS)
            wait_pT(pe, NSA_UNITS - 1)
            for c in range(NSA_END, FOX_END):
                project(c)
                if c - 1 in NORMED:
                    head_mean(c - 1)
            head_mean(FOX_END - 1)
            pe.wait_ge(stacked, 16 * stack_copies(len(NORMED)))
            pe.wait_ge(proj_read, proj_units(FOX_END))
            pe.wait_ge(norm_std, len(NORMED))
            pe.wait_ge(c_ready, 1)
            attention(NSA_UNITS, UNITS)
            pe.wait_ge(head_done, len(heads))
            for c in range(FOX_END, N_IN):
                project(c)
                i = c - FOX_END
                if i >= 2:
                    pe.wait_ge(y_ready, i - 1)
                src = o_nsa if i < 4 else o_fox
                for t in range(NT):
                    mm = pe.transpose(OUT[i % 2][:, t * P:(t + 1) * P], src[:, t, (i % 4) * P:(i % 4 + 1) * P], ident)
                mm.then_inc(oT_ready, 1)
            pe.wait_ge(y_ready, 8)
            pe.wait_ge(proj_read, proj_units(N_IN))
            for e in range(ET):
                c = N_IN + e
                pe.wait_ge(wl_ready, c + 1)
                pe.wait_ge(yl_ready, e + 1)
                for t in range(NT):
                    toks = slice(t * P, (t + 1) * P)
                    for half in range(2):
                        dst = bank[2 * t + half][:, :]
                        cols = slice(half * 512, (half + 1) * 512)
                        pe.matmul(dst, yh[:, e, toks], wh[:, c % HL, cols], start=(e == 0), stop=False)
                        pe.matmul(dst, yh[:, e, toks], wl[:, c % HL, cols], start=False, stop=False)
                        mm = pe.matmul(dst, yl[:, e, toks], wh[:, c % HL, cols], start=False, stop=(e == ET - 1))
                        if e == ET - 1:
                            mm.then_inc(out_sum, 1)
                if e < ET - 1:
                    mm.then_inc(w_used, 1)


def pack(x, norm_g, w_in, w_out, conv_w, conv_b, lru_wa, lru_ba, lru_wx, lru_bx, lru_lambda, nsa_q_g, nsa_k_g,
         cmp_pe_k, cmp_pe_v, cmp_wk, cmp_wv, nsa_gate_b, fox_q_g, fox_k_g, fox_f_b):
    f = np.float32
    w = w_in[0]
    chunks = np.zeros((N_IN, P, KT, P), f)
    for c, (kind, j) in enumerate(CHUNKS):
        if kind == "fg":
            chunks[c, :, :, 0:HEADS] = w[:, COLS["fl"]:COLS["fl"] + HEADS].reshape(KT, P, -1).transpose(1, 0, 2)
            chunks[c, :, :, 32:32 + 3 * HEADS] = (
                w[:, COLS["gl"]:COLS["gl"] + 3 * HEADS].reshape(KT, P, -1).transpose(1, 0, 2))
            continue
        o = COLS[("vs", "vw")[j]] if kind == "vn" else COLS[kind] + j * P
        chunks[c] = w[:, o:o + P].reshape(KT, P, P).transpose(1, 0, 2)
    chan = np.zeros((P, CH_W), f)

    def put(name, a):
        a = np.asarray(a)
        chan[0:a.shape[0], CH[name]:CH[name] + a.shape[1]] = a

    put("norm_g", norm_g[0].reshape(KT, P).T)
    put("conv_w", conv_w[0].reshape(CONV * LRU_T, P).T)
    for name, a in (("conv_b", conv_b), ("ba", lru_ba), ("bx", lru_bx), ("lam", lru_lambda)):
        put(name, a[0].reshape(LRU_T, P).T)
    for name, a in (("nq_g", nsa_q_g[0]), ("kcmp_g", nsa_k_g[0, 0]), ("ks_g", nsa_k_g[0, 1]), ("kw_g", nsa_k_g[0, 2]),
                    ("fq_g", fox_q_g[0]), ("fk_g", fox_k_g[0])):
        put(name, np.concatenate([a, a])[:, None])
    chan[0:HEADS, CH["fg_b"]] = fox_f_b[0]
    chan[32:32 + 3 * HEADS, CH["fg_b"]] = nsa_gate_b[0]
    for name, a in (("pe_k", cmp_pe_k), ("pe_v", cmp_pe_v)):
        put(name, a[0].reshape(CMP_LEN // 2, 2, HD).transpose(1, 2, 0).reshape(P, CMP_LEN // 2))
    lru = np.zeros((P, 2, LRU_T, P), f)
    for i, a in enumerate((lru_wa[0], lru_wx[0])):
        for b in range(2 * LRU_T):
            r = (b % 2) * HD
            lru[r:r + HD, i, b // 2, r:r + HD] = a[b]
    cmp = np.stack([a[0].reshape(CMP_LEN // 2, 2, HD, HD).transpose(1, 2, 0, 3).reshape(P, CMP_LEN // 2, HD)
                    for a in (cmp_wk, cmp_wv)], axis=1)
    return {
        "xT": x[0].T.reshape(KT, P, SEQ).transpose(1, 0, 2),
        "x_tok": x[0].reshape(NT, P, D).transpose(1, 0, 2),
        "w_in": chunks.reshape(N_IN, P, D),
        "w_out": w_out[0].reshape(ET, P, D),
        "chan": chan, "const": constants(), "lru_w": lru, "cmp_w": cmp,
    }


def constants():
    c = np.zeros((P, CONST_W), np.float32)
    i = np.arange(P)
    c[:, IDENT:IDENT + P] = np.eye(P)
    c[:, BLOCK:BLOCK + P] = (i[:, None] // HD == i[None, :] // HD) / HD
    c[:, ONES:ONES + P] = 1.0
    c[:, CAUSAL:CAUSAL + P] = np.where(i[None, :] > i[:, None], NEG, 0.0)
    n = np.arange(CMP_PAD)
    for t in range(NT):
        seen = (n[None, :] * CMP_STRIDE + CMP_LEN - 1 <= (t * P + i)[:, None]) & (n[None, :] < N_CMP)
        c[:, CMPMASK + t * CMP_PAD:CMPMASK + (t + 1) * CMP_PAD] = np.where(seen, 0.0, NEG)
    return c


def kernel(**inputs):
    import concourse.bacc as bacc
    from concourse.bass_utils import run_bass_kernel_spmd

    nc = bacc.Bacc("TRN2", target_bir_lowering=False, num_devices=1)
    arrays, args = {}, []
    for name, a in pack(**{k: np.asarray(v) for k, v in inputs.items()}).items():
        a = np.ascontiguousarray(a)
        arrays[f"in_{name}"] = a
        args.append(nc.dram_tensor(f"in_{name}", a.shape, mybir.dt.from_np(a.dtype), kind="ExternalInput").ap())
    y = nc.dram_tensor("out_y", (SEQ, D), F32, kind="ExternalOutput").ap()
    program(nc, *args, y)
    r = run_bass_kernel_spmd(nc, [arrays], core_ids=[0])
    return r.results[0]["out_y"].reshape(1, SEQ, D)
```

```python
from contextlib import ExitStack

import numpy as np

import concourse.bass as bass
from concourse import mybir

F32 = mybir.dt.float32
F32R = mybir.dt.float32r
BF16 = mybir.dt.bfloat16
ACT = mybir.ActivationFunctionType
ALU = mybir.AluOpType
AX = mybir.AxisListType

P = 128
SEQ, D = 512, 1024
HD = 64
KT = D // P
NT = SEQ // P
LRU_T = 512 // P
HEADS = 8
KVH = 2
GROUP = HEADS // KVH
CMP_LEN, CMP_STRIDE = 32, 16
N_CMP = (SEQ - CMP_LEN) // CMP_STRIDE + 1
CMP_PAD = 32
CONV = 4
D_MIX = 1536
ET = D_MIX // P
EPS = 1e-6
NEG = -1e30

CHUNKS = ([("u", j) for j in range(4)] + [("fg", 0), ("kc", 0), ("vc", 0), ("ks", 0), ("kw", 0)]
          + [("nq", j) for j in range(4)] + [("vn", 0), ("vn", 1)] + [("zl", j) for j in range(4)]
          + [("fq", j) for j in range(4)] + [("fk", 0), ("vf", 0), ("vf", 1)] + [("fk", j) for j in range(1, 4)]
          + [("vf", 2), ("vf", 3)] + [("zn", j) for j in range(4)] + [("zf", j) for j in range(4)])
N_IN = len(CHUNKS)
N_STREAM = N_IN + ET
AT = {x: c for c, x in enumerate(CHUNKS)}
NORMED = [c for c, (kind, _) in enumerate(CHUNKS) if kind in ("ks", "kw", "nq", "fq", "fk")]
TOKEN_MAJOR = ("vn", "vf")
NSA_END = AT["zl", 3] + 1
FOX_END = AT["zn", 3] + 1
RAW, HL = 2, 4
AHEAD = 3
T_LAG, V_LAG = 3, 5
S_RING, P_RING, PT_RING, M_RING = 4, 4, 3, 8

COLS = {"u": 0, "zl": 512, "nq": 1024, "kc": 1536, "vc": 1664, "ks": 1792, "vs": 1920, "kw": 2048, "vw": 2176,
        "gl": 2304, "zn": 2328, "fq": 2840, "fk": 3352, "vf": 3864, "fl": 4376, "zf": 4384}

CH = {}
_at = 0
for _n, _w in (("norm_g", KT), ("conv_w", CONV * LRU_T), ("conv_b", LRU_T), ("ba", LRU_T), ("bx", LRU_T),
               ("lam", LRU_T), ("nq_g", 1), ("kcmp_g", 1), ("ks_g", 1), ("kw_g", 1), ("fq_g", 1), ("fk_g", 1),
               ("fg_b", 1), ("pe_k", CMP_LEN // 2), ("pe_v", CMP_LEN // 2)):
    CH[_n] = _at
    _at += _w
CH_W = _at

IDENT, BLOCK, CAUSAL, CMPMASK, CONST_W = 0, P, 2 * P, 3 * P, 3 * P + NT * CMP_PAD

FIRST_Z = AT["zn", 0]
TAIL_AT = (AT["ks", 0], AT["kw", 0], AT["nq", 1], AT["nq", 2])

OUT_ORDER = (2, 0, 3, 1)

GAIN = {"ks": "ks_g", "kw": "kw_g", "nq": "nq_g", "fq": "fq_g", "fk": "fk_g"}


def program(nc, xT, x_tok, w_in, w_out, chan, const, lru_w, cmp_w, out):
    ctx = ExitStack()
    with ctx:
        def sem(name):
            return ctx.enter_context(nc.semaphore(name))

        def sb(name, shape, dt=F32, where=ctx):
            return where.enter_context(nc.sbuf_tensor(name, shape, dt))

        raw = sb("raw", [P, RAW, D])
        wh = sb("wh", [P, HL, D], F32R)
        wl = sb("wl", [P, HL, D], F32R)
        cst = sb("cst", [P, CONST_W])
        chn = sb("chn", [P, CH_W])
        ident, block_mean = (cst[:, o:o + P] for o in (IDENT, BLOCK))
        ones = sb("ones", [P, P])
        ident_b = sb("ident_b", [P, P], BF16)
        mask_b = sb("mask_b", [P, P], BF16)
        head_sel = sb("head_sel", [96, HEADS, P], BF16)
        c_parts = sb("c_parts", [96, SEQ], BF16)
        rstd_bc = sb("rstd_bc", [P, SEQ])
        rstd_col = sb("rstd_col", [P, NT])
        y_lru = sb("y_lru", [P, LRU_T, SEQ])
        gates = sb("gates", [P, NT, 3 * HEADS])
        qr = sb("qr", [P, 2, SEQ])
        sq = sb("sq", [P, SEQ])
        std = sb("std", [P, SEQ])
        work = sb("work", [P, SEQ])
        h_stage = sb("h_stage", [P, SEQ], F32R)
        l_stage = sb("l_stage", [P, SEQ], F32R)
        eps1 = sb("eps1", [P, 1])
        eps64 = sb("eps64", [P, 1])
        one1 = sb("one1", [P, 1])
        half_eps = sb("half_eps", [P, 2])
        csp = sb("csp", [P, 2, LRU_T])
        negmax = sb("negmax", [P, M_RING])
        rsum = sb("rsum", [P, 3, NT])
        rcp = sb("rcp", [P, 2, NT])
        k_cmp = sb("k_cmp", [HD, KVH, CMP_PAD])
        k_cmp_sq = sb("k_cmp_sq", [HD, KVH, CMP_PAD])
        k_cmp_y = sb("k_cmp_y", [HD, KVH, CMP_PAD])
        k_cmp_w = sb("k_cmp_w", [HD, KVH, CMP_PAD])
        v_nsa = sb("v_nsa", [P, NT, 2 * KVH * HD])
        o_nsa = sb("o_nsa", [P, NT, HEADS * HD])
        k_cmp_h = sb("k_cmp_h", [P, KVH, CMP_PAD], F32R)
        k_cmp_l = sb("k_cmp_l", [P, KVH, CMP_PAD], F32R)
        v_cmp = sb("v_cmp", [HD, KVH, CMP_PAD])
        v_blocks = sb("v_blocks", [P, KVH, GROUP * HD])
        cmp_stat = sb("cmp_stat", [P, 3, HEADS])

        with ExitStack() as v:
            xh = sb("xh", [P, KT, SEQ], F32R, v)
            xl = sb("xl", [P, KT, SEQ], F32R, v)
            with ExitStack() as m:
                q_nsa = sb("q_nsa", [P, HEADS, SEQ], F32R, m)
                kh_nsa = sb("kh_nsa", [P, 2 * KVH, SEQ], F32R, m)
                kl_nsa = sb("kl_nsa", [P, 2 * KVH, SEQ], F32R, m)
                cmp_w_sb = sb("cmp_w_sb", [P, 2, CMP_LEN // 2, HD], F32, m)
                kv_cm = sb("kv_cm", [P, 2, SEQ], F32, m)
                kv_pair = sb("kv_pair", [P, KVH, SEQ], F32, m)
                kv_pe = sb("kv_pe", [P, 2, KVH, SEQ // 16, 8], F32, m)
                with ExitStack() as w:
                    x_raw = sb("x_raw", [P, KT, SEQ], F32, w)
                with ExitStack() as w:
                    u_pad = sb("u_pad", [P, LRU_T, SEQ + CONV - 1], F32, w)
                    xc = sb("xc", [P, LRU_T, SEQ], F32, w)
                    tau = sb("tau", [P, LRU_T, SEQ], F32, w)
                    ig = sb("ig", [P, LRU_T, SEQ], F32, w)
                    lru_w_sb = sb("lru_w_sb", [P, 2, LRU_T, P], F32, w)
                with ExitStack() as w:
                    v_fox = sb("v_fox", [P, NT, HEADS * HD], F32, w)
                    o_fox = sb("o_fox", [P, NT, HEADS * HD], F32, w)
                    head_out = sb("head_out", [P, NT * HD], F32, w)
                    probs = sb("probs", [P, P_RING, SEQ], F32, w)
                    pT = sb("pT", [P, PT_RING, SEQ], F32, w)
            with ExitStack() as m:
                q_fox = sb("q_fox", [P, HEADS, SEQ], F32R, m)
                kh_fox = sb("kh_fox", [P, HEADS, SEQ], F32R, m)
                kl_fox = sb("kl_fox", [P, HEADS, SEQ], F32R, m)
            with ExitStack() as m:
                yh = sb("yh", [P, ET, SEQ], F32R, m)
                yl = sb("yl", [P, ET, SEQ], F32R, m)
        with ExitStack() as v:
            x_res = sb("x_res", [P, NT, D], F32, v)
            y_out = sb("y_out", [P, NT, D], F32, v)

        bank = [ctx.enter_context(nc.psum_tensor(f"bank{i}", [P, SEQ], F32)) for i in range(8)]
        PROJ = (bank[6], bank[0], bank[1])
        AUX_A, AUX_B, MEAN = bank[2], bank[3], bank[4]
        NORM_W = bank[5]
        SCORE = (bank[4], bank[5], bank[6], bank[0])
        PT = (bank[7], bank[1])
        PTB = len(PT)
        OUT = (bank[2], bank[3])

        x_loaded = [sem(f"x_loaded{k}") for k in range(KT)]
        const_loaded, chan_loaded = sem("const_loaded"), sem("chan_loaded")
        lru_w_loaded, cmp_w_loaded = sem("lru_w_loaded"), sem("cmp_w_loaded")
        raw_loaded = [sem(f"raw_loaded{i}") for i in range(RAW)]
        wh_ready, wl_ready, w_used = sem("wh_ready"), sem("wl_ready"), sem("w_used")
        xh_ready, xl_ready, x_sq = sem("xh_ready"), sem("xl_ready"), sem("x_sq")
        x_sq_used = sem("x_sq_used")
        std_ready = sem("std_ready")
        rstd_ready, rstd_T, rcol_ready = sem("rstd_ready"), sem("rstd_T"), sem("rcol_ready")
        small_consts = sem("small_consts")
        proj_done, proj_read = sem("proj_done"), sem("proj_read")
        conv_first, conv_done = sem("conv_first"), sem("conv_done")
        lru_gates, lru_sig, lru_tau = sem("lru_gates"), sem("lru_sig"), sem("lru_tau")
        lam_act, csp_ready = sem("lam_act"), sem("csp_ready")
        zl_sig, zl_done, sel_ready = sem("zl_sig"), sem("zl_done"), sem("sel_ready")
        ones_ready = sem("ones_ready")
        lru_sqrt, lru_seed = sem("lru_sqrt"), sem("lru_seed")
        lru_ix, lru_ixs, lru_h = sem("lru_ix"), sem("lru_ixs"), sem("lru_h")
        fg_act, gates_T, gates_ready, c_ready = sem("fg_act"), sem("gates_T"), sem("gates_ready"), sem("c_ready")
        kv_shifted = [sem("kv_shifted_k"), sem("kv_shifted_v")]
        kv_pe_ready, cmp_prod = sem("kv_pe_ready"), sem("cmp_prod")
        cmp_evac, cmp_sq, cmp_mean, cmp_std = sem("cmp_evac"), sem("cmp_sq"), sem("cmp_mean"), sem("cmp_std")
        k_cmp_n, k_cmp_hr, k_cmp_ready = sem("k_cmp_n"), sem("k_cmp_hr"), sem("k_cmp_ready")
        v_cmp_T, v_cmp_ready = sem("v_cmp_T"), sem("v_cmp_ready")
        sq_ready, norm_mean, norm_seed = sem("sq_ready"), sem("norm_mean"), sem("norm_seed")
        normed, h_ready, l_ready, stacked = sem("normed"), sem("h_ready"), sem("l_ready"), sem("stacked")
        cmp_s, cmp_shift, cmp_exp, cmp_p = sem("cmp_s"), sem("cmp_shift"), sem("cmp_exp"), sem("cmp_p")
        cmp_pT, cmp_pT_sb, cmp_o, cmp_o_read = sem("cmp_pT"), sem("cmp_pT_sb"), sem("cmp_o"), sem("cmp_o_read")
        s_ready, max_ready, p_ready = sem("s_ready"), sem("max_ready"), sem("p_ready")
        pT_ready, pT_dve, pT_act = sem("pT_ready"), sem("pT_dve"), sem("pT_act")
        av_done, head_done = sem("av_done"), sem("head_done")
        oT_ready, z_sig, y_ready = sem("oT_ready"), sem("z_sig"), sem("y_ready")
        yh_ready, yl_ready = sem("yh_ready"), sem("yl_ready")
        out_sum, out_ready, res_loaded, stored = sem("out_sum"), sem("out_ready"), sem("res_loaded"), sem("stored")

        def chain(eng, name):
            s, n = sem(name), [0]

            def link(ins):
                n[0] += 1
                ins.then_inc(s, 1)
                eng().wait_ge(s, n[0])
            return link

        def proj_units(c):
            return sum(1 if k not in TOKEN_MAJOR else NT if j % 2 == 0 else 0 for k, j in CHUNKS[:c])

        def proj_bank(unit):
            first = max(proj_units(c) for c in (0, NSA_END, FOX_END) if proj_units(c) <= unit)
            return PROJ[(unit - first) % len(PROJ)]

        def wait_bank(eng, unit):
            if unit >= len(PROJ):
                eng.wait_ge(proj_read, unit - len(PROJ) + 1)

        def nth_normed(c):
            return NORMED.index(c)

        def stack_copies(c):
            return sum(4 if CHUNKS[x][0] in ("nq", "fq") else 8 for x in NORMED[:c])

        def wait_slot(eng, c):
            k = c - HL
            if k >= N_IN:
                eng.wait_ge(w_used, k - N_IN + 1)
            elif k >= 0:
                eng.wait_ge(proj_done, proj_units(k + 1))

        heads = [("nsa", h, b) for h in range(HEADS) for b in (1, 2)] + [("fox", h, 0) for h in range(HEADS)]
        NSA_UNITS, UNITS = 2 * HEADS * NT, len(heads) * NT

        def scores_of(u):
            group, h, b = heads[u // NT]
            if group == "nsa":
                k = 2 * (b - 1) + h // GROUP
                return q_nsa[:, h, :], kh_nsa[:, k, :], kl_nsa[:, k, :]
            return q_fox[:, h, :], kh_fox[:, h, :], kl_fox[:, h, :]

        def values_of(u):
            group, h, b = heads[u // NT]
            if group == "nsa":
                k = 2 * (b - 1) + h // GROUP
                return v_nsa[:, :, k * HD:(k + 1) * HD]
            return v_fox[:, :, h * HD:(h + 1) * HD]

        def by_token(ap):
            return ap.rearrange("p (t q) -> p t q", t=NT)

        def wait_pT(eng, u):
            if u % NT == NT - 1:
                eng.wait_ge(pT_act, u // NT + 1)
            else:
                eng.wait_ge(pT_dve, 3 * (u // NT) + u % NT + 1)

        def steps(first, last):
            return [(s, (lambda u: u if first <= u < last else None)) for s in range(first, last + V_LAG + 2)]

        block = ctx.enter_context(nc.Block())

        @block.sync
        def _(sp):
            def load_w(c):
                if c >= N_STREAM:
                    return
                if c >= RAW:
                    sp.wait_ge(wl_ready, c - RAW + 1)
                src = w_in[c] if c < N_IN else w_out[c - N_IN]
                sp.dma_start(raw[:, c % RAW, :], src).then_inc(raw_loaded[c % RAW], 16)

            def stack(c):
                kind, j = CHUNKS[c]
                n = nth_normed(c)
                sp.wait_ge(h_ready, n + 1)
                sp.wait_ge(l_ready, n + 1)
                if kind == "fq" and j == 0:
                    sp.wait_ge(s_ready, NSA_UNITS)
                for s in range(2):
                    half = slice(s * HD, (s + 1) * HD)
                    if kind in ("nq", "fq"):
                        dst = (q_nsa if kind == "nq" else q_fox)[:, 2 * j + s, :]
                        copies = [(dst[0:HD], h_stage), (dst[HD:P], l_stage)]
                    else:
                        if kind == "fk":
                            dh, dl = kh_fox[:, 2 * j + s, :], kl_fox[:, 2 * j + s, :]
                        else:
                            k = s + (KVH if kind == "kw" else 0)
                            dh, dl = kh_nsa[:, k, :], kl_nsa[:, k, :]
                        copies = [(dh[0:HD], h_stage), (dh[HD:P], h_stage), (dl[0:HD], l_stage), (dl[HD:P], l_stage)]
                    for dst, src in copies:
                        sp.dma_start(dst.bitcast(F32), src[half, :].bitcast(F32)).then_inc(stacked, 16)

            def pair_up(i):
                sp.wait_ge(proj_read, proj_units(AT["kc" if i == 0 else "vc", 0]) + 1)
                if i == 1:
                    sp.wait_ge(kv_pe_ready, 1)
                for g in range(KVH):
                    half = slice(g * HD, (g + 1) * HD)
                    sp.dma_start(kv_pair[0:HD, g, :], kv_cm[half, i, :]).then_inc(kv_shifted[i], 16)
                    sp.dma_start(kv_pair[HD:P, g, 0:SEQ - 1], kv_cm[half, i, 1:SEQ]).then_inc(kv_shifted[i], 16)

            sp.dma_start(chn[:, :], chan).then_inc(chan_loaded, 16)
            for k in range(KT):
                sp.dma_start(x_raw[:, k, :], xT[:, k, :]).then_inc(x_loaded[k], 16)
            load_w(0)
            load_w(1)
            sp.dma_start(cst[:, :], const).then_inc(const_loaded, 16)
            sp.dma_start(cmp_w_sb[:, :, :, :], cmp_w).then_inc(cmp_w_loaded, 16)
            load_w(2)
            sp.wait_ge(xl_ready, KT)
            sp.wait_ge(x_sq, KT)
            sp.dma_start(lru_w_sb[:, :, :, :], lru_w).then_inc(lru_w_loaded, 16)
            for c in range(3, N_STREAM + 6):
                load_w(c)
                k = c - 5
                if 0 <= k < N_IN:
                    if CHUNKS[k][0] in ("kc", "vc"):
                        pair_up(0 if CHUNKS[k][0] == "kc" else 1)
                    elif k in NORMED:
                        stack(k)
                if c == N_IN + 4:
                    sp.wait_ge(proj_done, proj_units(N_IN))
                    sp.dma_start(x_res[:, :, :], x_tok).then_inc(res_loaded, 16)
            for n, t in enumerate(OUT_ORDER):
                sp.wait_ge(out_ready, 2 * (n + 1))
                sp.dma_start(out[t * P:(t + 1) * P, :], y_out[:, t, :]).then_inc(stored, 16)
            sp.wait_ge(stored, 16 * NT)

        @block.gpsimd
        def _(pool):
            nc.gpsimd.memset(ones[:, :], 1.0).then_inc(ones_ready, 1)
            nc.gpsimd.memset(eps1[:, :], EPS)
            nc.gpsimd.memset(half_eps[:, 0:1], -0.5 * EPS)
            nc.gpsimd.memset(half_eps[:, 1:2], -32 * EPS)
            nc.gpsimd.memset(eps64[:, :], 64 * EPS)
            nc.gpsimd.memset(one1[:, :], 1.0)
            nc.gpsimd.memset(c_parts[:, :], 0.0)
            nc.gpsimd.memset(k_cmp[:, :, :], 0.0)
            nc.gpsimd.memset(v_cmp[:, :, :], 0.0)
            nc.gpsimd.memset(v_blocks[:, :, :], 0.0).then_inc(small_consts, 1)
            for c in range(N_STREAM):
                pool.wait_ge(wh_ready, c + 1)
                nc.gpsimd.tensor_tensor(wl[:, c % HL, :], raw[:, c % RAW, :], wh[:, c % HL, :].bitcast(F32),
                                        ALU.subtract).then_inc(wl_ready, 1)
                j = c - AHEAD - 1
                if 0 <= j < LRU_T:
                    pool.wait_ge(lru_sig, 2 * j + 2)
                    nc.gpsimd.tensor_tensor(ig[:, j, :], ig[:, j, :], xc[:, j, :], ALU.mult).then_inc(lru_ix, 1)
                j = c - AHEAD - 1 - LRU_T
                if 0 <= j < LRU_T:
                    pool.wait_ge(lru_sqrt, j + 1)
                    pool.wait_ge(lru_ix, j + 1)
                    nc.gpsimd.tensor_tensor(ig[:, j, :], ig[:, j, :], u_pad[:, j, 0:SEQ],
                                            ALU.mult).then_inc(lru_ixs, 1)

        @block.scalar
        def _(act):
            link = chain(lambda: act, "act_chain")

            def split(c):
                if c >= N_STREAM:
                    return
                act.wait_ge(raw_loaded[c % RAW], 16 * (c // RAW + 1))
                wait_slot(act, c)
                act.activation(wh[:, c % HL, :], raw[:, c % RAW, :], ACT.Copy).then_inc(wh_ready, 1)

            def ch(name, j=0):
                return chn[:, CH[name] + j:CH[name] + j + 1]

            def rsqrt_seed(x, scale, y, y2, w, rows=P):
                big = scale != 1.0
                link(act.activation(y, x, ACT.Ln, bias=(eps64 if big else eps1)[0:rows, :], scale=scale))
                link(act.activation(y, y, ACT.Exp, scale=-0.5))
                act.activation(y2, y, ACT.Square)
                return act.activation(w, x, ACT.Identity, bias=half_eps[0:rows, int(big):int(big) + 1],
                                      scale=-0.5 * scale)

            def before(c):
                kind, j = CHUNKS[c]
                if kind == "u":
                    act.wait_ge(proj_read, proj_units(c) + 1)
                    act.activation(xc[:, j, :], u_pad[:, j, 0:SEQ], ACT.Identity, bias=ch("conv_b", j),
                                   scale=ch("conv_w", j)).then_inc(conv_first, 1)
                if kind == "zl":
                    act.wait_ge(proj_read, proj_units(c) + 1)
                    if j >= 1:
                        act.wait_ge(zl_done, j)
                    act.activation(sq[:, :], y_lru[:, j, :], ACT.Sigmoid).then_inc(zl_sig, 1)
                if c in NORMED:
                    act.wait_ge(proj_read, proj_units(c) + 1)
                    n = nth_normed(c)
                    if n >= 1:
                        act.wait_ge(norm_mean, n)
                    act.activation(sq[:, :], qr[:, n % 2, :], ACT.Square).then_inc(sq_ready, 1)

            def after(c):
                kind, j = CHUNKS[c]
                if kind == "u":
                    if j == 0:
                        act.wait_ge(csp_ready, 1)
                    act.wait_ge(lru_gates, j + 1)
                    act.activation(tau[:, j, :], AUX_A[:, :], ACT.Sigmoid, bias=ch("ba", j)).then_inc(lru_sig, 1)
                    act.activation(ig[:, j, :], AUX_B[:, :], ACT.Sigmoid, bias=ch("bx", j)).then_inc(lru_sig, 1)
                    act.wait_ge(lru_sig, 2 * j + 2)
                    act.activation(tau[:, j, :], tau[:, j, :], ACT.Tanh,
                                   scale=csp[:, 0, j:j + 1]).then_inc(lru_tau, 1)
                if kind == "fg":
                    act.wait_ge(proj_read, proj_units(c) + 1)
                    b = ch("fg_b")
                    act.activation(std[0:64, :], qr[0:64, 0, :], ACT.Sigmoid, bias=b[0:64]).then_inc(fg_act, 1)
                    link(act.activation(sq[0:HEADS, :], qr[0:HEADS, 0, :], ACT.Abs, bias=b[0:HEADS]))
                if c in NORMED:
                    n = nth_normed(c)
                    act.wait_ge(norm_mean, n + 1)
                    eighth = kind in ("nq", "fq")
                    if n == 0:
                        act.wait_ge(c_ready, 1)
                    if n >= 1:
                        act.wait_ge(normed, n)
                    rsqrt_seed(MEAN[:, :], 64.0 if eighth else 1.0, std[:, :], work[:, :],
                               NORM_W[:, :]).then_inc(norm_seed, 1)
                    act.wait_ge(normed, n + 1)
                    if n >= 1:
                        act.wait_ge(stacked, 16 * stack_copies(n))
                    act.activation(h_stage[:, :], qr[:, n % 2, :], ACT.Copy).then_inc(h_ready, 1)

            def z_gate(c):
                i = c - FIRST_Z
                act.wait_ge(proj_read, proj_units(c) + 1)
                if i >= 1:
                    act.wait_ge(y_ready, i)
                act.activation(sq[:, :], qr[:, i % 2, :], ACT.Sigmoid).then_inc(z_sig, 1)

            def unit_exp(u):
                v, t = divmod(u, NT)
                act.wait_ge(max_ready, u + 1)
                if u >= P_RING:
                    act.wait_ge(pT_ready, u - P_RING + 1)
                if v >= 3:
                    act.wait_ge(head_done, v - 2)
                n = (t + 1) * P
                act.activation(probs[:, u % P_RING, 0:n], SCORE[u % S_RING][:, 0:n], ACT.Exp,
                               bias=negmax[:, u % M_RING:u % M_RING + 1],
                               accum_out=rsum[:, v % 3, t:t + 1]).then_inc(p_ready, 1)

            def attention(first, last):
                for s, inside in steps(first, last):
                    u = inside(s - T_LAG)
                    if u is not None and u % NT == NT - 1:
                        act.wait_ge(pT_ready, u + 1)
                        if u >= PT_RING:
                            act.wait_ge(av_done, u - PT_RING + 1)
                        act.activation(pT[:, u % PT_RING, :], PT[u % PTB][:, :], ACT.Copy).then_inc(pT_act, 1)
                    if inside(s) is not None:
                        unit_exp(s)

            act.preload_act_table_set("natural_log_exp_and_others")
            act.wait_ge(chan_loaded, 16)
            act.wait_ge(small_consts, 1)
            lam = chn[:, CH["lam"]:CH["lam"] + LRU_T]
            link(act.activation(csp[:, 1, :], lam, ACT.Abs))
            link(act.activation(csp[:, 1, :], csp[:, 1, :], ACT.Exp, scale=-1.0))
            act.activation(csp[:, 1, :], csp[:, 1, :], ACT.Ln, bias=one1[:, :]).then_inc(lam_act, 1)
            for k in range(KT):
                act.wait_ge(x_loaded[k], 16)
                act.activation(xh[:, k, :], x_raw[:, k, :], ACT.Copy, scale=ch("norm_g", k)).then_inc(xh_ready, 1)
            split(0)
            split(1)
            act.wait_ge(x_sq_used, KT)
            act.activation(rstd_bc[:, :], MEAN[:, :], ACT.Sqrt, bias=eps1[:, :], scale=1.0 / D).then_inc(std_ready, 1)
            split(2)
            for c in range(NSA_END):
                split(c + AHEAD)
                before(c)
                if c >= 1:
                    after(c - 1)
                if c == AT["kc", 0]:
                    act.wait_ge(lru_tau, LRU_T)
                    act.wait_ge(conv_done, LRU_T)
                    for j in range(LRU_T):
                        act.activation(u_pad[:, j, 0:SEQ], tau[:, j, :], ACT.Sqrt, scale=4.0).then_inc(lru_sqrt, 1)
                    act.preload_act_table_set("natural_log_exp_and_others")
                    link(act.activation(sq[0:HEADS, :], sq[0:HEADS, :], ACT.Exp, scale=-1.0))
                    act.activation(sq[0:HEADS, :], sq[0:HEADS, :], ACT.Ln, bias=one1[0:HEADS, :]).then_inc(fg_act, 1)
                    for j in range(LRU_T):
                        act.wait_ge(lru_ix, j + 1)
                        link(act.activation(xc[:, j, :], tau[:, j, :], ACT.Ln, bias=one1[:, :]))
                        act.activation(xc[:, j, :], xc[:, j, :], ACT.Exp, scale=-1.0).then_inc(lru_seed, 1)
                if c == AT["nq", 0]:
                    act.wait_ge(cmp_evac, 1)
                    act.activation(k_cmp_sq[:, :, :], k_cmp[:, :, :], ACT.Square).then_inc(cmp_sq, 1)
                if c == AT["nq", 2]:
                    act.wait_ge(cmp_mean, 1)
                    rsqrt_seed(AUX_A[0:HD, 0:KVH * CMP_PAD].rearrange("p (g n) -> p g n", g=KVH), 1.0,
                               k_cmp_y[:, :, :], k_cmp_sq[:, :, :], k_cmp_w[:, :, :], HD).then_inc(cmp_std, 1)
                if c == AT["nq", 3]:
                    act.wait_ge(k_cmp_n, 1)
                    for half in (slice(0, HD), slice(HD, P)):
                        act.activation(k_cmp_h[half, :, :], k_cmp[:, :, :], ACT.Copy).then_inc(k_cmp_hr, 1)
                if CHUNKS[c][0] == "zl":
                    t = CHUNKS[c][1]
                    p = qr[:, t % 2, 0:HEADS * CMP_PAD]
                    act.wait_ge(cmp_shift, t + 1)
                    act.activation(p, p, ACT.Exp).then_inc(cmp_exp, 1)
            act.preload_act_table_set("natural_log_exp_and_others")
            attention(0, NSA_UNITS)
            for c in range(NSA_END, FOX_END):
                split(c + AHEAD)
                before(c)
                after(c - 1)
                if CHUNKS[c][0] == "zn":
                    z_gate(c)
            act.preload_act_table_set("natural_log_exp_and_others")
            attention(NSA_UNITS, UNITS)
            act.wait_ge(s_ready, UNITS)
            for e in range(LRU_T):
                act.activation(yh[:, e, :], y_lru[:, e, :], ACT.Copy).then_inc(yh_ready, 1)
            for e in range(4):
                act.activation(by_token(yh[:, LRU_T + e, :]), o_nsa[:, :, e * P:(e + 1) * P],
                               ACT.Copy).then_inc(yh_ready, 1)
            for c in range(FOX_END, N_IN):
                split(c + AHEAD)
                z_gate(c)
                i = c - FIRST_Z
                act.wait_ge(y_ready, i + 1)
                act.activation(yh[:, LRU_T + i, :], qr[:, i % 2, :], ACT.Copy).then_inc(yh_ready, 1)
            for e in range(ET):
                split(N_IN + e + AHEAD)

        @block.vector
        def _(dve):
            link = chain(lambda: dve, "dve_chain")

            def ch(name, j=0):
                return chn[:, CH[name] + j:CH[name] + j + 1]

            def evac(c):
                kind, j = CHUNKS[c]
                if kind in TOKEN_MAJOR:
                    if j % 2:
                        return
                    for t in range(NT):
                        unit = proj_units(c) + t
                        dve.wait_ge(proj_done, unit + 1)
                        if kind == "vn":
                            dst = v_nsa[:, t, :]
                        else:
                            dst = v_fox[:, t, j * P:(j + 2) * P]
                        dve.tensor_scalar(dst, proj_bank(unit)[:, 0:2 * P], rstd_col[:, t:t + 1], None,
                                          ALU.mult).then_inc(proj_read, 1)
                        if t == 1:
                            after(c - 1)
                    return
                unit = proj_units(c)
                dve.wait_ge(proj_done, unit + 1)
                rows = 64 if kind == "fg" else P
                if kind == "u":
                    dst = u_pad[:, j, CONV - 1:]
                elif kind == "zl":
                    dst = y_lru[:, j, :]
                elif kind in ("kc", "vc"):
                    dst = kv_cm[:, 0 if kind == "kc" else 1, :]
                elif kind == "fg":
                    dst = qr[0:64, 0, :]
                elif kind in ("zn", "zf"):
                    i = c - FIRST_Z
                    dst = qr[:, i % 2, :]
                    if i == 0:
                        dve.wait_ge(l_ready, len(NORMED))
                    elif kind == "zn" and i >= 2:
                        dve.wait_ge(y_ready, i - 1)
                    elif kind == "zf":
                        dve.wait_ge(yl_ready, LRU_T + max(i - 1, 4))
                else:
                    n = nth_normed(c)
                    dst = qr[:, n % 2, :]
                    if n >= 2:
                        dve.wait_ge(l_ready, n - 1)
                dve.tensor_tensor(dst, proj_bank(unit)[0:rows, :], rstd_bc[0:rows, :], ALU.mult).then_inc(proj_read, 1)

            def before(c):
                evac(c)
                kind, j = CHUNKS[c]
                if kind == "u":
                    for k in range(1, CONV):
                        if k == 1:
                            dve.wait_ge(conv_first, j + 1)
                        ins = dve.scalar_tensor_tensor(xc[:, j, :], u_pad[:, j, k:k + SEQ],
                                                       ch("conv_w", k * LRU_T + j), xc[:, j, :], ALU.mult, ALU.add)
                        if k < CONV - 1:
                            link(ins)
                        else:
                            ins.then_inc(conv_done, 1)

            def lru_output(j):
                dve.wait_ge(zl_sig, j + 1)
                dve.tensor_tensor(y_lru[:, j, :], y_lru[:, j, :], sq[:, :], ALU.mult).then_inc(zl_done, 1)
                dve.wait_ge(zl_done, j + 1)
                dve.wait_ge(lru_h, j + 1)
                link(dve.tensor_tensor(y_lru[:, j, :], y_lru[:, j, :], u_pad[:, j, 0:SEQ], ALU.mult))

            def after(c):
                kind, j = CHUNKS[c]
                if c in NORMED:
                    n = nth_normed(c)
                    dve.wait_ge(norm_seed, n + 1)
                    link(dve.tensor_tensor(work[:, :], work[:, :], NORM_W[:, :], ALU.mult))
                    link(dve.scalar_tensor_tensor(std[:, :], work[:, :], 1.5, std[:, :], ALU.add, ALU.mult))
                    dve.scalar_tensor_tensor(qr[:, n % 2, :], qr[:, n % 2, :], ch(GAIN[kind]), std[:, :], ALU.mult,
                                             ALU.mult).then_inc(normed, 1)
                    dve.wait_ge(h_ready, n + 1)
                    dve.tensor_tensor(l_stage[:, :], qr[:, n % 2, :], h_stage[:, :].bitcast(F32),
                                      ALU.subtract).then_inc(l_ready, 1)

            def forget_gates():
                f = qr[0:HEADS, 0, :]
                a, b = qr[0:HEADS, 1, :], work[0:HEADS, :]
                mid = a.bitcast(BF16)[:, 0:SEQ]
                dve.wait_ge(fg_act, 2)
                link(dve.tensor_scalar(f, f, ch("fg_b")[0:HEADS], 0.0, ALU.add, ALU.min))
                link(dve.tensor_tensor(f, f, sq[0:HEADS, :], ALU.subtract))
                link(dve.memset(a, 1.0))
                link(dve.tensor_tensor_scan(b, a, f, 0.0, ALU.mult, ALU.subtract))
                dve.wait_ge(small_consts, 1)
                link(dve.tensor_copy(c_parts[0:HEADS, :], b))
                link(dve.tensor_tensor(b, b, c_parts[0:HEADS, :], ALU.subtract))
                link(dve.tensor_copy(mid, b))
                link(dve.tensor_tensor(b, b, mid, ALU.subtract))
                dve.tensor_copy(c_parts[32:32 + HEADS, :], mid)
                dve.tensor_copy(c_parts[64:64 + HEADS, :], b).then_inc(c_ready, 1)

            def branch_gates():
                dve.wait_ge(gates_T, 1)
                dve.tensor_copy(gates[:, :, :], AUX_A[:, 0:NT * 64].rearrange("p (t c) -> p t c", t=NT)
                                [:, :, 32:32 + 3 * HEADS]).then_inc(gates_ready, 1)

            def lru_tail(j):
                t, h, g, d = tau[:, j, :], u_pad[:, j, 0:SEQ], ig[:, j, :], xc[:, j, :]
                dve.wait_ge(lru_seed, j + 1)
                dve.wait_ge(lru_ixs, j + 1)
                link(dve.scalar_tensor_tensor(h, t, 1.0, d, ALU.add, ALU.mult))
                link(dve.scalar_tensor_tensor(d, h, 2.0, d, ALU.subtract, ALU.mult))
                link(dve.scalar_tensor_tensor(t, t, 1.0, d, ALU.subtract, ALU.mult))
                link(dve.scalar_tensor_tensor(g, g, -1.0, d, ALU.mult, ALU.mult))
                dve.tensor_tensor_scan(h, t, g, 0.0, ALU.mult, ALU.add).then_inc(lru_h, 1)

            def pair_pe(i):
                dve.wait_ge(kv_shifted[i], 64)
                if i == 1:
                    dve.wait_ge(cmp_prod, 1)
                pairs = kv_pair[:, :, :].rearrange("p g (n j two) -> p g n j two", j=8, two=2)
                for part in range(2):
                    o = CH["pe_k" if i == 0 else "pe_v"] + 8 * part
                    for g in range(KVH):
                        pe_row = chn[:, o:o + 8].unsqueeze(1).broadcast_to([P, SEQ // 16, 8])
                        ins = dve.tensor_tensor(kv_pe[:, part, g, :, :], pairs[:, g, :, :, 0], pe_row, ALU.add)
                ins.then_inc(kv_pe_ready, 1)

            def cmp_out(i):
                dve.wait_ge(cmp_prod, i + 1)
                dve.wait_ge(small_consts, 1)
                src = (AUX_A if i == 0 else AUX_B)[0:HD, 0:KVH * CMP_PAD].rearrange("p (g n) -> p g n", g=KVH)
                dve.tensor_copy((k_cmp if i == 0 else v_cmp)[:, :, 0:N_CMP], src[:, :, 0:N_CMP]).then_inc(cmp_evac, 1)

            def cmp_norm():
                dve.wait_ge(cmp_std, 1)
                kc, ks, ky, kw = (x[:, :, :].rearrange("p g n -> p (g n)") for x in (k_cmp, k_cmp_sq, k_cmp_y, k_cmp_w))
                link(dve.tensor_tensor(ks, ks, kw, ALU.mult))
                link(dve.scalar_tensor_tensor(ky, ks, 1.5, ky, ALU.add, ALU.mult))
                dve.scalar_tensor_tensor(kc, kc, ch("kcmp_g")[0:HD], ky, ALU.mult, ALU.mult).then_inc(k_cmp_n, 1)
                dve.wait_ge(k_cmp_hr, 2)
                for half in (slice(0, HD), slice(HD, P)):
                    dve.tensor_tensor(k_cmp_l[half, :, :], k_cmp[:, :, :], k_cmp_h[0:HD, :, :].bitcast(F32),
                                      ALU.subtract).then_inc(k_cmp_ready, 1)

            def cmp_values():
                dve.wait_ge(v_cmp_T, 1)
                for g in range(KVH):
                    for r in range(GROUP):
                        dve.tensor_copy(v_blocks[32 * r:32 * r + 32, g, r * HD:(r + 1) * HD],
                                        AUX_B[0:CMP_PAD, g * HD:(g + 1) * HD]).then_inc(v_cmp_ready, 1)

            def cmp_probs(t):
                s3 = SCORE[t % 2][:, 0:HEADS * CMP_PAD].rearrange("p (h n) -> p h n", h=HEADS)
                p3 = qr[:, t % 2, 0:HEADS * CMP_PAD].rearrange("p (h n) -> p h n", h=HEADS)
                mask = cst[:, CMPMASK + t * CMP_PAD:CMPMASK + (t + 1) * CMP_PAD]
                mx, sm, rc = (cmp_stat[:, i, :] for i in range(3))
                dve.wait_ge(cmp_s, t + 1)
                if t == 0:
                    dve.wait_ge(l_ready, 6)
                if t >= 2:
                    dve.wait_ge(cmp_pT, t - 1)
                link(dve.tensor_tensor(p3, s3, mask.unsqueeze(1).broadcast_to([P, HEADS, CMP_PAD]), ALU.add))
                link(dve.tensor_reduce(mx, p3, AX.X, ALU.max))
                link(dve.tensor_scalar(mx, mx, NEG / 10, None, ALU.max))
                dve.tensor_tensor(p3, p3, mx.unsqueeze(2).broadcast_to([P, HEADS, CMP_PAD]),
                                  ALU.subtract).then_inc(cmp_shift, 1)
                if t >= 1:
                    cmp_out_read(t - 1)
                lru_output(t)
                dve.wait_ge(cmp_exp, t + 1)
                link(dve.tensor_reduce(sm, p3, AX.X, ALU.add))
                link(dve.tensor_scalar(sm, sm, 1e-30, None, ALU.max))
                link(dve.reciprocal(rc, sm))
                link(dve.tensor_tensor(rc, rc, gates[:, t, 0:3 * HEADS:3], ALU.mult))
                dve.tensor_tensor(p3, p3, rc.unsqueeze(2).broadcast_to([P, HEADS, CMP_PAD]),
                                  ALU.mult).then_inc(cmp_p, 1)

            def cmp_transposed(t):
                dve.wait_ge(cmp_pT, t + 1)
                if t == 0:
                    dve.wait_ge(normed, 6)
                if t >= 1:
                    dve.wait_ge(cmp_o, t)
                dve.tensor_copy(std[:, 0:2 * P], PT[0][:, 0:2 * P]).then_inc(cmp_pT_sb, 1)

            def cmp_out_read(t):
                dve.wait_ge(cmp_o, t + 1)
                dve.tensor_copy(o_nsa[:, t, :], OUT[t % 2][:, :]).then_inc(cmp_o_read, 1)

            def z_times_o(c):
                i = c - FIRST_Z
                z = qr[:, i % 2, :]
                dve.wait_ge(oT_ready, i + 1)
                dve.wait_ge(z_sig, i + 1)
                link(dve.tensor_tensor(z, z, sq[:, :], ALU.mult))
                o = by_token(OUT[i % 2][:, :])
                if i < 4:
                    dst = o_nsa[:, :, i * P:(i + 1) * P]
                else:
                    dst = by_token(z)
                dve.tensor_tensor(dst, by_token(z), o, ALU.mult).then_inc(y_ready, 1)

            def finish_head(v):
                group, h, b = heads[v]
                dve.wait_ge(av_done, NT * (v + 1))
                if v >= 1:
                    dve.wait_ge(head_done, v)
                link(dve.reciprocal(rcp[:, 0, :], rsum[:, v % 3, :]))
                o = OUT[v % 2][:, 0:NT * HD].rearrange("p (t d) -> p t d", t=NT)
                if group == "nsa":
                    if v == 0:
                        dve.wait_ge(cmp_o_read, NT)
                    link(dve.tensor_tensor(rcp[:, 0, :], rcp[:, 0, :], gates[:, :, 3 * h + b], ALU.mult))
                    scaled = head_out[:, :].rearrange("p (t d) -> p t d", t=NT)
                    link(dve.tensor_tensor(scaled, o, rcp[:, 0, :].unsqueeze(2).broadcast_to([P, NT, HD]), ALU.mult))
                    acc = o_nsa[:, :, h * HD:(h + 1) * HD]
                    dve.tensor_tensor(acc, acc, scaled, ALU.add).then_inc(head_done, 1)
                else:
                    dve.tensor_tensor(o_fox[:, :, h * HD:(h + 1) * HD], o,
                                      rcp[:, 0, :].unsqueeze(2).broadcast_to([P, NT, HD]),
                                      ALU.mult).then_inc(head_done, 1)

            def attention(first, last):
                for s, inside in steps(first, last):
                    if s == 2:
                        cmp_transposed(NT - 1)
                    if s == 4:
                        cmp_out_read(NT - 1)
                    if inside(s) is not None:
                        n = (s % NT + 1) * P
                        dve.wait_ge(s_ready, s + 1)
                        if s >= M_RING:
                            dve.wait_ge(p_ready, s - M_RING + 1)
                        dve.tensor_reduce(negmax[:, s % M_RING:s % M_RING + 1], SCORE[s % S_RING][:, 0:n], AX.X,
                                          ALU.max, negate=True).then_inc(max_ready, 1)
                    u = inside(s - T_LAG)
                    if u is not None and u % NT < NT - 1:
                        n = (u % NT + 1) * P
                        dve.wait_ge(pT_ready, u + 1)
                        if u >= PT_RING:
                            dve.wait_ge(av_done, u - PT_RING + 1)
                        dve.tensor_copy(pT[:, u % PT_RING, 0:n], PT[u % PTB][:, 0:n]).then_inc(pT_dve, 1)
                    u = inside(s - V_LAG - 1)
                    if u is not None and u % NT == NT - 1:
                        finish_head(u // NT)

            dve.wait_ge(chan_loaded, 16)
            for k in range(KT):
                dve.wait_ge(x_loaded[k], 16)
                if k >= 2:
                    dve.wait_ge(x_sq_used, k - 1)
                dve.tensor_tensor(qr[:, k % 2, :], x_raw[:, k, :], x_raw[:, k, :], ALU.mult).then_inc(x_sq, 1)
                dve.wait_ge(xh_ready, k + 1)
                dve.scalar_tensor_tensor(xl[:, k, :], x_raw[:, k, :], ch("norm_g", k), xh[:, k, :].bitcast(F32),
                                         ALU.mult, ALU.subtract).then_inc(xl_ready, 1)
            dve.wait_ge(const_loaded, 16)
            dve.tensor_copy(ident_b[:, :], ident)
            dve.tensor_copy(mask_b[:, :], cst[:, CAUSAL:CAUSAL + P])
            sel = work[0:96, 0:HEADS]
            link(dve.tensor_tensor(sel, cst[0:96, IDENT:IDENT + HEADS], cst[0:96, IDENT + 32:IDENT + 32 + HEADS],
                                   ALU.add))
            link(dve.tensor_tensor(sel, sel, cst[0:96, IDENT + 64:IDENT + 64 + HEADS], ALU.add))
            dve.tensor_copy(head_sel[:, :, :], sel.unsqueeze(2).broadcast_to([96, HEADS, P])).then_inc(sel_ready, 1)
            dve.wait_ge(lam_act, 1)
            lam = chn[:, CH["lam"]:CH["lam"] + LRU_T]
            link(dve.tensor_scalar(csp[:, 0, :], lam, -1.0, 0.0, ALU.mult, ALU.max))
            link(dve.tensor_tensor(csp[:, 0, :], csp[:, 0, :], csp[:, 1, :], ALU.add))
            dve.tensor_scalar(csp[:, 0, :], csp[:, 0, :], 4.0, None, ALU.mult).then_inc(csp_ready, 1)
            dve.wait_ge(x_sq_used, KT)
            dve.memset(u_pad[:, :, 0:CONV - 1], 0.0)
            dve.wait_ge(std_ready, 1)
            dve.reciprocal(rstd_bc[:, :], rstd_bc[:, :]).then_inc(rstd_ready, 1)
            dve.wait_ge(rstd_ready, 1)
            for c in range(NSA_END):
                before(c)
                if c == AT["kc", 0]:
                    dve.wait_ge(rstd_T, 1)
                    dve.tensor_copy(rstd_col[:, :], AUX_B[:, :].rearrange("p (t c) -> p t c", t=NT)[:, :, 0])\
                       .then_inc(rcol_ready, 1)
                if c == AT["vc", 0]:
                    branch_gates()
                    forget_gates()
                if c == AT["ks", 0]:
                    pair_pe(0)
                if c in TAIL_AT:
                    lru_tail(TAIL_AT.index(c))
                if c == AT["nq", 0]:
                    cmp_out(0)
                    pair_pe(1)
                if c == AT["nq", 2]:
                    cmp_out(1)
                if c == AT["vn", 0]:
                    cmp_values()
                if c >= 1 and CHUNKS[c][0] not in TOKEN_MAJOR:
                    after(c - 1)
                if c == AT["nq", 3]:
                    cmp_norm()
                if CHUNKS[c][0] == "zl":
                    t = CHUNKS[c][1]
                    if t >= 1:
                        cmp_transposed(t - 1)
                    cmp_probs(t)
            attention(0, NSA_UNITS)
            for c in range(NSA_END, FOX_END):
                before(c)
                if CHUNKS[c][0] not in TOKEN_MAJOR:
                    after(c - 1)
                if CHUNKS[c][0] == "zn":
                    z_times_o(c)
            attention(NSA_UNITS, UNITS)
            dve.wait_ge(s_ready, UNITS)
            for e in range(LRU_T + 4):
                dve.wait_ge(yh_ready, e + 1)
                if e < LRU_T:
                    dve.tensor_tensor(yl[:, e, :], y_lru[:, e, :], yh[:, e, :].bitcast(F32),
                                      ALU.subtract).then_inc(yl_ready, 1)
                else:
                    i = e - LRU_T
                    dve.tensor_tensor(by_token(yl[:, e, :]), o_nsa[:, :, i * P:(i + 1) * P],
                                      by_token(yh[:, e, :].bitcast(F32)), ALU.subtract).then_inc(yl_ready, 1)
            for c in range(FOX_END, N_IN):
                i = c - FIRST_Z
                evac(c)
                z_times_o(c)
                dve.wait_ge(yh_ready, LRU_T + i + 1)
                dve.tensor_tensor(yl[:, LRU_T + i, :], qr[:, i % 2, :], yh[:, LRU_T + i, :].bitcast(F32),
                                  ALU.subtract).then_inc(yl_ready, 1)
            dve.wait_ge(res_loaded, 16)
            for n, t in enumerate(OUT_ORDER):
                for half in range(2):
                    dve.wait_ge(out_sum, 2 * n + half + 1)
                    cols = slice(half * 512, (half + 1) * 512)
                    dve.tensor_tensor(y_out[:, t, cols], bank[2 * t + half][:, :], x_res[:, t, cols],
                                      ALU.add).then_inc(out_ready, 1)

        @block.tensor
        def _(pe):
            def project(c):
                kind, j = CHUNKS[c]
                slot = c % HL
                if kind in TOKEN_MAJOR:
                    if j % 2:
                        return
                    pe.wait_ge(wl_ready, c + 2)
                    hi = wh[:, slot:slot + 2, :].rearrange("p s (k c) -> p k s c", k=KT)
                    lo = wl[:, slot:slot + 2, :].rearrange("p s (k c) -> p k s c", k=KT)
                    for t in range(NT):
                        unit = proj_units(c) + t
                        wait_bank(pe, unit)
                        dst = proj_bank(unit)[:, 0:2 * P].rearrange("p (s c) -> p s c", s=2)
                        toks = slice(t * P, (t + 1) * P)
                        for k in range(KT):
                            pe.matmul(dst, xh[:, k, toks], hi[:, k], start=(k == 0), stop=False)
                            pe.matmul(dst, xh[:, k, toks], lo[:, k], start=False, stop=False)
                            mm = pe.matmul(dst, xl[:, k, toks], hi[:, k], start=False, stop=(k == KT - 1))
                        mm.then_inc(proj_done, 1)
                        if t == 0:
                            head_mean(c - 1)
                    return
                unit = proj_units(c)
                wait_bank(pe, unit)
                pe.wait_ge(wl_ready, c + 1)
                m = 64 if kind == "fg" else P
                dst = proj_bank(unit)[0:m, :]
                for k in range(KT):
                    if c == 0:
                        pe.wait_ge(xl_ready, k + 1)
                    hi, lo = wh[:, slot, k * P:k * P + m], wl[:, slot, k * P:k * P + m]
                    pe.matmul(dst, hi, xh[:, k, :], start=(k == 0), stop=False)
                    pe.matmul(dst, hi, xl[:, k, :], start=False, stop=False)
                    mm = pe.matmul(dst, lo, xh[:, k, :], start=False, stop=(k == KT - 1))
                mm.then_inc(proj_done, 1)

            def head_mean(c):
                n = nth_normed(c)
                pe.wait_ge(sq_ready, n + 1)
                if n >= 1:
                    pe.wait_ge(norm_seed, n)
                pe.matmul(MEAN[:, :], block_mean, sq[:, :], start=True, stop=True).then_inc(norm_mean, 1)

            def gates_of(j):
                pe.wait_ge(conv_done, j + 1)
                if j >= 1:
                    pe.wait_ge(lru_sig, 2 * j)
                if j == 0:
                    pe.wait_ge(lru_w_loaded, 16)
                pe.matmul(AUX_A[:, :], lru_w_sb[:, 0, j, :], xc[:, j, :], start=True, stop=True)
                pe.matmul(AUX_B[:, :], lru_w_sb[:, 1, j, :], xc[:, j, :], start=True, stop=True)\
                    .then_inc(lru_gates, 1)

            def compress(i):
                pe.wait_ge(kv_pe_ready, i + 1)
                pe.wait_ge(cmp_w_loaded, 16)
                dst = (AUX_A if i == 0 else AUX_B)[0:HD, 0:KVH * CMP_PAD].rearrange("p (g n) -> p g n", g=KVH)
                for j in range(CMP_LEN // 2):
                    part = j // 8
                    mm = pe.matmul(dst[:, :, 0:N_CMP], cmp_w_sb[:, i, j, :],
                                   kv_pe[:, part, :, part:part + N_CMP, j % 8],
                                   start=(j == 0), stop=(j == CMP_LEN // 2 - 1))
                mm.then_inc(cmp_prod, 1)

            def cmp_scores(t):
                if t == 0:
                    pe.wait_ge(k_cmp_ready, 2)
                    pe.wait_ge(v_cmp_ready, KVH * GROUP)
                    pe.wait_ge(stacked, 16 * stack_copies(6))
                    pe.wait_ge(normed, 6)
                if t >= 2:
                    pe.wait_ge(cmp_shift, t - 1)
                for h in range(HEADS):
                    dst = SCORE[t % 2][:, h * CMP_PAD:(h + 1) * CMP_PAD]
                    q = q_nsa[:, h, t * P:(t + 1) * P]
                    pe.matmul(dst, q, k_cmp_h[:, h // GROUP, :], start=True, stop=False)
                    mm = pe.matmul(dst, q, k_cmp_l[:, h // GROUP, :], start=False, stop=True)
                mm.then_inc(cmp_s, 1)

            def cmp_transpose(t):
                pe.wait_ge(cmp_p, t + 1)
                if t >= 1:
                    pe.wait_ge(cmp_pT_sb, t)
                for g in range(KVH):
                    mm = pe.transpose(PT[0][:, g * P:(g + 1) * P], qr[:, t % 2, g * P:(g + 1) * P], ident)
                mm.then_inc(cmp_pT, 1)

            def cmp_values(t):
                pe.wait_ge(cmp_pT_sb, t + 1)
                if t >= 2:
                    pe.wait_ge(cmp_o_read, t - 1)
                for g in range(KVH):
                    mm = pe.matmul(OUT[t % 2][:, g * GROUP * HD:(g + 1) * GROUP * HD], std[:, g * P:(g + 1) * P],
                                   v_blocks[:, g, :], start=True, stop=True)
                mm.then_inc(cmp_o, 1)

            def unit_scores(u):
                v, t = divmod(u, NT)
                n = (t + 1) * P
                q, kh, kl = scores_of(u)
                if u >= S_RING:
                    pe.wait_ge(p_ready, u - S_RING + 1)
                elif u < 2:
                    pe.wait_ge(cmp_shift, NT - 1 + u)
                dst, q = SCORE[u % S_RING], q[:, t * P:(t + 1) * P]
                pe.matmul(dst[:, 0:n], q, kh[:, 0:n], start=True, stop=False)
                pe.matmul(dst[:, t * P:n], ident_b[:, :], mask_b[:, :], start=False, stop=False)
                if heads[v][0] == "fox":
                    pe.matmul(dst[:, 0:n], head_sel[:, heads[v][1], :], c_parts[:, 0:n], start=False, stop=False)
                pe.matmul(dst[:, 0:n], q, kl[:, 0:n], start=False, stop=True).then_inc(s_ready, 1)

            def unit_transpose(u):
                pe.wait_ge(p_ready, u + 1)
                if u >= PTB:
                    wait_pT(pe, u - PTB)
                for j in range(u % NT + 1):
                    cols = slice(j * P, (j + 1) * P)
                    mm = pe.transpose(PT[u % PTB][:, cols], probs[:, u % P_RING, cols], ident)
                mm.then_inc(pT_ready, 1)

            def unit_values(u):
                v, t = divmod(u, NT)
                wait_pT(pe, u)
                if t == 0 and v >= 2:
                    pe.wait_ge(head_done, v - 1)
                elif t == 0:
                    pe.wait_ge(cmp_o_read, NT - 1 + v)
                val = values_of(u)
                for j in range(t + 1):
                    mm = pe.matmul(OUT[v % 2][:, t * HD:(t + 1) * HD], pT[:, u % PT_RING, j * P:(j + 1) * P], val[:, j, :],
                                   start=(j == 0), stop=(j == t))
                mm.then_inc(av_done, 1)

            def attention(first, last):
                for s, inside in steps(first, last):
                    if s == 2:
                        cmp_transpose(NT - 1)
                    if s == 3:
                        cmp_values(NT - 1)
                    if s == last + T_LAG - 1:
                        pe.wait_ge(p_ready, last)
                        project(NSA_END if last == NSA_UNITS else FOX_END)
                    if inside(s) is not None:
                        unit_scores(s)
                    if inside(s - T_LAG) is not None:
                        unit_transpose(s - T_LAG)
                    if inside(s - V_LAG) is not None:
                        unit_values(s - V_LAG)

            pe.wait_ge(ones_ready, 1)
            for k in range(KT):
                pe.wait_ge(x_sq, k + 1)
                pe.matmul(MEAN[:, :], ones[:, :], qr[:, k % 2, :], start=(k == 0),
                          stop=(k == KT - 1)).then_inc(x_sq_used, 1)
            for c in range(NSA_END):
                project(c)
                if c >= 1 and CHUNKS[c - 1][0] == "u":
                    gates_of(CHUNKS[c - 1][1])
                if c >= 1 and c - 1 in NORMED and CHUNKS[c][0] not in TOKEN_MAJOR:
                    head_mean(c - 1)
                if c == AT["kc", 0]:
                    pe.wait_ge(rstd_ready, 1)
                    pe.wait_ge(const_loaded, 16)
                    pe.wait_ge(lru_sig, 2 * LRU_T)
                    for t in range(NT):
                        mm = pe.transpose(AUX_B[:, t * P:(t + 1) * P], rstd_bc[:, t * P:(t + 1) * P], ident)
                    mm.then_inc(rstd_T, 1)
                if c == AT["vc", 0]:
                    pe.wait_ge(fg_act, 1)
                    for t in range(NT):
                        mm = pe.transpose(AUX_A[:, t * 64:(t + 1) * 64], std[0:64, t * P:(t + 1) * P], ident[0:64, 0:64])
                    mm.then_inc(gates_T, 1)
                if c == AT["kw", 0]:
                    pe.wait_ge(gates_ready, 1)
                    compress(0)
                if c == AT["nq", 1]:
                    pe.wait_ge(rcol_ready, 1)
                    compress(1)
                    pe.wait_ge(cmp_sq, 1)
                    pe.matmul(AUX_A[0:HD, 0:KVH * CMP_PAD], block_mean[0:HD, 0:HD],
                              k_cmp_sq[:, :, :].rearrange("p g n -> p (g n)"), start=True, stop=True)\
                        .then_inc(cmp_mean, 1)
                if c == AT["nq", 3]:
                    pe.wait_ge(cmp_evac, 2)
                    for g in range(KVH):
                        mm = pe.transpose(AUX_B[0:CMP_PAD, g * HD:(g + 1) * HD], v_cmp[:, g, :], ident[0:HD, 0:HD])
                    mm.then_inc(v_cmp_T, 1)
                if CHUNKS[c][0] == "zl":
                    t = CHUNKS[c][1]
                    if t >= 1:
                        cmp_transpose(t - 1)
                    cmp_scores(t)
                    if t >= 1:
                        cmp_values(t - 1)
            pe.wait_ge(proj_read, proj_units(NSA_END))
            attention(0, NSA_UNITS)

            def o_transposed(c):
                i = c - FIRST_Z
                if i >= 2:
                    pe.wait_ge(y_ready, i - 1)
                src = o_nsa if i < 4 else o_fox
                for t in range(NT):
                    mm = pe.transpose(OUT[i % 2][:, t * P:(t + 1) * P], src[:, t, (i % 4) * P:(i % 4 + 1) * P], ident)
                mm.then_inc(oT_ready, 1)

            for c in range(NSA_END, FOX_END):
                if c == NSA_END + 1:
                    wait_pT(pe, NSA_UNITS - 1)
                    pe.wait_ge(head_done, 2 * HEADS)
                if c > NSA_END:
                    project(c)
                if c - 1 in NORMED and CHUNKS[c][0] not in TOKEN_MAJOR:
                    head_mean(c - 1)
                if CHUNKS[c][0] == "zn":
                    o_transposed(c)
            pe.wait_ge(stacked, 16 * stack_copies(len(NORMED)))
            pe.wait_ge(proj_read, proj_units(FOX_END))
            pe.wait_ge(normed, len(NORMED))
            pe.wait_ge(y_ready, 4)
            pe.wait_ge(c_ready, 1)
            attention(NSA_UNITS, UNITS)
            for c in range(FOX_END, N_IN):
                if c == FOX_END + 1:
                    wait_pT(pe, UNITS - 1)
                if c > FOX_END:
                    project(c)
                if c == FOX_END:
                    pe.wait_ge(head_done, len(heads))
                o_transposed(c)
            for e in range(ET):
                c = N_IN + e
                pe.wait_ge(wl_ready, c + 1)
                pe.wait_ge(yl_ready, e + 1)
                for n, t in enumerate(OUT_ORDER):
                    if e == 0:
                        pe.wait_ge(proj_read, proj_units(N_IN))
                        if n == NT - 1:
                            pe.wait_ge(y_ready, 8)
                    toks = slice(t * P, (t + 1) * P)
                    for half in range(2):
                        dst = bank[2 * t + half][:, :]
                        cols = slice(half * 512, (half + 1) * 512)
                        pe.matmul(dst, yh[:, e, toks], wh[:, c % HL, cols], start=(e == 0), stop=False)
                        pe.matmul(dst, yh[:, e, toks], wl[:, c % HL, cols], start=False, stop=False)
                        mm = pe.matmul(dst, yl[:, e, toks], wh[:, c % HL, cols], start=False, stop=(e == ET - 1))
                        if e == ET - 1:
                            mm.then_inc(out_sum, 1)
                if e < ET - 1:
                    mm.then_inc(w_used, 1)


def pack(x, norm_g, w_in, w_out, conv_w, conv_b, lru_wa, lru_ba, lru_wx, lru_bx, lru_lambda, nsa_q_g, nsa_k_g,
         cmp_pe_k, cmp_pe_v, cmp_wk, cmp_wv, nsa_gate_b, fox_q_g, fox_k_g, fox_f_b):
    f = np.float32
    w = w_in[0]
    chunks = np.zeros((N_IN, P, KT, P), f)
    for c, (kind, j) in enumerate(CHUNKS):
        if kind == "fg":
            chunks[c, :, :, 0:HEADS] = w[:, COLS["fl"]:COLS["fl"] + HEADS].reshape(KT, P, -1).transpose(1, 0, 2)
            chunks[c, :, :, 32:32 + 3 * HEADS] = (
                w[:, COLS["gl"]:COLS["gl"] + 3 * HEADS].reshape(KT, P, -1).transpose(1, 0, 2))
            continue
        o = COLS[("vs", "vw")[j]] if kind == "vn" else COLS[kind] + j * P
        chunks[c] = w[:, o:o + P].reshape(KT, P, P).transpose(1, 0, 2)
    chan = np.zeros((P, CH_W), f)

    def put(name, a):
        a = np.asarray(a)
        chan[0:a.shape[0], CH[name]:CH[name] + a.shape[1]] = a

    put("norm_g", norm_g[0].reshape(KT, P).T)
    put("conv_w", conv_w[0].reshape(CONV * LRU_T, P).T)
    for name, a in (("conv_b", conv_b), ("ba", lru_ba), ("bx", lru_bx), ("lam", lru_lambda)):
        put(name, a[0].reshape(LRU_T, P).T)
    for name, a in (("nq_g", nsa_q_g[0]), ("kcmp_g", nsa_k_g[0, 0]), ("ks_g", nsa_k_g[0, 1]), ("kw_g", nsa_k_g[0, 2]),
                    ("fq_g", fox_q_g[0]), ("fk_g", fox_k_g[0])):
        put(name, np.concatenate([a, a])[:, None])
    chan[0:HEADS, CH["fg_b"]] = fox_f_b[0]
    chan[32:32 + 3 * HEADS, CH["fg_b"]] = nsa_gate_b[0]
    for name, a in (("pe_k", cmp_pe_k), ("pe_v", cmp_pe_v)):
        put(name, a[0].reshape(CMP_LEN // 2, 2, HD).transpose(1, 2, 0).reshape(P, CMP_LEN // 2))
    lru = np.zeros((P, 2, LRU_T, P), f)
    for i, a in enumerate((lru_wa[0], lru_wx[0])):
        for b in range(2 * LRU_T):
            r = (b % 2) * HD
            lru[r:r + HD, i, b // 2, r:r + HD] = a[b]
    cmp = np.stack([a[0].reshape(CMP_LEN // 2, 2, HD, HD).transpose(1, 2, 0, 3).reshape(P, CMP_LEN // 2, HD)
                    for a in (cmp_wk, cmp_wv)], axis=1)
    return {
        "xT": x[0].T.reshape(KT, P, SEQ).transpose(1, 0, 2),
        "x_tok": x[0].reshape(NT, P, D).transpose(1, 0, 2),
        "w_in": chunks.reshape(N_IN, P, D),
        "w_out": w_out[0].reshape(ET, P, D),
        "chan": chan, "const": constants(), "lru_w": lru, "cmp_w": cmp,
    }


def constants():
    c = np.zeros((P, CONST_W), np.float32)
    i = np.arange(P)
    c[:, IDENT:IDENT + P] = np.eye(P)
    c[:, BLOCK:BLOCK + P] = (i[:, None] // HD == i[None, :] // HD) / HD
    c[:, CAUSAL:CAUSAL + P] = np.where(i[None, :] > i[:, None], NEG, 0.0)
    n = np.arange(CMP_PAD)
    for t in range(NT):
        seen = (n[None, :] * CMP_STRIDE + CMP_LEN - 1 <= (t * P + i)[:, None]) & (n[None, :] < N_CMP)
        c[:, CMPMASK + t * CMP_PAD:CMPMASK + (t + 1) * CMP_PAD] = np.where(seen, 0.0, NEG)
    return c


def kernel(**inputs):
    import concourse.bacc as bacc
    from concourse.bass_utils import run_bass_kernel_spmd

    nc = bacc.Bacc("TRN2", target_bir_lowering=False, num_devices=1)
    arrays, args = {}, []
    for name, a in pack(**{k: np.asarray(v) for k, v in inputs.items()}).items():
        a = np.ascontiguousarray(a)
        arrays[f"in_{name}"] = a
        args.append(nc.dram_tensor(f"in_{name}", a.shape, mybir.dt.from_np(a.dtype), kind="ExternalInput").ap())
    y = nc.dram_tensor("out_y", (SEQ, D), F32, kind="ExternalOutput").ap()
    program(nc, *args, y)
    r = run_bass_kernel_spmd(nc, [arrays], core_ids=[0])
    return r.results[0]["out_y"].reshape(1, SEQ, D)
```

```python
from contextlib import ExitStack

import numpy as np

import concourse.bass as bass
from concourse import mybir

F32 = mybir.dt.float32
F32R = mybir.dt.float32r
BF16 = mybir.dt.bfloat16
ACT = mybir.ActivationFunctionType
ALU = mybir.AluOpType
AX = mybir.AxisListType

P = 128
SEQ, D = 512, 1024
HD = 64
KT = D // P
NT = SEQ // P
LRU_T = 512 // P
HEADS = 8
KVH = 2
GROUP = HEADS // KVH
CMP_LEN, CMP_STRIDE = 32, 16
N_CMP = (SEQ - CMP_LEN) // CMP_STRIDE + 1
CMP_PAD = 32
CONV = 4
D_MIX = 1536
ET = D_MIX // P
EPS = 1e-6
NEG = -1e30

CHUNKS = ([("u", j) for j in range(4)] + [("fg", 0), ("kc", 0), ("vc", 0), ("ks", 0), ("kw", 0)]
          + [("nq", j) for j in range(4)] + [("vn", 0), ("vn", 1)] + [("zl", j) for j in range(4)]
          + [("fq", j) for j in range(4)] + [("fk", 0), ("vf", 0), ("vf", 1)] + [("fk", j) for j in range(1, 4)]
          + [("vf", 2), ("vf", 3)] + [("zn", j) for j in range(4)] + [("zf", j) for j in range(4)])
N_IN = len(CHUNKS)
N_STREAM = N_IN + ET
AT = {x: c for c, x in enumerate(CHUNKS)}
NORMED = [c for c, (kind, _) in enumerate(CHUNKS) if kind in ("ks", "kw", "nq", "fq", "fk")]
TOKEN_MAJOR = ("vn", "vf")
NSA_END = AT["zl", 3] + 1
FOX_END = AT["zn", 3] + 1
RAW, HL = 3, 4
AHEAD = 3
T_LAG, V_LAG = 3, 5
S_RING, P_RING, PT_RING, M_RING = 4, 4, 3, 8

MIDDLE = 3

COLS = {"u": 0, "zl": 512, "nq": 1024, "kc": 1536, "vc": 1664, "ks": 1792, "vs": 1920, "kw": 2048, "vw": 2176,
        "gl": 2304, "zn": 2328, "fq": 2840, "fk": 3352, "vf": 3864, "fl": 4376, "zf": 4384}

CH = {}
_at = 0
for _n, _w in (("norm_g", KT), ("conv_w", CONV * LRU_T), ("conv_b", LRU_T), ("ba", LRU_T), ("bx", LRU_T),
               ("lam", LRU_T), ("nq_g", 1), ("kcmp_g", 1), ("ks_g", 1), ("kw_g", 1), ("fq_g", 1), ("fk_g", 1),
               ("fg_b", 1), ("pe_k", CMP_LEN // 2), ("pe_v", CMP_LEN // 2)):
    CH[_n] = _at
    _at += _w
CH_W = _at

IDENT, BLOCK, CAUSAL, CMPMASK, CONST_W = 0, P, 2 * P, 3 * P, 3 * P + NT * CMP_PAD

FIRST_Z = AT["zn", 0]
TAIL_AT = (AT["vc", 0], AT["vc", 0], AT["ks", 0], AT["ks", 0], AT["kw", 0], AT["nq", 0], AT["vn", 0], AT["vn", 0])
OUT_ORDER = (2, 0, 3, 1)
STACK_LAG = 6
POOL_SQUARES = (1, 3, 5)
VECTOR_SQUARES = tuple(k for k in range(KT) if k not in POOL_SQUARES)

GAIN = {"ks": "ks_g", "kw": "kw_g", "nq": "nq_g", "fq": "fq_g", "fk": "fk_g"}


def program(nc, xT, x_tok, w_in, w_out, chan, const, lru_w, cmp_w, out):
    ctx = ExitStack()
    with ctx:
        def sem(name):
            return ctx.enter_context(nc.semaphore(name))

        def sb(name, shape, dt=F32, where=ctx):
            return where.enter_context(nc.sbuf_tensor(name, shape, dt))

        raw = sb("raw", [P, RAW, D])
        wh = sb("wh", [P, HL, D], F32R)
        wl = sb("wl", [P, HL, D], F32R)
        cst = sb("cst", [P, CONST_W])
        chn = sb("chn", [P, CH_W])
        ident, block_mean = (cst[:, o:o + P] for o in (IDENT, BLOCK))
        ones = sb("ones", [P, P])
        ident_b = sb("ident_b", [P, P], BF16)
        mask_b = sb("mask_b", [P, P], BF16)
        head_sel_f = sb("head_sel_f", [P, HEADS * P], BF16)
        head_sel = head_sel_f[0:96, :].rearrange("p (h q) -> p h q", h=HEADS)
        log_f = head_sel_f[96:96 + HEADS, :].bitcast(F32)
        c_parts = sb("c_parts", [96, SEQ], BF16)
        rstd_bc = sb("rstd_bc", [P, SEQ])
        rstd_col = sb("rstd_col", [P, NT])
        y_lru = sb("y_lru", [P, LRU_T, SEQ])
        gates = sb("gates", [P, NT, 3 * HEADS])
        qr = sb("qr", [P, 2, SEQ])
        sq = sb("sq", [P, SEQ])
        std = sb("std", [P, SEQ])
        work = sb("work", [P, SEQ])
        eps1 = sb("eps1", [P, 1])
        eps64 = sb("eps64", [P, 1])
        one1 = sb("one1", [P, 1])
        half_eps = sb("half_eps", [P, 2])
        csp = sb("csp", [P, 2, LRU_T])
        negmax = sb("negmax", [P, M_RING])
        rsum = sb("rsum", [P, 3, NT])
        rcp = sb("rcp", [P, 2, NT])
        k_cmp = sb("k_cmp", [HD, KVH, CMP_PAD])
        k_cmp_sq = sb("k_cmp_sq", [HD, KVH, CMP_PAD])
        k_cmp_y = sb("k_cmp_y", [HD, KVH, CMP_PAD])
        k_cmp_w = sb("k_cmp_w", [HD, KVH, CMP_PAD])
        v_nsa = sb("v_nsa", [P, NT, 2 * KVH * HD])
        o_nsa = sb("o_nsa", [P, NT, HEADS * HD])
        k_cmp_parts = sb("k_cmp_parts", [P, KVH, 2, CMP_PAD], F32R)
        k_cmp_h, k_cmp_l = k_cmp_parts[:, :, 0, :], k_cmp_parts[:, :, 1, :]
        v_cmp = sb("v_cmp", [HD, KVH, CMP_PAD])
        v_blocks = sb("v_blocks", [P, KVH, GROUP * HD])
        cmp_stat = sb("cmp_stat", [P, 3, HEADS])

        with ExitStack() as v:
            xh = sb("xh", [P, KT, SEQ], F32R, v)
            xl = sb("xl", [P, KT, SEQ], F32R, v)
            with ExitStack() as m:
                q_nsa = sb("q_nsa", [P, HEADS, SEQ], F32R, m)
                kh_nsa = sb("kh_nsa", [P, 2 * KVH, SEQ], F32R, m)
                kl_nsa = sb("kl_nsa", [P, 2 * KVH, SEQ], F32R, m)
                cmp_w_sb = sb("cmp_w_sb", [P, 2, CMP_LEN // 2, HD], F32, m)
                kv_cm = sb("kv_cm", [P, 2, SEQ], F32, m)
                kv_pair = sb("kv_pair", [P, KVH, SEQ], F32, m)
                kv_pe = sb("kv_pe", [P, 2, KVH, SEQ // 16, 8], F32, m)
                with ExitStack() as w:
                    x_raw = sb("x_raw", [P, KT, SEQ], F32, w)
                with ExitStack() as w:
                    u_pad = sb("u_pad", [P, LRU_T, SEQ + CONV - 1], F32, w)
                    xc = sb("xc", [P, LRU_T, SEQ], F32, w)
                    tau = sb("tau", [P, LRU_T, SEQ], F32, w)
                    ig = sb("ig", [P, LRU_T, SEQ], F32, w)
                    lru_w_sb = sb("lru_w_sb", [P, 2, LRU_T, P], F32, w)
                with ExitStack() as w:
                    v_fox = sb("v_fox", [P, NT, HEADS * HD], F32, w)
                    o_fox = sb("o_fox", [P, NT, HEADS * HD], F32, w)
                    head_out = sb("head_out", [P, NT * HD], F32, w)
                    probs = sb("probs", [P, P_RING, SEQ], F32, w)
                    pT = sb("pT", [P, PT_RING, SEQ], F32, w)
            with ExitStack() as m:
                q_fox = sb("q_fox", [P, HEADS, SEQ], F32R, m)
                kh_fox = sb("kh_fox", [P, HEADS, SEQ], F32R, m)
                kl_fox = sb("kl_fox", [P, HEADS, SEQ], F32R, m)
            with ExitStack() as m:
                yh = sb("yh", [P, ET, SEQ], F32R, m)
                yl = sb("yl", [P, ET, SEQ], F32R, m)
        with ExitStack() as v:
            x_res = sb("x_res", [P, NT, D], F32, v)
            y_out = sb("y_out", [P, NT, D], F32, v)

        bank = [ctx.enter_context(nc.psum_tensor(f"bank{i}", [P, SEQ], F32)) for i in range(8)]
        PROJ = (bank[6], bank[0], bank[1])
        AUX_A, AUX_B, MEAN = bank[2], bank[3], bank[4]
        NORM_W = bank[5]
        SCORE = (bank[4], bank[5], bank[6], bank[0])
        PT = (bank[7], bank[1])
        PTB = len(PT)
        OUT = (bank[2], bank[3])

        x_loaded = [sem(f"x_loaded{k}") for k in range(KT)]
        const_loaded, chan_loaded = sem("const_loaded"), sem("chan_loaded")
        lru_w_loaded, cmp_w_loaded = sem("lru_w_loaded"), sem("cmp_w_loaded")
        raw_loaded = [sem(f"raw_loaded{i}") for i in range(RAW)]
        wh_ready, wl_ready, w_used = sem("wh_ready"), sem("wl_ready"), sem("w_used")
        xh_ready, xl_ready, x_sq = sem("xh_ready"), sem("xl_ready"), sem("x_sq")
        x_sq_pool, x_sq_used = sem("x_sq_pool"), sem("x_sq_used")
        std_ready = sem("std_ready")
        rstd_ready, rstd_T, rcol_ready = sem("rstd_ready"), sem("rstd_T"), sem("rcol_ready")
        small_consts = sem("small_consts")
        proj_done, proj_read = sem("proj_done"), sem("proj_read")
        conv_first, conv_done = sem("conv_first"), sem("conv_done")
        lru_gates, lru_sig, lru_tau = sem("lru_gates"), sem("lru_sig"), sem("lru_tau")
        lam_act, csp_ready = sem("lam_act"), sem("csp_ready")
        zl_sig, zl_done, sel_ready = sem("zl_sig"), sem("zl_done"), sem("sel_ready")
        ones_ready = sem("ones_ready")
        lru_sqrt, lru_seed = sem("lru_sqrt"), sem("lru_seed")
        lru_ix, lru_ixs, lru_h = sem("lru_ix"), sem("lru_ixs"), sem("lru_h")
        fg_act, gates_T, gates_ready, c_ready = sem("fg_act"), sem("gates_T"), sem("gates_ready"), sem("c_ready")
        kv_shifted = [sem("kv_shifted_k"), sem("kv_shifted_v")]
        kv_pe_ready, cmp_prod = sem("kv_pe_ready"), sem("cmp_prod")
        cmp_evac, cmp_sq, cmp_mean, cmp_std = sem("cmp_evac"), sem("cmp_sq"), sem("cmp_mean"), sem("cmp_std")
        k_cmp_n, k_cmp_hr, k_cmp_ready = sem("k_cmp_n"), sem("k_cmp_hr"), sem("k_cmp_ready")
        v_cmp_T, v_cmp_ready = sem("v_cmp_T"), sem("v_cmp_ready")
        sq_ready, norm_mean, norm_seed = sem("sq_ready"), sem("norm_mean"), sem("norm_seed")
        normed, h_ready, l_ready, stacked = sem("normed"), sem("h_ready"), sem("l_ready"), sem("stacked")
        cmp_s, cmp_shift, cmp_exp, cmp_p = sem("cmp_s"), sem("cmp_shift"), sem("cmp_exp"), sem("cmp_p")
        cmp_pT, cmp_pT_sb, cmp_o, cmp_o_read = sem("cmp_pT"), sem("cmp_pT_sb"), sem("cmp_o"), sem("cmp_o_read")
        s_ready, max_ready, p_ready = sem("s_ready"), sem("max_ready"), sem("p_ready")
        pT_ready, pT_dve, pT_act = sem("pT_ready"), sem("pT_dve"), sem("pT_act")
        av_done, head_done = sem("av_done"), sem("head_done")
        oT_ready, z_sig, y_ready = sem("oT_ready"), sem("z_sig"), sem("y_ready")
        yh_ready, yl_ready = sem("yh_ready"), sem("yl_ready")
        out_sum, out_ready, res_loaded, stored = sem("out_sum"), sem("out_ready"), sem("res_loaded"), sem("stored")

        def chain(eng, name):
            s, n = sem(name), [0]

            def link(ins):
                n[0] += 1
                ins.then_inc(s, 1)
                eng().wait_ge(s, n[0])
            return link

        def proj_units(c):
            return sum(1 if k not in TOKEN_MAJOR else NT if j % 2 == 0 else 0 for k, j in CHUNKS[:c])

        def proj_bank(unit):
            first = max(proj_units(c) for c in (0, NSA_END, FOX_END) if proj_units(c) <= unit)
            return PROJ[(unit - first) % len(PROJ)]

        def wait_bank(eng, unit):
            if unit >= len(PROJ):
                eng.wait_ge(proj_read, unit - len(PROJ) + 1)

        def nth_normed(c):
            return NORMED.index(c)

        def stack_copies(c):
            return sum(0 if CHUNKS[x][0] in ("nq", "fq") else 4 for x in NORMED[:c])

        def pool_square(k):
            return (sq, work, std)[POOL_SQUARES.index(k)][:, :]

        def half_of(s):
            return slice(s * HD, (s + 1) * HD)

        def key_planes(c, s):
            kind, j = CHUNKS[c]
            if kind == "fk":
                return kh_fox[:, 2 * j + s, :], kl_fox[:, 2 * j + s, :]
            k = s + (KVH if kind == "kw" else 0)
            return kh_nsa[:, k, :], kl_nsa[:, k, :]

        def operand_parts(c, s):
            kind, j = CHUNKS[c]
            own, other = half_of(s), half_of(1 - s)
            if kind in ("nq", "fq"):
                q = (q_nsa if kind == "nq" else q_fox)[:, 2 * j + s, :]
                return q[own, :], q[other, :]
            return tuple(plane[own, :] for plane in key_planes(c, s))

        def wait_slot(eng, c):
            k = c - HL
            if k >= N_IN:
                eng.wait_ge(w_used, k - N_IN + 1)
            elif k >= 0:
                eng.wait_ge(proj_done, proj_units(k + 1))

        heads = [("nsa", h, b) for h in range(HEADS) for b in (1, 2)] + [("fox", h, 0) for h in range(HEADS)]
        NSA_UNITS, UNITS = 2 * HEADS * NT, len(heads) * NT

        def scores_of(u):
            group, h, b = heads[u // NT]
            if group == "nsa":
                k = 2 * (b - 1) + h // GROUP
                return q_nsa[:, h, :], kh_nsa[:, k, :], kl_nsa[:, k, :]
            return q_fox[:, h, :], kh_fox[:, h, :], kl_fox[:, h, :]

        def values_of(u):
            group, h, b = heads[u // NT]
            if group == "nsa":
                k = 2 * (b - 1) + h // GROUP
                return v_nsa[:, :, k * HD:(k + 1) * HD]
            return v_fox[:, :, h * HD:(h + 1) * HD]

        def by_token(ap):
            return ap.rearrange("p (t q) -> p t q", t=NT)

        def older_outputs(i):
            return (2 * (i - 4), 2 * (i - 4) + 1)

        def split_outputs(e):
            order = [x for i in range(4, 8) for x in (LRU_T + i,) + older_outputs(i)]
            return order.index(e) + 1

        def output_tile(e):
            if e < LRU_T:
                return lambda y: y[:, e, :], y_lru[:, e, :]
            i = e - LRU_T
            return lambda y: by_token(y[:, e, :]), o_nsa[:, :, i * P:(i + 1) * P]

        def wait_pT(eng, u):
            if u % NT == NT - 1:
                eng.wait_ge(pT_act, u // NT + 1)
            else:
                eng.wait_ge(pT_dve, 3 * (u // NT) + u % NT + 1)

        def steps(first, last):
            return [(s, (lambda u: u if first <= u < last else None)) for s in range(first, last + V_LAG + 2)]

        block = ctx.enter_context(nc.Block())

        @block.sync
        def _(sp):
            def load_w(c):
                if c >= N_STREAM:
                    return
                if c >= RAW:
                    sp.wait_ge(wl_ready, c - RAW + 1)
                src = w_in[c] if c < N_IN else w_out[c - N_IN]
                sp.dma_start(raw[:, c % RAW, :], src).then_inc(raw_loaded[c % RAW], 16)

            def stack(c):
                n = nth_normed(c)
                sp.wait_ge(h_ready, 2 * n + 2)
                sp.wait_ge(l_ready, n + 1)
                for s in range(2):
                    own, other = half_of(s), half_of(1 - s)
                    for plane in key_planes(c, s):
                        sp.dma_start(plane[other, :].bitcast(F32), plane[own, :].bitcast(F32)).then_inc(stacked, 16)

            def pair_up(i):
                sp.wait_ge(proj_read, proj_units(AT["kc" if i == 0 else "vc", 0]) + 1)
                if i == 1:
                    sp.wait_ge(kv_pe_ready, 1)
                for g in range(KVH):
                    half = slice(g * HD, (g + 1) * HD)
                    sp.dma_start(kv_pair[0:HD, g, :], kv_cm[half, i, :]).then_inc(kv_shifted[i], 16)
                    sp.dma_start(kv_pair[HD:P, g, 0:SEQ - 1], kv_cm[half, i, 1:SEQ]).then_inc(kv_shifted[i], 16)

            for k in range(KT):
                sp.dma_start(x_raw[:, k, :], xT[:, k, :]).then_inc(x_loaded[k], 16)
                if k == 0:
                    sp.dma_start(chn[:, :], chan).then_inc(chan_loaded, 16)
                if k == KT // 2 - 1:
                    load_w(0)
            load_w(1)
            load_w(2)
            sp.dma_start(cst[:, :], const).then_inc(const_loaded, 16)
            sp.dma_start(cmp_w_sb[:, :, :, :], cmp_w).then_inc(cmp_w_loaded, 16)
            load_w(3)
            sp.wait_ge(xl_ready, KT)
            sp.wait_ge(x_sq, len(VECTOR_SQUARES))
            sp.wait_ge(x_sq_pool, len(POOL_SQUARES))
            sp.dma_start(lru_w_sb[:, :, :, :], lru_w).then_inc(lru_w_loaded, 16)
            for c in range(4, N_STREAM + 6):
                load_w(c)
                k = c - 5
                if 0 <= k < N_IN:
                    if CHUNKS[k][0] in ("kc", "vc"):
                        pair_up(0 if CHUNKS[k][0] == "kc" else 1)
                k = c - STACK_LAG
                if 0 <= k < N_IN and CHUNKS[k][0] in ("ks", "kw", "fk"):
                    stack(k)
                if c == N_IN + 4:
                    sp.wait_ge(proj_done, proj_units(N_IN))
                    sp.dma_start(x_res[:, :, :], x_tok).then_inc(res_loaded, 16)
            for n, t in enumerate(OUT_ORDER):
                for half in range(2):
                    cols = slice(half * 512, (half + 1) * 512)
                    sp.wait_ge(out_ready, 2 * n + half + 1)
                    sp.dma_start(out[t * P:(t + 1) * P, cols], y_out[:, t, cols]).then_inc(stored, 16)
            sp.wait_ge(stored, 16 * 2 * NT)

        @block.gpsimd
        def _(pool):
            nc.gpsimd.memset(ones[:, :], 1.0).then_inc(ones_ready, 1)
            nc.gpsimd.memset(eps1[:, :], EPS)
            nc.gpsimd.memset(half_eps[:, 0:1], -0.5 * EPS)
            nc.gpsimd.memset(half_eps[:, 1:2], -32 * EPS)
            nc.gpsimd.memset(eps64[:, :], 64 * EPS)
            nc.gpsimd.memset(one1[:, :], 1.0)
            nc.gpsimd.memset(c_parts[:, :], 0.0)
            nc.gpsimd.memset(k_cmp[:, :, :], 0.0)
            nc.gpsimd.memset(v_cmp[:, :, :], 0.0)
            nc.gpsimd.memset(v_blocks[:, :, :], 0.0).then_inc(small_consts, 1)
            for k in POOL_SQUARES:
                pool.wait_ge(x_loaded[k], 16)
                nc.gpsimd.tensor_tensor(pool_square(k), x_raw[:, k, :], x_raw[:, k, :], ALU.mult).then_inc(x_sq_pool, 1)
            for c in range(N_STREAM):
                pool.wait_ge(wh_ready, c + 1)
                nc.gpsimd.tensor_tensor(wl[:, c % HL, :], raw[:, c % RAW, :], wh[:, c % HL, :].bitcast(F32),
                                        ALU.subtract).then_inc(wl_ready, 1)
                j = c - AHEAD - 1
                if 0 <= j < LRU_T:
                    pool.wait_ge(lru_sig, 2 * j + 2)
                    nc.gpsimd.tensor_tensor(ig[:, j, :], ig[:, j, :], xc[:, j, :], ALU.mult).then_inc(lru_ix, 1)
                j = c - AHEAD - 1 - LRU_T
                if 0 <= j < LRU_T:
                    pool.wait_ge(lru_sqrt, j + 1)
                    pool.wait_ge(lru_ix, j + 1)
                    nc.gpsimd.tensor_tensor(ig[:, j, :], ig[:, j, :], u_pad[:, j, 0:SEQ],
                                            ALU.mult).then_inc(lru_ixs, 1)

        @block.scalar
        def _(act):
            link = chain(lambda: act, "act_chain")

            def split(c):
                if c >= N_STREAM:
                    return
                act.wait_ge(raw_loaded[c % RAW], 16 * (c // RAW + 1))
                wait_slot(act, c)
                act.activation(wh[:, c % HL, :], raw[:, c % RAW, :], ACT.Copy).then_inc(wh_ready, 1)

            def ch(name, j=0):
                return chn[:, CH[name] + j:CH[name] + j + 1]

            def rsqrt_seed(x, scale, y, y2, w, rows=P):
                big = scale != 1.0
                link(act.activation(y, x, ACT.Ln, bias=(eps64 if big else eps1)[0:rows, :], scale=scale))
                link(act.activation(y, y, ACT.Exp, scale=-0.5))
                act.activation(y2, y, ACT.Square)
                return act.activation(w, x, ACT.Identity, bias=half_eps[0:rows, int(big):int(big) + 1],
                                      scale=-0.5 * scale)

            def before(c):
                kind, j = CHUNKS[c]
                if kind == "u":
                    act.wait_ge(proj_read, proj_units(c) + 1)
                    act.activation(xc[:, j, :], u_pad[:, j, 0:SEQ], ACT.Identity, bias=ch("conv_b", j),
                                   scale=ch("conv_w", j)).then_inc(conv_first, 1)
                if kind == "zl":
                    act.wait_ge(proj_read, proj_units(c) + 1)
                    if j >= 1:
                        act.wait_ge(zl_done, j)
                    act.activation(sq[:, :], y_lru[:, j, :], ACT.Sigmoid).then_inc(zl_sig, 1)
                if c in NORMED:
                    act.wait_ge(proj_read, proj_units(c) + 1)
                    n = nth_normed(c)
                    if n >= 1:
                        act.wait_ge(norm_mean, n)
                    act.activation(sq[:, :], qr[:, n % 2, :], ACT.Square).then_inc(sq_ready, 1)

            def after(c):
                kind, j = CHUNKS[c]
                if kind == "u":
                    if j == 0:
                        act.wait_ge(csp_ready, 1)
                    act.wait_ge(lru_gates, j + 1)
                    act.activation(tau[:, j, :], AUX_A[:, :], ACT.Sigmoid, bias=ch("ba", j)).then_inc(lru_sig, 1)
                    act.activation(ig[:, j, :], AUX_B[:, :], ACT.Sigmoid, bias=ch("bx", j)).then_inc(lru_sig, 1)
                    act.wait_ge(lru_sig, 2 * j + 2)
                    act.activation(tau[:, j, :], tau[:, j, :], ACT.Tanh,
                                   scale=csp[:, 0, j:j + 1]).then_inc(lru_tau, 1)
                if kind == "fg":
                    act.wait_ge(proj_read, proj_units(c) + 1)
                    b = ch("fg_b")
                    act.activation(std[0:64, :], qr[0:64, 0, :], ACT.Sigmoid, bias=b[0:64]).then_inc(fg_act, 1)
                    link(act.activation(sq[0:HEADS, :], qr[0:HEADS, 0, :], ACT.Abs, bias=b[0:HEADS]))

            def norm_seeds(c):
                kind = CHUNKS[c][0]
                if c in NORMED:
                    n = nth_normed(c)
                    act.wait_ge(norm_mean, n + 1)
                    eighth = kind in ("nq", "fq")
                    if n >= 1:
                        act.wait_ge(normed, n)
                    rsqrt_seed(MEAN[:, :], 64.0 if eighth else 1.0, std[:, :], work[:, :],
                               NORM_W[:, :]).then_inc(norm_seed, 1)

            def norm_high(c):
                kind, j = CHUNKS[c]
                if c in NORMED:
                    n = nth_normed(c)
                    act.wait_ge(normed, n + 1)
                    if kind == "fq" and j == 0:
                        act.wait_ge(s_ready, NSA_UNITS)
                    for s in range(2):
                        high, _ = operand_parts(c, s)
                        act.activation(high, qr[half_of(s), n % 2, :], ACT.Copy).then_inc(h_ready, 1)

            def read_tokens(c, first, last):
                kind, j = CHUNKS[c]
                if kind not in TOKEN_MAJOR or j % 2:
                    return
                for t in range(first, last):
                    unit = proj_units(c) + t
                    if t == 0:
                        act.wait_ge(proj_read, unit)
                        act.wait_ge(rcol_ready, 1)
                    act.wait_ge(proj_done, unit + 1)
                    dst = v_nsa[:, t, :] if kind == "vn" else v_fox[:, t, j * P:(j + 2) * P]
                    act.activation(dst, proj_bank(unit)[:, 0:2 * P], ACT.Copy,
                                   scale=rstd_col[:, t:t + 1]).then_inc(proj_read, 1)

            def z_gate(c):
                i = c - FIRST_Z
                act.wait_ge(proj_read, proj_units(c) + 1)
                if i >= 1:
                    act.wait_ge(y_ready, i)
                act.activation(sq[:, :], qr[:, i % 2, :], ACT.Sigmoid).then_inc(z_sig, 1)

            def unit_exp(u):
                v, t = divmod(u, NT)
                act.wait_ge(max_ready, u + 1)
                if u >= P_RING:
                    act.wait_ge(pT_ready, u - P_RING + 1)
                if v >= 3:
                    act.wait_ge(head_done, v - 2)
                n = (t + 1) * P
                act.activation(probs[:, u % P_RING, 0:n], SCORE[u % S_RING][:, 0:n], ACT.Exp,
                               bias=negmax[:, u % M_RING:u % M_RING + 1],
                               accum_out=rsum[:, v % 3, t:t + 1]).then_inc(p_ready, 1)

            def attention(first, last):
                for s, inside in steps(first, last):
                    u = inside(s - T_LAG)
                    if u is not None and u % NT == NT - 1:
                        act.wait_ge(pT_ready, u + 1)
                        if u >= PT_RING:
                            act.wait_ge(av_done, u - PT_RING + 1)
                        act.activation(pT[:, u % PT_RING, :], PT[u % PTB][:, :], ACT.Copy).then_inc(pT_act, 1)
                    if inside(s) is not None:
                        unit_exp(s)

            act.preload_act_table_set("natural_log_exp_and_others")
            act.wait_ge(chan_loaded, 16)
            act.wait_ge(small_consts, 1)
            lam = chn[:, CH["lam"]:CH["lam"] + LRU_T]
            link(act.activation(csp[:, 1, :], lam, ACT.Abs))
            link(act.activation(csp[:, 1, :], csp[:, 1, :], ACT.Exp, scale=-1.0))
            act.activation(csp[:, 1, :], csp[:, 1, :], ACT.Ln, bias=one1[:, :]).then_inc(lam_act, 1)
            for k in range(KT):
                act.wait_ge(x_loaded[k], 16)
                act.activation(xh[:, k, :], x_raw[:, k, :], ACT.Copy, scale=ch("norm_g", k)).then_inc(xh_ready, 1)
                if k == KT // 2:
                    split(0)
            split(1)
            act.wait_ge(x_sq_used, KT)
            act.activation(rstd_bc[:, :], MEAN[:, :], ACT.Sqrt, bias=eps1[:, :], scale=1.0 / D).then_inc(std_ready, 1)
            split(2)
            for c in range(NSA_END):
                if CHUNKS[c][0] == "zl":
                    t = CHUNKS[c][1]
                    p = qr[:, t % 2, 0:HEADS * CMP_PAD]
                    act.wait_ge(cmp_shift, t + 1)
                    act.activation(p, p, ACT.Exp).then_inc(cmp_exp, 1)
                if c >= 1:
                    norm_seeds(c - 1)
                split(c + AHEAD)
                before(c)
                read_tokens(c, 0, MIDDLE)
                if c >= 1:
                    after(c - 1)
                    norm_high(c - 1)
                read_tokens(c, MIDDLE, NT)
                if c == AT["kc", 0]:
                    act.wait_ge(lru_tau, LRU_T)
                    act.wait_ge(conv_done, LRU_T)
                    for j in range(LRU_T):
                        act.activation(u_pad[:, j, 0:SEQ], tau[:, j, :], ACT.Sqrt, scale=4.0).then_inc(lru_sqrt, 1)
                    act.preload_act_table_set("natural_log_exp_and_others")
                    link(act.activation(sq[0:HEADS, :], sq[0:HEADS, :], ACT.Exp, scale=-1.0))
                    act.activation(sq[0:HEADS, :], sq[0:HEADS, :], ACT.Ln, bias=one1[0:HEADS, :]).then_inc(fg_act, 1)
                    for j in range(LRU_T):
                        act.wait_ge(lru_ix, j + 1)
                        link(act.activation(xc[:, j, :], tau[:, j, :], ACT.Ln, bias=one1[:, :]))
                        act.activation(xc[:, j, :], xc[:, j, :], ACT.Exp, scale=-1.0).then_inc(lru_seed, 1)
                if c == AT["nq", 0]:
                    act.wait_ge(cmp_evac, 1)
                    act.activation(k_cmp_sq[:, :, :], k_cmp[:, :, :], ACT.Square).then_inc(cmp_sq, 1)
                if c == AT["nq", 2]:
                    act.wait_ge(cmp_mean, 1)
                    rsqrt_seed(AUX_A[0:HD, 0:KVH * CMP_PAD].rearrange("p (g n) -> p g n", g=KVH), 1.0,
                               k_cmp_y[:, :, :], k_cmp_sq[:, :, :], k_cmp_w[:, :, :], HD).then_inc(cmp_std, 1)
                if c == AT["nq", 3]:
                    act.wait_ge(k_cmp_n, 1)
                    for half in (slice(0, HD), slice(HD, P)):
                        act.activation(k_cmp_h[half], k_cmp[:, :, :], ACT.Copy).then_inc(k_cmp_hr, 1)
            act.preload_act_table_set("natural_log_exp_and_others")
            attention(0, NSA_UNITS)
            for c in range(NSA_END, FOX_END):
                norm_seeds(c - 1)
                split(c + AHEAD)
                before(c)
                read_tokens(c, 0, MIDDLE)
                norm_high(c - 1)
                read_tokens(c, MIDDLE, NT)
                if CHUNKS[c][0] == "zn":
                    z_gate(c)
            act.preload_act_table_set("natural_log_exp_and_others")
            attention(NSA_UNITS, UNITS)
            act.wait_ge(s_ready, UNITS)
            for c in range(FOX_END, N_IN):
                split(c + AHEAD)
                z_gate(c)
                i = c - FIRST_Z
                act.wait_ge(y_ready, i + 1)
                act.activation(yh[:, LRU_T + i, :], qr[:, i % 2, :], ACT.Copy).then_inc(yh_ready, 1)
                for e in older_outputs(i):
                    dst, src = output_tile(e)
                    act.activation(dst(yh), src, ACT.Copy).then_inc(yh_ready, 1)
            for e in range(ET):
                split(N_IN + e + AHEAD)

        @block.vector
        def _(dve):
            link = chain(lambda: dve, "dve_chain")

            def ch(name, j=0):
                return chn[:, CH[name] + j:CH[name] + j + 1]

            def evac(c):
                kind, j = CHUNKS[c]
                unit = proj_units(c)
                if CHUNKS[c - 1][0] in TOKEN_MAJOR:
                    dve.wait_ge(proj_read, unit)
                dve.wait_ge(proj_done, unit + 1)
                rows = 64 if kind == "fg" else P
                if kind == "u":
                    dst = u_pad[:, j, CONV - 1:]
                elif kind == "zl":
                    dst = y_lru[:, j, :]
                elif kind in ("kc", "vc"):
                    dst = kv_cm[:, 0 if kind == "kc" else 1, :]
                elif kind == "fg":
                    dst = qr[0:64, 0, :]
                elif kind in ("zn", "zf"):
                    i = c - FIRST_Z
                    dst = qr[:, i % 2, :]
                    if i == 0:
                        dve.wait_ge(l_ready, len(NORMED))
                    elif 2 <= i < 6:
                        dve.wait_ge(y_ready, i - 1)
                    elif i >= 6:
                        dve.wait_ge(yl_ready, split_outputs(LRU_T + i - 2))
                else:
                    n = nth_normed(c)
                    dst = qr[:, n % 2, :]
                    if n >= 2:
                        dve.wait_ge(l_ready, n - 1)
                dve.tensor_tensor(dst, proj_bank(unit)[0:rows, :], rstd_bc[0:rows, :], ALU.mult).then_inc(proj_read, 1)

            def before(c):
                kind, j = CHUNKS[c]
                if kind in TOKEN_MAJOR:
                    return
                evac(c)
                if kind == "u":
                    for k in range(1, CONV):
                        if k == 1:
                            dve.wait_ge(conv_first, j + 1)
                        ins = dve.scalar_tensor_tensor(xc[:, j, :], u_pad[:, j, k:k + SEQ],
                                                       ch("conv_w", k * LRU_T + j), xc[:, j, :], ALU.mult, ALU.add)
                        if k < CONV - 1:
                            link(ins)
                        else:
                            ins.then_inc(conv_done, 1)

            def lru_output(j):
                dve.wait_ge(zl_sig, j + 1)
                dve.tensor_tensor(y_lru[:, j, :], y_lru[:, j, :], sq[:, :], ALU.mult).then_inc(zl_done, 1)
                dve.wait_ge(zl_done, j + 1)
                dve.wait_ge(lru_h, j + 1)
                link(dve.tensor_tensor(y_lru[:, j, :], y_lru[:, j, :], u_pad[:, j, 0:SEQ], ALU.mult))

            def after(c):
                kind, j = CHUNKS[c]
                if c in NORMED:
                    n = nth_normed(c)
                    dve.wait_ge(norm_seed, n + 1)
                    link(dve.tensor_tensor(work[:, :], work[:, :], NORM_W[:, :], ALU.mult))
                    link(dve.scalar_tensor_tensor(std[:, :], work[:, :], 1.5, std[:, :], ALU.add, ALU.mult))
                    dve.scalar_tensor_tensor(qr[:, n % 2, :], qr[:, n % 2, :], ch(GAIN[kind]), std[:, :], ALU.mult,
                                             ALU.mult).then_inc(normed, 1)
                    for s in range(2):
                        high, low = operand_parts(c, s)
                        dve.wait_ge(h_ready, 2 * n + s + 1)
                        ins = dve.tensor_tensor(low, qr[half_of(s), n % 2, :], high.bitcast(F32), ALU.subtract)
                    ins.then_inc(l_ready, 1)

            def log_sigmoid():
                f = qr[0:HEADS, 0, :]
                dve.wait_ge(fg_act, 2)
                link(dve.tensor_scalar(f, f, ch("fg_b")[0:HEADS], 0.0, ALU.add, ALU.min))
                link(dve.tensor_tensor(log_f, f, sq[0:HEADS, :], ALU.subtract))

            def forget_gates():
                one, b = std[96:96 + HEADS, :], work[0:HEADS, :]
                mid = std[0:HEADS, :].bitcast(BF16)[:, 0:SEQ]
                dve.wait_ge(normed, len(NORMED))
                link(dve.memset(one, 1.0))
                link(dve.tensor_tensor_scan(b, one, log_f, 0.0, ALU.mult, ALU.subtract))
                dve.wait_ge(small_consts, 1)
                link(dve.tensor_copy(c_parts[0:HEADS, :], b))
                link(dve.tensor_tensor(b, b, c_parts[0:HEADS, :], ALU.subtract))
                link(dve.tensor_copy(mid, b))
                link(dve.tensor_tensor(b, b, mid, ALU.subtract))
                dve.tensor_copy(c_parts[32:32 + HEADS, :], mid)
                dve.tensor_copy(c_parts[64:64 + HEADS, :], b).then_inc(c_ready, 1)

            def branch_gates():
                dve.wait_ge(gates_T, 1)
                dve.tensor_copy(gates[:, :, :], AUX_A[:, 0:NT * 64].rearrange("p (t c) -> p t c", t=NT)
                                [:, :, 32:32 + 3 * HEADS]).then_inc(gates_ready, 1)

            def lru_tail(j, half):
                t, h, g, d = tau[:, j, :], u_pad[:, j, 0:SEQ], ig[:, j, :], xc[:, j, :]
                if half == 0:
                    dve.wait_ge(lru_seed, j + 1)
                    dve.wait_ge(lru_ixs, j + 1)
                    link(dve.scalar_tensor_tensor(h, t, 1.0, d, ALU.add, ALU.mult))
                    link(dve.scalar_tensor_tensor(d, h, 2.0, d, ALU.subtract, ALU.mult))
                    return
                link(dve.scalar_tensor_tensor(t, t, 1.0, d, ALU.subtract, ALU.mult))
                link(dve.scalar_tensor_tensor(g, g, -1.0, d, ALU.mult, ALU.mult))
                dve.tensor_tensor_scan(h, t, g, 0.0, ALU.mult, ALU.add).then_inc(lru_h, 1)

            def pair_pe(i):
                dve.wait_ge(kv_shifted[i], 64)
                if i == 1:
                    dve.wait_ge(cmp_prod, 1)
                pairs = kv_pair[:, :, :].rearrange("p g (n j two) -> p g n j two", j=8, two=2)
                for part in range(2):
                    o = CH["pe_k" if i == 0 else "pe_v"] + 8 * part
                    for g in range(KVH):
                        pe_row = chn[:, o:o + 8].unsqueeze(1).broadcast_to([P, SEQ // 16, 8])
                        ins = dve.tensor_tensor(kv_pe[:, part, g, :, :], pairs[:, g, :, :, 0], pe_row, ALU.add)
                ins.then_inc(kv_pe_ready, 1)

            def cmp_out(i):
                dve.wait_ge(cmp_prod, i + 1)
                dve.wait_ge(small_consts, 1)
                src = (AUX_A if i == 0 else AUX_B)[0:HD, 0:KVH * CMP_PAD].rearrange("p (g n) -> p g n", g=KVH)
                dve.tensor_copy((k_cmp if i == 0 else v_cmp)[:, :, 0:N_CMP], src[:, :, 0:N_CMP]).then_inc(cmp_evac, 1)

            def cmp_norm():
                dve.wait_ge(cmp_std, 1)
                kc, ks, ky, kw = (x[:, :, :].rearrange("p g n -> p (g n)") for x in (k_cmp, k_cmp_sq, k_cmp_y, k_cmp_w))
                link(dve.tensor_tensor(ks, ks, kw, ALU.mult))
                link(dve.scalar_tensor_tensor(ky, ks, 1.5, ky, ALU.add, ALU.mult))
                dve.scalar_tensor_tensor(kc, kc, ch("kcmp_g")[0:HD], ky, ALU.mult, ALU.mult).then_inc(k_cmp_n, 1)
                dve.wait_ge(k_cmp_hr, 2)
                for half in (slice(0, HD), slice(HD, P)):
                    dve.tensor_tensor(k_cmp_l[half], k_cmp[:, :, :], k_cmp_h[0:HD].bitcast(F32),
                                      ALU.subtract).then_inc(k_cmp_ready, 1)

            def cmp_values():
                dve.wait_ge(v_cmp_T, 1)
                for g in range(KVH):
                    for r in range(GROUP):
                        dve.tensor_copy(v_blocks[32 * r:32 * r + 32, g, r * HD:(r + 1) * HD],
                                        AUX_B[0:CMP_PAD, g * HD:(g + 1) * HD]).then_inc(v_cmp_ready, 1)

            def cmp_probs(t):
                s4 = SCORE[t % 2][:, 0:2 * HEADS * CMP_PAD].rearrange("p (h i n) -> p h i n", h=HEADS, i=2)
                p3 = qr[:, t % 2, 0:HEADS * CMP_PAD].rearrange("p (h n) -> p h n", h=HEADS)
                mask = cst[:, CMPMASK + t * CMP_PAD:CMPMASK + (t + 1) * CMP_PAD]
                mx, sm, rc = (cmp_stat[:, i, :] for i in range(3))
                dve.wait_ge(cmp_s, t + 1)
                if t == 0:
                    dve.wait_ge(l_ready, 6)
                if t >= 2:
                    dve.wait_ge(cmp_pT, t - 1)
                link(dve.tensor_tensor(p3, s4[:, :, 1, :], mask.unsqueeze(1).broadcast_to([P, HEADS, CMP_PAD]),
                                       ALU.add))
                link(dve.tensor_tensor(p3, p3, s4[:, :, 0, :], ALU.add))
                link(dve.tensor_reduce(mx, p3, AX.X, ALU.max))
                link(dve.tensor_scalar(mx, mx, NEG / 10, None, ALU.max))
                dve.tensor_tensor(p3, p3, mx.unsqueeze(2).broadcast_to([P, HEADS, CMP_PAD]),
                                  ALU.subtract).then_inc(cmp_shift, 1)
                if t >= 1:
                    cmp_out_read(t - 1)
                    lru_output(t - 1)
                dve.wait_ge(cmp_exp, t + 1)
                link(dve.tensor_reduce(sm, p3, AX.X, ALU.add))
                link(dve.tensor_scalar(sm, sm, 1e-30, None, ALU.max))
                link(dve.reciprocal(rc, sm))
                link(dve.tensor_tensor(rc, rc, gates[:, t, 0:3 * HEADS:3], ALU.mult))
                dve.tensor_tensor(p3, p3, rc.unsqueeze(2).broadcast_to([P, HEADS, CMP_PAD]),
                                  ALU.mult).then_inc(cmp_p, 1)

            def cmp_transposed(t):
                dve.wait_ge(cmp_pT, t + 1)
                if t == 0:
                    dve.wait_ge(normed, 6)
                if t >= 1:
                    dve.wait_ge(cmp_o, t)
                dve.tensor_copy(std[:, 0:2 * P], PT[0][:, 0:2 * P]).then_inc(cmp_pT_sb, 1)

            def cmp_out_read(t):
                dve.wait_ge(cmp_o, t + 1)
                dve.tensor_copy(o_nsa[:, t, :], OUT[t % 2][:, :]).then_inc(cmp_o_read, 1)

            def z_times_o(c):
                i = c - FIRST_Z
                z = qr[:, i % 2, :]
                dve.wait_ge(oT_ready, i + 1)
                dve.wait_ge(z_sig, i + 1)
                link(dve.tensor_tensor(z, z, sq[:, :], ALU.mult))
                o = by_token(OUT[i % 2][:, :])
                if i < 4:
                    dst = o_nsa[:, :, i * P:(i + 1) * P]
                else:
                    dst = by_token(z)
                dve.tensor_tensor(dst, by_token(z), o, ALU.mult).then_inc(y_ready, 1)

            def finish_head(v):
                group, h, b = heads[v]
                dve.wait_ge(av_done, NT * (v + 1))
                if v >= 1:
                    dve.wait_ge(head_done, v)
                link(dve.reciprocal(rcp[:, 0, :], rsum[:, v % 3, :]))
                o = OUT[v % 2][:, 0:NT * HD].rearrange("p (t d) -> p t d", t=NT)
                if group == "nsa":
                    if v == 0:
                        dve.wait_ge(cmp_o_read, NT)
                    link(dve.tensor_tensor(rcp[:, 0, :], rcp[:, 0, :], gates[:, :, 3 * h + b], ALU.mult))
                    scaled = head_out[:, :].rearrange("p (t d) -> p t d", t=NT)
                    link(dve.tensor_tensor(scaled, o, rcp[:, 0, :].unsqueeze(2).broadcast_to([P, NT, HD]), ALU.mult))
                    acc = o_nsa[:, :, h * HD:(h + 1) * HD]
                    dve.tensor_tensor(acc, acc, scaled, ALU.add).then_inc(head_done, 1)
                else:
                    dve.tensor_tensor(o_fox[:, :, h * HD:(h + 1) * HD], o,
                                      rcp[:, 0, :].unsqueeze(2).broadcast_to([P, NT, HD]),
                                      ALU.mult).then_inc(head_done, 1)

            def attention(first, last):
                for s, inside in steps(first, last):
                    if s == 7:
                        cmp_out_read(NT - 1)
                    if s == 16:
                        lru_output(LRU_T - 1)
                    if first > 0 and s == first + 5:
                        z_times_o(FOX_END - 1)
                    if inside(s) is not None:
                        n = (s % NT + 1) * P
                        dve.wait_ge(s_ready, s + 1)
                        if s >= M_RING:
                            dve.wait_ge(p_ready, s - M_RING + 1)
                        dve.tensor_reduce(negmax[:, s % M_RING:s % M_RING + 1], SCORE[s % S_RING][:, 0:n], AX.X,
                                          ALU.max, negate=True).then_inc(max_ready, 1)
                    u = inside(s - T_LAG)
                    if u is not None and u % NT < NT - 1:
                        n = (u % NT + 1) * P
                        dve.wait_ge(pT_ready, u + 1)
                        if u >= PT_RING:
                            dve.wait_ge(av_done, u - PT_RING + 1)
                        dve.tensor_copy(pT[:, u % PT_RING, 0:n], PT[u % PTB][:, 0:n]).then_inc(pT_dve, 1)
                    u = inside(s - V_LAG - 1)
                    if u is not None and u % NT == NT - 1:
                        finish_head(u // NT)

            for k in range(KT):
                dve.wait_ge(x_loaded[k], 16)
                if k in VECTOR_SQUARES:
                    i = VECTOR_SQUARES.index(k)
                    if i >= 2:
                        dve.wait_ge(x_sq_used, VECTOR_SQUARES[i - 2] + 1)
                    dve.tensor_tensor(qr[:, i % 2, :], x_raw[:, k, :], x_raw[:, k, :], ALU.mult).then_inc(x_sq, 1)
                if k == 0:
                    dve.wait_ge(chan_loaded, 16)
                dve.wait_ge(xh_ready, k + 1)
                dve.scalar_tensor_tensor(xl[:, k, :], x_raw[:, k, :], ch("norm_g", k), xh[:, k, :].bitcast(F32),
                                         ALU.mult, ALU.subtract).then_inc(xl_ready, 1)
            dve.wait_ge(const_loaded, 16)
            dve.tensor_copy(ident_b[:, :], ident)
            dve.tensor_copy(mask_b[:, :], cst[:, CAUSAL:CAUSAL + P])
            sel = work[0:96, 0:HEADS]
            link(dve.tensor_tensor(sel, cst[0:96, IDENT:IDENT + HEADS], cst[0:96, IDENT + 32:IDENT + 32 + HEADS],
                                   ALU.add))
            link(dve.tensor_tensor(sel, sel, cst[0:96, IDENT + 64:IDENT + 64 + HEADS], ALU.add))
            dve.tensor_copy(head_sel[:, :, :], sel.unsqueeze(2).broadcast_to([96, HEADS, P])).then_inc(sel_ready, 1)
            dve.wait_ge(lam_act, 1)
            lam = chn[:, CH["lam"]:CH["lam"] + LRU_T]
            link(dve.tensor_scalar(csp[:, 0, :], lam, -1.0, 0.0, ALU.mult, ALU.max))
            link(dve.tensor_tensor(csp[:, 0, :], csp[:, 0, :], csp[:, 1, :], ALU.add))
            dve.tensor_scalar(csp[:, 0, :], csp[:, 0, :], 4.0, None, ALU.mult).then_inc(csp_ready, 1)
            dve.wait_ge(x_sq_used, KT)
            dve.memset(u_pad[:, :, 0:CONV - 1], 0.0)
            dve.wait_ge(std_ready, 1)
            dve.reciprocal(rstd_bc[:, :], rstd_bc[:, :]).then_inc(rstd_ready, 1)
            dve.wait_ge(rstd_ready, 1)
            for c in range(NSA_END):
                if CHUNKS[c][0] == "zl":
                    cmp_probs(CHUNKS[c][1])
                before(c)
                if c == AT["kc", 0]:
                    dve.wait_ge(rstd_T, 1)
                    dve.tensor_copy(rstd_col[:, :], AUX_B[:, :].rearrange("p (t c) -> p t c", t=NT)[:, :, 0])\
                       .then_inc(rcol_ready, 1)
                if c == AT["vc", 0]:
                    branch_gates()
                    log_sigmoid()
                if c == AT["ks", 0]:
                    pair_pe(0)
                if c == AT["nq", 0]:
                    cmp_out(0)
                    pair_pe(1)
                if c == AT["nq", 2]:
                    cmp_out(1)
                if c == AT["vn", 0]:
                    cmp_values()
                if c >= 1:
                    after(c - 1)
                for i, step in enumerate(TAIL_AT):
                    if step == c:
                        lru_tail(i // 2, i % 2)
                if c == AT["nq", 3]:
                    cmp_norm()
                if CHUNKS[c][0] == "zl":
                    cmp_transposed(CHUNKS[c][1])
            attention(0, NSA_UNITS)
            for c in range(NSA_END, FOX_END):
                before(c)
                after(c - 1)
                if c == FIRST_Z + 1:
                    forget_gates()
                if CHUNKS[c][0] == "zn" and c < FOX_END - 1:
                    z_times_o(c)
            attention(NSA_UNITS, UNITS)
            dve.wait_ge(s_ready, UNITS)
            for c in range(FOX_END, N_IN):
                i = c - FIRST_Z
                evac(c)
                z_times_o(c)
                dve.wait_ge(yh_ready, split_outputs(LRU_T + i))
                dve.tensor_tensor(yl[:, LRU_T + i, :], qr[:, i % 2, :], yh[:, LRU_T + i, :].bitcast(F32),
                                  ALU.subtract).then_inc(yl_ready, 1)
                for e in older_outputs(i):
                    dst, src = output_tile(e)
                    dve.wait_ge(yh_ready, split_outputs(e))
                    dve.tensor_tensor(dst(yl), src, dst(yh).bitcast(F32), ALU.subtract).then_inc(yl_ready, 1)
            dve.wait_ge(res_loaded, 16)
            for n, t in enumerate(OUT_ORDER):
                for half in range(2):
                    dve.wait_ge(out_sum, 2 * n + half + 1)
                    cols = slice(half * 512, (half + 1) * 512)
                    dve.tensor_tensor(y_out[:, t, cols], bank[2 * t + half][:, :], x_res[:, t, cols],
                                      ALU.add).then_inc(out_ready, 1)

        @block.tensor
        def _(pe):
            def project(c):
                kind, j = CHUNKS[c]
                slot = c % HL
                if kind in TOKEN_MAJOR:
                    if j % 2:
                        return
                    pe.wait_ge(wl_ready, c + 2)
                    hi = wh[:, slot:slot + 2, :].rearrange("p s (k c) -> p k s c", k=KT)
                    lo = wl[:, slot:slot + 2, :].rearrange("p s (k c) -> p k s c", k=KT)
                    for t in range(NT):
                        unit = proj_units(c) + t
                        wait_bank(pe, unit)
                        dst = proj_bank(unit)[:, 0:2 * P].rearrange("p (s c) -> p s c", s=2)
                        toks = slice(t * P, (t + 1) * P)
                        for k in range(KT):
                            pe.matmul(dst, xh[:, k, toks], hi[:, k], start=(k == 0), stop=False)
                            pe.matmul(dst, xh[:, k, toks], lo[:, k], start=False, stop=False)
                            mm = pe.matmul(dst, xl[:, k, toks], hi[:, k], start=False, stop=(k == KT - 1))
                        mm.then_inc(proj_done, 1)
                        if t == 0:
                            head_mean(c - 1)
                    return
                unit = proj_units(c)
                wait_bank(pe, unit)
                pe.wait_ge(wl_ready, c + 1)
                m = 64 if kind == "fg" else P
                dst = proj_bank(unit)[0:m, :]
                for k in range(KT):
                    if k == KT // 2 + 1 and c - 1 in NORMED:
                        head_mean(c - 1)
                    if k == KT // 2 and c == AT["zl", 0]:
                        cmp_scores(0)
                    if c == 0:
                        pe.wait_ge(xl_ready, k + 1)
                    hi, lo = wh[:, slot, k * P:k * P + m], wl[:, slot, k * P:k * P + m]
                    pe.matmul(dst, hi, xh[:, k, :], start=(k == 0), stop=False)
                    pe.matmul(dst, hi, xl[:, k, :], start=False, stop=False)
                    mm = pe.matmul(dst, lo, xh[:, k, :], start=False, stop=(k == KT - 1))
                mm.then_inc(proj_done, 1)

            def head_mean(c):
                n = nth_normed(c)
                pe.wait_ge(sq_ready, n + 1)
                if n >= 1:
                    pe.wait_ge(norm_seed, n)
                pe.matmul(MEAN[:, :], block_mean, sq[:, :], start=True, stop=True).then_inc(norm_mean, 1)

            def gates_of(j):
                pe.wait_ge(conv_done, j + 1)
                if j >= 1:
                    pe.wait_ge(lru_sig, 2 * j)
                if j == 0:
                    pe.wait_ge(lru_w_loaded, 16)
                pe.matmul(AUX_A[:, :], lru_w_sb[:, 0, j, :], xc[:, j, :], start=True, stop=True)
                pe.matmul(AUX_B[:, :], lru_w_sb[:, 1, j, :], xc[:, j, :], start=True, stop=True)\
                    .then_inc(lru_gates, 1)

            def compress(i):
                pe.wait_ge(kv_pe_ready, i + 1)
                pe.wait_ge(cmp_w_loaded, 16)
                dst = (AUX_A if i == 0 else AUX_B)[0:HD, 0:KVH * CMP_PAD].rearrange("p (g n) -> p g n", g=KVH)
                for j in range(CMP_LEN // 2):
                    part = j // 8
                    mm = pe.matmul(dst[:, :, 0:N_CMP], cmp_w_sb[:, i, j, :],
                                   kv_pe[:, part, :, part:part + N_CMP, j % 8],
                                   start=(j == 0), stop=(j == CMP_LEN // 2 - 1))
                mm.then_inc(cmp_prod, 1)

            def cmp_scores(t):
                if t == 0:
                    pe.wait_ge(k_cmp_ready, 2)
                    pe.wait_ge(l_ready, 6)
                    pe.wait_ge(stacked, 16 * stack_copies(6))
                    pe.wait_ge(normed, 6)
                if t >= 2:
                    pe.wait_ge(cmp_shift, t - 1)
                for h in range(HEADS):
                    dst = SCORE[t % 2][:, 2 * h * CMP_PAD:2 * (h + 1) * CMP_PAD].rearrange("p (i n) -> p i n", i=2)
                    mm = pe.matmul(dst, q_nsa[:, h, t * P:(t + 1) * P], k_cmp_parts[:, h // GROUP, :, :],
                                   start=True, stop=True)
                mm.then_inc(cmp_s, 1)

            def cmp_transpose(t):
                pe.wait_ge(cmp_p, t + 1)
                if t >= 1:
                    pe.wait_ge(cmp_pT_sb, t)
                for g in range(KVH):
                    mm = pe.transpose(PT[0][:, g * P:(g + 1) * P], qr[:, t % 2, g * P:(g + 1) * P], ident)
                mm.then_inc(cmp_pT, 1)

            def cmp_values(t):
                pe.wait_ge(cmp_pT_sb, t + 1)
                if t == 0:
                    pe.wait_ge(v_cmp_ready, KVH * GROUP)
                if t >= 2:
                    pe.wait_ge(cmp_o_read, t - 1)
                for g in range(KVH):
                    mm = pe.matmul(OUT[t % 2][:, g * GROUP * HD:(g + 1) * GROUP * HD], std[:, g * P:(g + 1) * P],
                                   v_blocks[:, g, :], start=True, stop=True)
                mm.then_inc(cmp_o, 1)

            def unit_scores(u):
                v, t = divmod(u, NT)
                n = (t + 1) * P
                q, kh, kl = scores_of(u)
                if u >= S_RING:
                    pe.wait_ge(p_ready, u - S_RING + 1)
                elif u < 2:
                    pe.wait_ge(cmp_shift, NT - 1 + u)
                if u in (2, NSA_UNITS + 2):
                    pe.wait_ge(proj_read, proj_units(NSA_END if u == 2 else FOX_END) - 1)
                if u in (3, NSA_UNITS + 3):
                    pe.wait_ge(proj_read, proj_units(NSA_END if u == 3 else FOX_END))
                dst, q = SCORE[u % S_RING], q[:, t * P:(t + 1) * P]
                pe.matmul(dst[:, 0:n], q, kh[:, 0:n], start=True, stop=False)
                pe.matmul(dst[:, t * P:n], ident_b[:, :], mask_b[:, :], start=False, stop=False)
                if heads[v][0] == "fox":
                    pe.matmul(dst[:, 0:n], head_sel[:, heads[v][1], :], c_parts[:, 0:n], start=False, stop=False)
                pe.matmul(dst[:, 0:n], q, kl[:, 0:n], start=False, stop=True).then_inc(s_ready, 1)

            def unit_transpose(u):
                pe.wait_ge(p_ready, u + 1)
                if u >= PTB:
                    wait_pT(pe, u - PTB)
                for j in range(u % NT + 1):
                    cols = slice(j * P, (j + 1) * P)
                    mm = pe.transpose(PT[u % PTB][:, cols], probs[:, u % P_RING, cols], ident)
                mm.then_inc(pT_ready, 1)

            def unit_values(u):
                v, t = divmod(u, NT)
                wait_pT(pe, u)
                if t == 0 and v >= 2:
                    pe.wait_ge(head_done, v - 1)
                elif t == 0:
                    pe.wait_ge(cmp_o_read, NT - 1 + v)
                if t == 0 and v in (2 * HEADS, 2 * HEADS + 1):
                    pe.wait_ge(y_ready, 3 + v % 2)
                val = values_of(u)
                for j in range(t + 1):
                    mm = pe.matmul(OUT[v % 2][:, t * HD:(t + 1) * HD], pT[:, u % PT_RING, j * P:(j + 1) * P], val[:, j, :],
                                   start=(j == 0), stop=(j == t))
                mm.then_inc(av_done, 1)

            def attention(first, last):
                for s, inside in steps(first, last):
                    if s == 3:
                        cmp_values(NT - 1)
                    if s == last + T_LAG:
                        project(NSA_END if last == NSA_UNITS else FOX_END)
                    if inside(s) is not None:
                        unit_scores(s)
                    if inside(s - T_LAG) is not None:
                        unit_transpose(s - T_LAG)
                    if inside(s - V_LAG) is not None:
                        unit_values(s - V_LAG)

            pe.wait_ge(ones_ready, 1)
            for k in range(KT):
                if k in POOL_SQUARES:
                    pe.wait_ge(x_sq_pool, POOL_SQUARES.index(k) + 1)
                    square = pool_square(k)
                else:
                    i = VECTOR_SQUARES.index(k)
                    pe.wait_ge(x_sq, i + 1)
                    square = qr[:, i % 2, :]
                pe.matmul(MEAN[:, :], ones[:, :], square, start=(k == 0),
                          stop=(k == KT - 1)).then_inc(x_sq_used, 1)
            for c in range(NSA_END):
                project(c)
                if c >= 1 and CHUNKS[c - 1][0] == "u":
                    gates_of(CHUNKS[c - 1][1])
                if c == AT["kc", 0]:
                    pe.wait_ge(rstd_ready, 1)
                    pe.wait_ge(const_loaded, 16)
                    pe.wait_ge(lru_sig, 2 * LRU_T)
                    for t in range(NT):
                        mm = pe.transpose(AUX_B[:, t * P:(t + 1) * P], rstd_bc[:, t * P:(t + 1) * P], ident)
                    mm.then_inc(rstd_T, 1)
                if c == AT["vc", 0]:
                    pe.wait_ge(fg_act, 1)
                    for t in range(NT):
                        mm = pe.transpose(AUX_A[:, t * 64:(t + 1) * 64], std[0:64, t * P:(t + 1) * P], ident[0:64, 0:64])
                    mm.then_inc(gates_T, 1)
                if c == AT["kw", 0]:
                    pe.wait_ge(gates_ready, 1)
                    compress(0)
                if c == AT["nq", 1]:
                    pe.wait_ge(rcol_ready, 1)
                    compress(1)
                    pe.wait_ge(cmp_sq, 1)
                    pe.matmul(AUX_A[0:HD, 0:KVH * CMP_PAD], block_mean[0:HD, 0:HD],
                              k_cmp_sq[:, :, :].rearrange("p g n -> p (g n)"), start=True, stop=True)\
                        .then_inc(cmp_mean, 1)
                if c == AT["nq", 3]:
                    pe.wait_ge(cmp_evac, 2)
                    for g in range(KVH):
                        mm = pe.transpose(AUX_B[0:CMP_PAD, g * HD:(g + 1) * HD], v_cmp[:, g, :], ident[0:HD, 0:HD])
                    mm.then_inc(v_cmp_T, 1)
                if CHUNKS[c][0] == "zl":
                    t = CHUNKS[c][1]
                    cmp_transpose(t)
                    if t < NT - 1:
                        cmp_scores(t + 1)
                        cmp_values(t)
            attention(0, NSA_UNITS)

            def o_transposed(c):
                i = c - FIRST_Z
                if i >= 2:
                    pe.wait_ge(y_ready, i - 1)
                src = o_nsa if i < 4 else o_fox
                for t in range(NT):
                    mm = pe.transpose(OUT[i % 2][:, t * P:(t + 1) * P], src[:, t, (i % 4) * P:(i % 4 + 1) * P], ident)
                mm.then_inc(oT_ready, 1)

            for c in range(NSA_END, FOX_END):
                if c == NSA_END + 2:
                    wait_pT(pe, NSA_UNITS - 1)
                if c == FIRST_Z:
                    pe.wait_ge(head_done, 2 * HEADS)
                if c > NSA_END:
                    project(c)
                if CHUNKS[c][0] == "zn":
                    o_transposed(c)
            pe.wait_ge(l_ready, len(NORMED))
            pe.wait_ge(stacked, 16 * stack_copies(len(NORMED)))
            pe.wait_ge(normed, len(NORMED))
            pe.wait_ge(c_ready, 1)
            attention(NSA_UNITS, UNITS)
            for c in range(FOX_END, N_IN):
                if c == FOX_END + 2:
                    wait_pT(pe, UNITS - 1)
                if c > FOX_END:
                    project(c)
                if c <= FOX_END + 1:
                    pe.wait_ge(head_done, len(heads) - 1 + c - FOX_END)
                o_transposed(c)
            for e in range(ET):
                c = N_IN + e
                pe.wait_ge(wl_ready, c + 1)
                pe.wait_ge(yl_ready, split_outputs(e))
                for n, t in enumerate(OUT_ORDER):
                    if e == 0:
                        pe.wait_ge(proj_read, proj_units(N_IN))
                        if n == NT - 1:
                            pe.wait_ge(y_ready, 8)
                    toks = slice(t * P, (t + 1) * P)
                    for half in range(2):
                        dst = bank[2 * t + half][:, :]
                        cols = slice(half * 512, (half + 1) * 512)
                        pe.matmul(dst, yh[:, e, toks], wh[:, c % HL, cols], start=(e == 0), stop=False)
                        pe.matmul(dst, yh[:, e, toks], wl[:, c % HL, cols], start=False, stop=False)
                        mm = pe.matmul(dst, yl[:, e, toks], wh[:, c % HL, cols], start=False, stop=(e == ET - 1))
                        if e == ET - 1:
                            mm.then_inc(out_sum, 1)
                if e < ET - 1:
                    mm.then_inc(w_used, 1)


def pack(x, norm_g, w_in, w_out, conv_w, conv_b, lru_wa, lru_ba, lru_wx, lru_bx, lru_lambda, nsa_q_g, nsa_k_g,
         cmp_pe_k, cmp_pe_v, cmp_wk, cmp_wv, nsa_gate_b, fox_q_g, fox_k_g, fox_f_b):
    f = np.float32
    w = w_in[0]
    chunks = np.zeros((N_IN, P, KT, P), f)
    for c, (kind, j) in enumerate(CHUNKS):
        if kind == "fg":
            chunks[c, :, :, 0:HEADS] = w[:, COLS["fl"]:COLS["fl"] + HEADS].reshape(KT, P, -1).transpose(1, 0, 2)
            chunks[c, :, :, 32:32 + 3 * HEADS] = (
                w[:, COLS["gl"]:COLS["gl"] + 3 * HEADS].reshape(KT, P, -1).transpose(1, 0, 2))
            continue
        o = COLS[("vs", "vw")[j]] if kind == "vn" else COLS[kind] + j * P
        chunks[c] = w[:, o:o + P].reshape(KT, P, P).transpose(1, 0, 2)
    chan = np.zeros((P, CH_W), f)

    def put(name, a):
        a = np.asarray(a)
        chan[0:a.shape[0], CH[name]:CH[name] + a.shape[1]] = a

    put("norm_g", norm_g[0].reshape(KT, P).T)
    put("conv_w", conv_w[0].reshape(CONV * LRU_T, P).T)
    for name, a in (("conv_b", conv_b), ("ba", lru_ba), ("bx", lru_bx), ("lam", lru_lambda)):
        put(name, a[0].reshape(LRU_T, P).T)
    for name, a in (("nq_g", nsa_q_g[0]), ("kcmp_g", nsa_k_g[0, 0]), ("ks_g", nsa_k_g[0, 1]), ("kw_g", nsa_k_g[0, 2]),
                    ("fq_g", fox_q_g[0]), ("fk_g", fox_k_g[0])):
        put(name, np.concatenate([a, a])[:, None])
    chan[0:HEADS, CH["fg_b"]] = fox_f_b[0]
    chan[32:32 + 3 * HEADS, CH["fg_b"]] = nsa_gate_b[0]
    for name, a in (("pe_k", cmp_pe_k), ("pe_v", cmp_pe_v)):
        put(name, a[0].reshape(CMP_LEN // 2, 2, HD).transpose(1, 2, 0).reshape(P, CMP_LEN // 2))
    lru = np.zeros((P, 2, LRU_T, P), f)
    for i, a in enumerate((lru_wa[0], lru_wx[0])):
        for b in range(2 * LRU_T):
            r = (b % 2) * HD
            lru[r:r + HD, i, b // 2, r:r + HD] = a[b]
    cmp = np.stack([a[0].reshape(CMP_LEN // 2, 2, HD, HD).transpose(1, 2, 0, 3).reshape(P, CMP_LEN // 2, HD)
                    for a in (cmp_wk, cmp_wv)], axis=1)
    return {
        "xT": x[0].T.reshape(KT, P, SEQ).transpose(1, 0, 2),
        "x_tok": x[0].reshape(NT, P, D).transpose(1, 0, 2),
        "w_in": chunks.reshape(N_IN, P, D),
        "w_out": w_out[0].reshape(ET, P, D),
        "chan": chan, "const": constants(), "lru_w": lru, "cmp_w": cmp,
    }


def constants():
    c = np.zeros((P, CONST_W), np.float32)
    i = np.arange(P)
    c[:, IDENT:IDENT + P] = np.eye(P)
    c[:, BLOCK:BLOCK + P] = (i[:, None] // HD == i[None, :] // HD) / HD
    c[:, CAUSAL:CAUSAL + P] = np.where(i[None, :] > i[:, None], NEG, 0.0)
    n = np.arange(CMP_PAD)
    for t in range(NT):
        seen = (n[None, :] * CMP_STRIDE + CMP_LEN - 1 <= (t * P + i)[:, None]) & (n[None, :] < N_CMP)
        c[:, CMPMASK + t * CMP_PAD:CMPMASK + (t + 1) * CMP_PAD] = np.where(seen, 0.0, NEG)
    return c


def kernel(**inputs):
    import concourse.bacc as bacc
    from concourse.bass_utils import run_bass_kernel_spmd

    nc = bacc.Bacc("TRN2", target_bir_lowering=False, num_devices=1)
    arrays, args = {}, []
    for name, a in pack(**{k: np.asarray(v) for k, v in inputs.items()}).items():
        a = np.ascontiguousarray(a)
        arrays[f"in_{name}"] = a
        args.append(nc.dram_tensor(f"in_{name}", a.shape, mybir.dt.from_np(a.dtype), kind="ExternalInput").ap())
    y = nc.dram_tensor("out_y", (SEQ, D), F32, kind="ExternalOutput").ap()
    program(nc, *args, y)
    r = run_bass_kernel_spmd(nc, [arrays], core_ids=[0])
    return r.results[0]["out_y"].reshape(1, SEQ, D)
```
